# Optimizing a Trainium2 kernel written in Bass

```python
import jax, jax.numpy as jnp
from jax import lax
import numpy as np
import math
import jax
import jax.numpy as jnp

D_MODEL = 1024
BATCH = 1
SEQ = 256
DEPTH = 1

N_BRANCH = 4
BRANCH_WIDTH = 512
EPS = 1e-6
Q_BLOCK = 128
GM_GROUPS = 4
GM_CHUNK = 128
GM_GROUP_DIM = BRANCH_WIDTH // GM_GROUPS
DSA_HEADS = 4
DSA_HEAD_DIM = BRANCH_WIDTH // DSA_HEADS
DSA_LATENT = 128
IDX_HEADS = 4
IDX_DIM = 64
TOPK_MAX = 256
CONV_WIDTH = 3
FOX_HEADS = 4
FOX_HEAD_DIM = BRANCH_WIDTH // FOX_HEADS

W = BRANCH_WIDTH
IN_SPLITS = (
    W, W, W,
    W, DSA_LATENT, IDX_HEADS * IDX_DIM, IDX_DIM, IDX_HEADS, W,
    W, W, W, W,
    W, W, W, FOX_HEADS, W,
    N_BRANCH * D_MODEL,
)
IN_WIDTH = sum(IN_SPLITS)


def rms_norm(x, g):
    xf = x.astype(jnp.float32)
    y = xf * lax.rsqrt(jnp.mean(xf * xf, axis=-1, keepdims=True) + EPS)
    return (y * g.astype(jnp.float32)).astype(x.dtype)

def layer_norm(x, g, b):
    xf = x.astype(jnp.float32)
    mu = jnp.mean(xf, axis=-1, keepdims=True)
    var = jnp.mean(jnp.square(xf - mu), axis=-1, keepdims=True)
    y = (xf - mu) * lax.rsqrt(var + EPS)
    return (y * g.astype(jnp.float32) + b.astype(jnp.float32)).astype(x.dtype)

def to_blocks(a):
    b, s = a.shape[0], a.shape[1]
    return jnp.moveaxis(a.reshape(b, s // Q_BLOCK, Q_BLOCK, *a.shape[2:]), 1, 0)

def from_blocks(a):
    nb, b = a.shape[0], a.shape[1]
    return jnp.moveaxis(a, 0, 1).reshape(b, nb * Q_BLOCK, a.shape[-1])

def chunked_spatial_gating(u, v, ln_g, ln_b, w_s, b_s):
    bsz, s, _ = v.shape
    v = layer_norm(v, ln_g, ln_b)
    vc = v.reshape(bsz, s // GM_CHUNK, GM_CHUNK, GM_GROUPS, GM_GROUP_DIM)
    mask = jnp.tril(jnp.ones((GM_CHUNK, GM_CHUNK), dtype=bool))
    w = jnp.where(mask[None], w_s, jnp.zeros_like(w_s))
    mixed = jnp.einsum('gts,bcsge->bctge', w, vc) + jnp.transpose(b_s)[None, None, :, :, None]
    return u * mixed.reshape(bsz, s, W)

def dsa_attention(q, c_kv, q_idx, k_idx, w_idx, kv_g, w_uk, w_uv):
    bsz, s, _ = q.shape
    k_sel = min(TOPK_MAX, s // 4)
    c = rms_norm(c_kv, kv_g)
    qh = q.reshape(bsz, s, DSA_HEADS, DSA_HEAD_DIM)
    q_lat = jnp.einsum('bshd,hld->bshl', qh, w_uk)
    qi = q_idx.reshape(bsz, s, IDX_HEADS, IDX_DIM)
    wi = w_idx * (IDX_HEADS ** -0.5)
    key_pos = jnp.arange(s)
    gather = jax.vmap(lambda cb, ib: cb[ib])

    def block(args):
        qlb, qib, wib, blk = args
        pos_q = blk * Q_BLOCK + jnp.arange(Q_BLOCK)
        dots = jnp.einsum('bqhd,bsd->bqhs', qib, k_idx).astype(jnp.float32) * (IDX_DIM ** -0.5)
        score = jnp.einsum('bqh,bqhs->bqs', wib.astype(jnp.float32), jax.nn.relu(dots))
        causal = key_pos[None, :] <= pos_q[:, None]
        score = jnp.where(causal[None], score, -jnp.inf)
        _, idx = lax.top_k(score, k_sel)
        valid = idx <= pos_q[None, :, None]
        c_sel = gather(c, idx)
        logits = jnp.einsum('bqhl,bqkl->bqhk', qlb, c_sel).astype(jnp.float32) * (DSA_HEAD_DIM ** -0.5)
        logits = jnp.where(valid[:, :, None, :], logits, -jnp.inf)
        p = jax.nn.softmax(logits, axis=-1).astype(c.dtype)
        o_lat = jnp.einsum('bqhk,bqkl->bqhl', p, c_sel)
        o = jnp.einsum('bqhl,hld->bqhd', o_lat, w_uv)
        return o.reshape(bsz, Q_BLOCK, W)

    nb = s // Q_BLOCK
    out = lax.map(block, (to_blocks(q_lat), to_blocks(qi), to_blocks(wi), jnp.arange(nb)))
    return from_blocks(out)

def short_gated_conv(b_gate, c_gate, x_in, conv_w):
    s = x_in.shape[1]
    y = c_gate * x_in
    yp = jnp.pad(y, ((0, 0), (CONV_WIDTH - 1, 0), (0, 0)))
    conv = conv_w[0] * yp[:, 0:s]
    for j in range(1, CONV_WIDTH):
        conv = conv + conv_w[j] * yp[:, j:j + s]
    return b_gate * conv

def forgetting_attention(q, k, v, f_logit, b_f):
    bsz, s, _ = q.shape
    qh = q.reshape(bsz, s, FOX_HEADS, FOX_HEAD_DIM)
    kh = k.reshape(bsz, s, FOX_HEADS, FOX_HEAD_DIM)
    vh = v.reshape(bsz, s, FOX_HEADS, FOX_HEAD_DIM)
    cum = jnp.cumsum(jax.nn.log_sigmoid((f_logit + b_f).astype(jnp.float32)), axis=1)
    cum_k = jnp.transpose(cum, (0, 2, 1))
    key_pos = jnp.arange(s)

    def block(args):
        qb, cq, blk = args
        pos_q = blk * Q_BLOCK + jnp.arange(Q_BLOCK)
        logits = jnp.einsum('bqhd,bshd->bhqs', qb, kh).astype(jnp.float32) * (FOX_HEAD_DIM ** -0.5)
        logits = logits + jnp.transpose(cq, (0, 2, 1))[..., None] - cum_k[:, :, None, :]
        logits = jnp.where((key_pos[None, :] <= pos_q[:, None])[None, None], logits, -jnp.inf)
        p = jax.nn.softmax(logits, axis=-1).astype(vh.dtype)
        o = jnp.einsum('bhqs,bshd->bqhd', p, vh)
        return o.reshape(bsz, Q_BLOCK, W)

    nb = s // Q_BLOCK
    out = lax.map(block, (to_blocks(qh), to_blocks(cum), jnp.arange(nb)))
    return from_blocks(out)

def hybrid_layer(x, norm_g, w_in, gm_ln_g, gm_ln_b, gm_w_s, gm_b_s, dsa_kv_g, dsa_w_uk, dsa_w_uv,
                 conv_w, fox_b_f, w_branch, w_out):
    bsz, s, d = x.shape
    h = rms_norm(x, norm_g)
    proj = h @ w_in
    points = [int(p) for p in np.cumsum(np.array(IN_SPLITS))[:-1]]
    (a_u, a_v, a_z,
     b_q, b_c, b_qi, b_ki, b_wi, b_z,
     c_b, c_c, c_x, c_z,
     d_q, d_k, d_v, d_f, d_z,
     gates) = jnp.split(proj, points, axis=-1)
    y_a = chunked_spatial_gating(a_u, a_v, gm_ln_g, gm_ln_b, gm_w_s, gm_b_s) * jax.nn.silu(a_z)
    y_b = dsa_attention(b_q, b_c, b_qi, b_ki, b_wi, dsa_kv_g, dsa_w_uk, dsa_w_uv) * jax.nn.silu(b_z)
    y_c = short_gated_conv(c_b, c_c, c_x, conv_w) * jax.nn.silu(c_z)
    y_d = forgetting_attention(d_q, d_k, d_v, d_f, fox_b_f) * jax.nn.silu(d_z)
    ys = jnp.stack([y_a, y_b, y_c, y_d], axis=0)
    branch_d = jnp.einsum('nbsw,nwd->bsnd', ys, w_branch)
    g = jax.nn.sigmoid(gates.reshape(bsz, s, N_BRANCH, d))
    merged = jnp.sum(g * branch_d, axis=2)
    return x + merged @ w_out

def first_inputs(seed: int = 0) -> dict:
    key = jax.random.key(seed)
    ks = jax.random.split(key, 16)
    f32 = jnp.float32
    nrm = lambda k, shp, sc: jax.random.normal(k, shp, f32) * sc
    return {
        'x': nrm(ks[0], (BATCH, SEQ, D_MODEL), 1.0),
        'norm_g': 1.0 + nrm(ks[1], (DEPTH, D_MODEL), 0.05),
        'w_in': nrm(ks[2], (DEPTH, D_MODEL, IN_WIDTH), D_MODEL ** -0.5),
        'gm_ln_g': 1.0 + nrm(ks[3], (DEPTH, W), 0.05),
        'gm_ln_b': nrm(ks[4], (DEPTH, W), 0.02),
        'gm_w_s': nrm(ks[5], (DEPTH, GM_GROUPS, GM_CHUNK, GM_CHUNK), GM_CHUNK ** -0.5),
        'gm_b_s': 1.0 + nrm(ks[6], (DEPTH, GM_GROUPS, GM_CHUNK), 0.1),
        'dsa_kv_g': 1.0 + nrm(ks[7], (DEPTH, DSA_LATENT), 0.05),
        'dsa_w_uk': nrm(ks[8], (DEPTH, DSA_HEADS, DSA_LATENT, DSA_HEAD_DIM), DSA_LATENT ** -0.5),
        'dsa_w_uv': nrm(ks[9], (DEPTH, DSA_HEADS, DSA_LATENT, DSA_HEAD_DIM), DSA_LATENT ** -0.5),
        'conv_w': nrm(ks[10], (DEPTH, CONV_WIDTH, W), CONV_WIDTH ** -0.5),
        'fox_b_f': jax.random.uniform(ks[11], (DEPTH, FOX_HEADS), f32, minval=1.0, maxval=4.0),
        'w_branch': nrm(ks[12], (DEPTH, N_BRANCH, W, D_MODEL), W ** -0.5),
        'w_out': nrm(ks[13], (DEPTH, D_MODEL, D_MODEL), 0.5 * D_MODEL ** -0.5),
        'final_g': 1.0 + nrm(ks[14], (D_MODEL,), 0.05),
    }

def first_block(x, norm_g, w_in, gm_ln_g, gm_ln_b, gm_w_s, gm_b_s, dsa_kv_g, dsa_w_uk, dsa_w_uv,
              conv_w, fox_b_f, w_branch, w_out, final_g):
    h = x
    for l in range(DEPTH):
        h = hybrid_layer(h, norm_g[l], w_in[l], gm_ln_g[l], gm_ln_b[l], gm_w_s[l], gm_b_s[l],
                         dsa_kv_g[l], dsa_w_uk[l], dsa_w_uv[l], conv_w[l], fox_b_f[l],
                         w_branch[l], w_out[l])
    return rms_norm(h, final_g)


N_META = 16
CHUNK = 64
META_PAD = (-N_META) % CHUNK
N_FGROUPS = 4
FGROUP_DIM = 128
F_WIDTH = N_FGROUPS * FGROUP_DIM
N_HEADS = 8
HEAD_DK = 128
HEAD_DV = 128
QK_WIDTH = N_HEADS * HEAD_DK
V_WIDTH = N_HEADS * HEAD_DV
QKV_WIDTH = 2 * QK_WIDTH + V_WIDTH
CONV_K = 5
SPLIT_SIZES = (F_WIDTH, QKV_WIDTH, V_WIDTH, 4 * N_HEADS, D_MODEL, D_MODEL)
IN_WIDTH_2 = sum(SPLIT_SIZES)
N_GROUPS = 8
EXPERTS_PER_GROUP = 8
N_EXPERTS = N_GROUPS * EXPERTS_PER_GROUP
TOP_K = 2
D_EXPERT = 256
EXPERT_BLOCK = 128
NORM_EPS = 1e-6


def rms_norm_2(x, gain):
    xf = x.astype(jnp.float32)
    y = xf * lax.rsqrt(jnp.mean(xf * xf, axis=-1, keepdims=True) + NORM_EPS)
    return (y * gain.astype(jnp.float32)).astype(x.dtype)

def l2_normalize(x):
    return x * lax.rsqrt(jnp.sum(x * x, axis=-1, keepdims=True) + NORM_EPS)

def depthwise_conv_centred(x, w):
    k = w.shape[0]
    return lax.conv_general_dilated(
        x, w[:, None, :].astype(x.dtype), window_strides=(1,),
        padding=[((k - 1) // 2, k // 2)],
        dimension_numbers=("NWC", "WIO", "NWC"),
        feature_group_count=x.shape[-1])

def gated_delta_chunked(q, k, v, g, beta):
    b, h, lp, dk = k.shape
    dv = v.shape[-1]
    nc = lp // CHUNK
    q = q.reshape(b, h, nc, CHUNK, dk)
    k = k.reshape(b, h, nc, CHUNK, dk)
    v = v.reshape(b, h, nc, CHUNK, dv)
    beta = beta.reshape(b, h, nc, CHUNK)
    g = jnp.cumsum(g.reshape(b, h, nc, CHUNK), axis=-1)
    lower = jnp.tril(jnp.ones((CHUNK, CHUNK), dtype=bool))
    strict = jnp.tril(jnp.ones((CHUNK, CHUNK), dtype=bool), -1)
    diff = g[..., :, None] - g[..., None, :]
    decay = jnp.where(lower, jnp.exp(jnp.where(lower, diff, 0.0)), 0.0)
    k_beta = k * beta[..., None]
    a_mat = jnp.where(strict, jnp.einsum("bhncd,bhnsd->bhncs", k_beta, k) * decay, 0.0)
    eye = jnp.eye(CHUNK, dtype=a_mat.dtype)
    t_mat = lax.linalg.triangular_solve(
        eye + a_mat, jnp.broadcast_to(eye, a_mat.shape),
        left_side=True, lower=True, unit_diagonal=True)
    u = jnp.einsum("bhncs,bhnsv->bhncv", t_mat, v * beta[..., None])
    w = jnp.einsum("bhncs,bhnsd->bhncd", t_mat, k_beta * jnp.exp(g)[..., None])
    qk = jnp.where(lower, jnp.einsum("bhncd,bhnsd->bhncs", q, k) * decay, 0.0)
    q_dec = q * jnp.exp(g)[..., None]
    k_dec = k * jnp.exp(g[..., -1:] - g)[..., None]
    chunk_decay = jnp.exp(g[..., -1])

    def step(state, inp):
        q_c, k_c, u_c, w_c, qk_c, dec_c = inp
        v_new = u_c - jnp.einsum("bhcd,bhdv->bhcv", w_c, state)
        o_c = (jnp.einsum("bhcd,bhdv->bhcv", q_c, state)
               + jnp.einsum("bhcs,bhsv->bhcv", qk_c, v_new))
        state = state * dec_c[..., None, None] + jnp.einsum("bhcd,bhcv->bhdv", k_c, v_new)
        return state, o_c

    xs = tuple(jnp.moveaxis(t, 2, 0) for t in (q_dec, k_dec, u, w, qk, chunk_decay))
    state0 = jnp.zeros((b, h, dk, dv), jnp.float32)
    _, o = lax.scan(step, state0, xs)
    return jnp.moveaxis(o, 0, 2).reshape(b, h, lp, dv)

def pad_to_chunks(t):
    t = jnp.pad(t, [(0, 0), (META_PAD, 0)] + [(0, 0)] * (t.ndim - 2))
    return jnp.moveaxis(t, 1, 2)

def hybrid_mixer(h, norm_g, w_in, conv_w, a_log_f, dt_bias_f, a_log_b, dt_bias_b,
                 out_norm_g, w_fourier, w_delta, w_out):
    bsz, seq_len, _ = h.shape
    hn = rms_norm_2(h, norm_g)
    proj = hn @ w_in
    points = np.cumsum(SPLIT_SIZES)[:-1].tolist()
    f_in, qkv, z, ab, gate_f, gate_d = jnp.split(proj, points, axis=-1)

    fg = f_in.reshape(bsz, seq_len, N_FGROUPS, FGROUP_DIM).astype(jnp.float32)
    f_mix = jnp.real(jnp.fft.fft2(fg, axes=(1, 3), norm="ortho")).astype(h.dtype)
    y_f = f_mix.reshape(bsz, seq_len, F_WIDTH) @ w_fourier

    qkv = jax.nn.silu(depthwise_conv_centred(qkv, conv_w))
    q, k, v = jnp.split(qkv, [QK_WIDTH, 2 * QK_WIDTH], axis=-1)
    q = l2_normalize(q.reshape(bsz, seq_len, N_HEADS, HEAD_DK).astype(jnp.float32)) * (HEAD_DK ** -0.5)
    k = l2_normalize(k.reshape(bsz, seq_len, N_HEADS, HEAD_DK).astype(jnp.float32))
    v = v.reshape(bsz, seq_len, N_HEADS, HEAD_DV).astype(jnp.float32)
    a_f, b_f, a_b, b_b = jnp.split(ab.astype(jnp.float32), 4, axis=-1)
    g_f = -jnp.exp(a_log_f.astype(jnp.float32)) * jax.nn.softplus(a_f + dt_bias_f.astype(jnp.float32))
    g_b = -jnp.exp(a_log_b.astype(jnp.float32)) * jax.nn.softplus(a_b + dt_bias_b.astype(jnp.float32))
    beta_f = jax.nn.sigmoid(b_f)
    beta_b = jax.nn.sigmoid(b_b)

    qp, kp, vp = pad_to_chunks(q), pad_to_chunks(k), pad_to_chunks(v)
    o_fwd = gated_delta_chunked(qp, kp, vp, pad_to_chunks(g_f), pad_to_chunks(beta_f))
    flip = lambda t: jnp.flip(t, axis=2)
    o_bwd = flip(gated_delta_chunked(flip(qp), flip(kp), flip(vp),
                                     flip(pad_to_chunks(g_b)), flip(pad_to_chunks(beta_b))))
    o = jnp.moveaxis(o_fwd + o_bwd, 1, 2)[:, META_PAD:]
    zf = z.reshape(bsz, seq_len, N_HEADS, HEAD_DV).astype(jnp.float32)
    o = rms_norm_2(o, out_norm_g) * jax.nn.silu(zf)
    y_d = o.reshape(bsz, seq_len, V_WIDTH).astype(h.dtype) @ w_delta

    merged = jax.nn.sigmoid(gate_f) * y_f + jax.nn.sigmoid(gate_d) * y_d
    return merged @ w_out

def hierarchical_moe(h, norm_g, w_rg, b_rg, w_re, b_re, w_gate, w_up, w_down):
    bsz, seq_len, d = h.shape
    hn = rms_norm_2(h, norm_g).reshape(-1, d)
    n_tok = hn.shape[0]
    gl = (hn @ w_rg).astype(jnp.float32) + b_rg.astype(jnp.float32)
    gp = jax.nn.softmax(gl, axis=-1)
    p_group, g_idx = lax.top_k(gp, 1)
    el = (hn @ w_re).astype(jnp.float32) + b_re.astype(jnp.float32)
    el = el.reshape(n_tok, N_GROUPS, EXPERTS_PER_GROUP)
    el_g = jnp.take_along_axis(el, g_idx[:, :, None], axis=1)[:, 0]
    ep = jax.nn.softmax(el_g, axis=-1)
    top_w, top_i = lax.top_k(ep, TOP_K)
    top_w = top_w / jnp.sum(top_w, axis=-1, keepdims=True)
    weights = p_group * top_w
    expert_idx = g_idx * EXPERTS_PER_GROUP + top_i

    n_assign = n_tok * TOP_K
    n_blocks = -(-n_assign // EXPERT_BLOCK) + N_EXPERTS
    n_slots = n_blocks * EXPERT_BLOCK
    flat_e = expert_idx.reshape(-1).astype(jnp.int32)
    flat_tok = jnp.repeat(jnp.arange(n_tok, dtype=jnp.int32), TOP_K)
    flat_w = weights.reshape(-1)
    order = jnp.argsort(flat_e, stable=True)
    e_sorted = flat_e[order]
    counts = jnp.bincount(flat_e, length=N_EXPERTS)
    padded_counts = (counts + EXPERT_BLOCK - 1) // EXPERT_BLOCK * EXPERT_BLOCK
    padded_ends = jnp.cumsum(padded_counts)
    padded_start = padded_ends - padded_counts
    start = jnp.cumsum(counts) - counts
    rank = jnp.arange(n_assign, dtype=jnp.int32) - start[e_sorted]
    dest = padded_start[e_sorted] + rank
    slot_tok = jnp.zeros((n_slots,), jnp.int32).at[dest].set(flat_tok[order])
    slot_w = jnp.zeros((n_slots,), hn.dtype).at[dest].set(flat_w[order].astype(hn.dtype))
    block_start = jnp.arange(n_blocks, dtype=jnp.int32) * EXPERT_BLOCK
    block_expert = jnp.minimum(jnp.searchsorted(padded_ends, block_start, side="right"),
                               N_EXPERTS - 1).astype(jnp.int32)
    xb = hn[slot_tok].reshape(n_blocks, EXPERT_BLOCK, d)

    def expert_block(args):
        x_blk, e = args
        return (jax.nn.silu(x_blk @ w_gate[e]) * (x_blk @ w_up[e])) @ w_down[e]

    yb = lax.map(expert_block, (xb, block_expert)).reshape(n_slots, d)
    out = jnp.zeros((n_tok, d), hn.dtype).at[slot_tok].add(yb * slot_w[:, None])
    return out.reshape(bsz, seq_len, d)

def second_inputs(seed: int = 0) -> dict:
    key = jax.random.key(seed)
    ks = jax.random.split(key, 24)
    nrm = lambda k, shape, scale: jax.random.normal(k, shape, jnp.float32) * scale
    gain = lambda k, shape: 1.0 + 0.05 * jax.random.normal(k, shape, jnp.float32)

    def a_log(k):
        return jnp.log(jax.random.uniform(k, (DEPTH, N_HEADS), jnp.float32, minval=1.0, maxval=16.0))

    def dt_bias(k):
        dt = jnp.exp(jax.random.uniform(k, (DEPTH, N_HEADS), jnp.float32,
                                        minval=math.log(1e-3), maxval=math.log(1e-1)))
        return dt + jnp.log(-jnp.expm1(-dt))

    return {
        "x": nrm(ks[0], (BATCH, SEQ, D_MODEL), 1.0),
        "meta_tokens": nrm(ks[1], (N_META, D_MODEL), 1.0),
        "norm1_g": gain(ks[2], (DEPTH, D_MODEL)),
        "w_in": nrm(ks[3], (DEPTH, D_MODEL, IN_WIDTH_2), D_MODEL ** -0.5),
        "conv_w": nrm(ks[4], (DEPTH, CONV_K, QKV_WIDTH), CONV_K ** -0.5),
        "a_log_fwd": a_log(ks[5]),
        "dt_bias_fwd": dt_bias(ks[6]),
        "a_log_bwd": a_log(ks[7]),
        "dt_bias_bwd": dt_bias(ks[8]),
        "out_norm_g": gain(ks[9], (DEPTH, HEAD_DV)),
        "w_fourier": nrm(ks[10], (DEPTH, F_WIDTH, D_MODEL), F_WIDTH ** -0.5),
        "w_delta": nrm(ks[11], (DEPTH, V_WIDTH, D_MODEL), V_WIDTH ** -0.5),
        "w_out": nrm(ks[12], (DEPTH, D_MODEL, D_MODEL), D_MODEL ** -0.5),
        "norm2_g": gain(ks[13], (DEPTH, D_MODEL)),
        "w_router_group": nrm(ks[14], (DEPTH, D_MODEL, N_GROUPS), D_MODEL ** -0.5),
        "b_router_group": nrm(ks[15], (DEPTH, N_GROUPS), 0.01),
        "w_router_expert": nrm(ks[16], (DEPTH, D_MODEL, N_EXPERTS), D_MODEL ** -0.5),
        "b_router_expert": nrm(ks[17], (DEPTH, N_EXPERTS), 0.01),
        "w_gate_e": nrm(ks[18], (DEPTH, N_EXPERTS, D_MODEL, D_EXPERT), D_MODEL ** -0.5),
        "w_up_e": nrm(ks[19], (DEPTH, N_EXPERTS, D_MODEL, D_EXPERT), D_MODEL ** -0.5),
        "w_down_e": nrm(ks[20], (DEPTH, N_EXPERTS, D_EXPERT, D_MODEL), D_EXPERT ** -0.5),
        "final_norm_g": gain(ks[21], (D_MODEL,)),
    }

def second_block(x, meta_tokens, norm1_g, w_in, conv_w, a_log_fwd, dt_bias_fwd, a_log_bwd,
              dt_bias_bwd, out_norm_g, w_fourier, w_delta, w_out, norm2_g, w_router_group,
              b_router_group, w_router_expert, b_router_expert, w_gate_e, w_up_e, w_down_e,
              final_norm_g):
    bsz = x.shape[0]
    meta = jnp.broadcast_to(meta_tokens[None].astype(x.dtype), (bsz, N_META, D_MODEL))
    h = jnp.concatenate([meta, x], axis=1)
    for layer in range(DEPTH):
        h = h + hybrid_mixer(h, norm1_g[layer], w_in[layer], conv_w[layer],
                             a_log_fwd[layer], dt_bias_fwd[layer], a_log_bwd[layer],
                             dt_bias_bwd[layer], out_norm_g[layer], w_fourier[layer],
                             w_delta[layer], w_out[layer])
        h = h + hierarchical_moe(h, norm2_g[layer], w_router_group[layer], b_router_group[layer],
                                 w_router_expert[layer], b_router_expert[layer],
                                 w_gate_e[layer], w_up_e[layer], w_down_e[layer])
    return rms_norm_2(h, final_norm_g)[:, N_META:]


def setup_inputs(seed=0):
    out = dict(first_inputs(seed))
    for name, value in second_inputs(seed + 1).items():
        if name != "x":
            out[name + "_2"] = value
    return out


def reference(
    x, norm_g, w_in, gm_ln_g, gm_ln_b, gm_w_s, gm_b_s, dsa_kv_g, dsa_w_uk, dsa_w_uv, conv_w,
    fox_b_f, w_branch, w_out, final_g, meta_tokens_2, norm1_g_2, w_in_2, conv_w_2, a_log_fwd_2,
    dt_bias_fwd_2, a_log_bwd_2, dt_bias_bwd_2, out_norm_g_2, w_fourier_2, w_delta_2, w_out_2,
    norm2_g_2, w_router_group_2, b_router_group_2, w_router_expert_2, b_router_expert_2,
    w_gate_e_2, w_up_e_2, w_down_e_2, final_norm_g_2,
):
    x = first_block(
        x, norm_g, w_in, gm_ln_g, gm_ln_b, gm_w_s, gm_b_s, dsa_kv_g, dsa_w_uk, dsa_w_uv, conv_w,
        fox_b_f, w_branch, w_out, final_g,
    )
    return second_block(
        x, meta_tokens_2, norm1_g_2, w_in_2, conv_w_2, a_log_fwd_2, dt_bias_fwd_2, a_log_bwd_2,
        dt_bias_bwd_2, out_norm_g_2, w_fourier_2, w_delta_2, w_out_2, norm2_g_2,
        w_router_group_2, b_router_group_2, w_router_expert_2, b_router_expert_2, w_gate_e_2,
        w_up_e_2, w_down_e_2, final_norm_g_2,
    )


_drawn_inputs = setup_inputs


def setup_inputs(seed=0):
    import zlib

    import numpy as np

    out = dict(_drawn_inputs(seed))
    spreads = {}
    factors = {'gm_ln_g': 3.941,
     'gm_ln_b': 8.0,
     'dsa_kv_g': 5.136,
     'fox_b_f': 2.703,
     'out_norm_g_2': 3.178,
     'b_router_group_2': 7.25,
     'b_router_expert_2': 7.294}
    for name, (base, spread) in spreads.items():
        noise = np.random.default_rng([zlib.crc32(name.encode()), seed]).standard_normal(out[name].shape)
        drawn = base * np.exp(spread * noise) if base else spread * noise
        out[name] = jnp.asarray(drawn.astype(out[name].dtype))
    for name, factor in factors.items():
        out[name] = (out[name] * factor).astype(out[name].dtype)
    return out
```

```python
from contextlib import ExitStack

import numpy as np

import concourse.bass as bass
from concourse import mybir

D = 1024
SEQ = 256
P = 128
KD = D // P
TT = SEQ // P
META = 16
LEN = SEQ + META
W1 = 512
CW = W1 // P
NH = 4
TOPK = SEQ // 4
IDX = 64
EPS = 1e-6
BIG = 3e38
HEADS = 8
EXPERTS, GROUPS, FE = 64, 8, 256
SLOTS = 4
BLOCK = 4096
PER, CAP = 4, 32
MOST = SEQ // CAP

COLS, _at = {}, 0
for _n, _w in (("norm_g", KD), ("final_g", KD), ("conv_w", 3 * CW), ("kv_g", 1), ("b_f", 1), ("norm1_g", KD),
               ("norm2_g", KD), ("last_g", KD), ("conv5", 5 * 24), ("out_g", 1)):
    COLS[_n] = (_at, _at + _w)
    _at += _w
N_COLS = _at
ROWS, _at = {}, 0
for _n, _w in (("dt", 16), ("a_log", 16), ("b_router", 72)):
    ROWS[_n] = (_at, _at + _w)
    _at += _w
N_ROWS = _at


class Fill:

    def __init__(self, b, n, bank):
        self.b, self.n, self.bank = b, n, bank


class Lane:

    def __init__(self, i, d, tile, half):
        self.i, self.d, self.tile, self.half, self.r = i, d, tile, half, 0
        self.hs = list(range(HEADS)) if tile == 0 else list(range(4 * half, 4 * half + 4))
        self.n = META if tile == 0 else P
        self.at = 0 if tile == 0 else META + (tile - 1) * P
        self.j = 0 if d == "f" else 8
        self.levels = 4 if tile == 0 else 7
        self.key = f"{d}{tile}{half}"
        self.s_before, self.first_out = 0, False


class Work:

    def __init__(self, u, a, am, t, z, tt, qk=None, qd=None, x=None, z2=None):
        self.u, self.a, self.am, self.t, self.z, self.tt = u, a, am, t, z, tt
        self.qk, self.qd, self.x, self.z2 = qk, qd, x, z2


def build(nc, A):
    f32 = mybir.dt.float32
    ALU, ACT, AX = mybir.AluOpType, mybir.ActivationFunctionType, mybir.AxisListType
    ctx = ExitStack()
    with ctx:
        sems = {}

        def sem(name):
            if name not in sems:
                sems[name] = ctx.enter_context(nc.semaphore(name))
            return sems[name]

        ARENA = 53208
        arena = ctx.enter_context(nc.sbuf_tensor("arena", [P, ARENA], f32))
        top = [0]

        def place(cols):
            at = top[0]
            top[0] += cols
            assert top[0] <= ARENA, top[0]
            return arena[:, at:at + cols]

        ring = [place(BLOCK) for _ in range(SLOTS)]
        res = place(KD * LEN).rearrange("p (k t) -> p k t", k=KD)
        cols = place(N_COLS)
        consts_at = top[0]
        ident = place(P)
        ones = place(P)
        mask = place(2 * P)
        stats = place(256)
        rows = place(N_ROWS)
        tri = place(4 * P)
        layer_base = top[0]

        def col(name, j=0):
            a = COLS[name][0]
            return cols[:, a + j:a + j + 1]

        stat_at = [0]

        def stat(n):
            a = stat_at[0]
            stat_at[0] += n
            assert stat_at[0] <= 256
            return stats[:, a:a + n]

        banks = [ctx.enter_context(nc.psum_tensor(f"bank{b}", [P, 512], f32)) for b in range(8)]
        full = [sem(f"bank{b}_full") for b in range(8)]
        free = [sem(f"bank{b}_free") for b in range(8)]
        fills, uses, turn, readers = {}, [0] * 8, {}, {}

        def fill(name, pool, block=None):
            b = pool[turn.get(pool, 0) % len(pool)]
            turn[pool] = turn.get(pool, 0) + 1
            fills[name] = Fill(b, uses[b], banks[b])
            uses[b] += 1
            if block is not None:
                readers[block] = fills[name]

        PJ, WK = (0, 1, 2), (3, 4, 5, 6, 7)
        MIX, IDXB, BQ, DQ, DK, DV, AV, AU, AZ, DZ, BZ, CB, CC, CX, CZ = range(15)
        ORDER = (0, 3, 2, 1)
        GATE = {n: 15 + 3 * i for i, n in enumerate(ORDER)}
        WB = {n: 17 + 3 * i for i, n in enumerate(ORDER)}
        WO = 27
        blk = lambda b: b - 1
        FIN, K0, V0, WF, GF, Q0, K1, V1, Q1, ZB, GD, WD, WO2 = 28, 29, 30, 31, 32, 34, 35, 36, 37, 38, 40, 41, 44
        N_BLOCKS = 46

        top[0] = layer_base
        g_ = lambda n: place(n)
        h1 = g_(KD * SEQ).rearrange("p (k t) -> p k t", k=KD)
        tmp = g_(KD * SEQ)
        qi = g_(2 * SEQ).rearrange("p (k t) -> p k t", k=2)
        ki = g_(SEQ)
        cn = g_(TT * P).rearrange("p (k t) -> p k t", k=TT)
        wi = stat(TT * NH)
        cT = g_(SEQ)
        ff = g_(5 * SEQ).rearrange("p (k t) -> p k t", k=5)
        sel = g_(NH * SEQ).rearrange("p (h t) -> p h t", h=NH)
        bq = g_(CW * SEQ).rearrange("p (k t) -> p k t", k=CW)
        qlat = g_(CW * SEQ).rearrange("p (k t) -> p k t", k=CW)
        dq = g_(CW * SEQ).rearrange("p (k t) -> p k t", k=CW)
        dk = g_(CW * SEQ).rearrange("p (k t) -> p k t", k=CW)
        dv = g_(TT * W1).rearrange("p (k t) -> p k t", k=TT)
        av = g_(TT * W1).rearrange("p (k t) -> p k t", k=TT)
        ln_rows = g_(2 * W1)
        relu0 = g_(NH * P).rearrange("p (h k) -> p h k", h=NH)
        relu1 = g_(NH * SEQ).rearrange("p (h k) -> p h k", h=NH)
        score = [g_(P), g_(SEQ)]
        lg = {a: [g_(NH * P).rearrange("p (h k) -> p h k", h=NH), g_(NH * SEQ).rearrange("p (h k) -> p h k", h=NH)] for a in "fb"}
        pT = g_(3 * NH * P).rearrange("p (j h q) -> p j h q", j=3, h=NH)
        olat = g_(NH * SEQ).rearrange("p (h t) -> p h t", h=NH)
        wuk = g_(NH * P).rearrange("p (h l) -> p h l", h=NH)
        wuv = g_(NH * P).rearrange("p (h l) -> p h l", h=NH)
        wsT = g_(NH * P).rearrange("p (h l) -> p h l", h=NH)
        bs = g_(NH * P)
        y = [g_(CW * SEQ).rearrange("p (k t) -> p k t", k=CW) for _ in range(4)]
        cpad = g_(CW * (SEQ + 2)).rearrange("p (k t) -> p k t", k=CW)
        cc = relu1
        cv = lg["f"][1]
        rms = g_(SEQ)
        css, lnsd, best, bns, mv = stat(TT), stat(TT), stat(8), stat(6), stat(4)
        nmax = {a: stat(TT * NH) for a in "fb"}
        psum = {a: stat(TT * NH) for a in "fb"}
        merged = g_(KD * SEQ).rearrange("p (k t) -> p k t", k=KD)

        top[0] = layer_base
        hn = place(KD * LEN).rearrange("p (k t) -> p k t", k=KD)
        qT = place(HEADS * SEQ).rearrange("p (h t) -> p h t", h=HEADS)
        kT = place(HEADS * LEN).rearrange("p (h t) -> p h t", h=HEADS)
        k_tok = place(TT * D).rearrange("p (t c) -> p t c", t=TT)
        v_tok = place(TT * D).rearrange("p (t c) -> p t c", t=TT)
        y_four = place(KD * SEQ).rearrange("p (k t) -> p k t", k=KD)
        o_T = place(HEADS * SEQ).rearrange("p (h t) -> p h t", h=HEADS)
        state = {d: place(D) for d in "fb"}
        level_mask = place(14 * P)
        gate_at = top[0]
        beta = place(3 * 16).rearrange("p (t j) -> p t j", t=3)
        gl = place(3 * 16).rearrange("p (t j) -> p t j", t=3)
        gx = place(3 * 16).rearrange("p (t j) -> p t j", t=3)
        gsum = place(3 * 32).rearrange("p (t j) -> p t j", t=3)
        edec = place(3 * 16).rearrange("p (t j) -> p t j", t=3)
        krem = place(3 * 16).rearrange("p (t j) -> p t j", t=3)
        eall = place(3 * 16).rearrange("p (t j) -> p t j", t=3)
        nea = place(16)
        k_meta, v_meta = (o_T[:, 4 * i:4 * i + 4, :].rearrange("p h t -> p (h t)") for i in range(2))
        zone = top[0]
        rms2 = place(LEN)
        dft_d = place(2 * P)
        dft_l = place(3 * 2 * SEQ).rearrange("p (t c) -> p t c", t=3)
        w_ab = place(KD * 32).rearrange("p (k c) -> p k c", k=KD)
        f_T = place(4 * LEN).rearrange("p (g t) -> p g t", g=4)
        fa = place(2 * 4 * 2 * P).rearrange("p (t g c) -> p t g c", t=2, g=4)
        fa0 = place(4 * 2 * P).rearrange("p (g c) -> p g c", g=4)
        yf_T = place(4 * SEQ).rearrange("p (g t) -> p g t", g=4)
        gate2 = place(2 * 512).rearrange("p (j k t) -> p j k t", j=2, k=2)
        sq2 = place(4 * LEN).rearrange("p (h t) -> p h t", h=4)
        rn2 = place(4 * LEN).rearrange("p (h t) -> p h t", h=4)
        v_T = [place(4 * LEN).rearrange("p (h t) -> p h t", h=4) for _ in range(2)]
        top[0] = zone
        four = lambda: place(512).rearrange("p (h c) -> p h c", h=4)
        lane_u = [four() for _ in range(2)]
        lane_z = lane_u
        lane_a = [four() for _ in range(2)]
        lane_am = [[four() for _ in range(2)] for _ in range(2)]
        lane_t = [four() for _ in range(2)]
        lane_tt = [[four() for _ in range(2)] for _ in range(2)]
        lane_qk = [[four() for _ in range(2)] for _ in range(2)]
        lane_qd = [[four() for _ in range(2)] for _ in range(2)]
        x_meta = arena[:, top[0]:top[0] + D]
        lane_x = [four() for _ in range(2)]
        mt_at = top[0]
        lane_z2 = [four() for _ in range(2)]
        lanes_end = top[0]
        top[0] = mt_at
        mt = {n: place(P).rearrange("p (h c) -> p h c", h=HEADS) for n in ("u", "a", "am0", "am1", "t", "z", "tt")}
        assert top[0] <= lanes_end
        o_sq = k_tok.rearrange("p t c -> p (t c)").rearrange("p (h t) -> p h t", h=HEADS)
        o_rn = v_tok.rearrange("p t c -> p (t c)").rearrange("p (h t) -> p h t", h=HEADS)
        z_g = kT.rearrange("p h t -> p (h t)")[:, 0:4 * 512].rearrange("p (j k t) -> p j k t", j=4, k=2)

        sq_all = arena[:, layer_base + 3 * KD * LEN:layer_base + 4 * KD * LEN].rearrange("p (k t) -> p k t", k=KD)

        meta = Lane(2, "f", 0, 0)
        ROUNDS = [[Lane(0, "f", 1, 0), Lane(1, "b", 2, 0)], [Lane(0, "f", 1, 1), Lane(1, "b", 2, 1)],
                  [Lane(0, "f", 2, 0), Lane(1, "b", 1, 0)], [Lane(0, "f", 2, 1), Lane(1, "b", 1, 1)]]
        for _r, _round in enumerate(ROUNDS):
            for _l in _round:
                _l.r = _r
        meta.r = 0
        for _l in (x for r in ROUNDS for x in r):
            _l.s_before = {"f": 2, "b": 2}[_l.d] + (0 if _l.r < 2 else (_l.r % 2) + 1)
            _l.first_out = _l.r < 2
        tt_end = {meta.key: 4} | {x.key: 7 * (x.r + 1) for r in ROUNDS for x in r}

        def work(l):
            if l.tile == 0:
                return Work(u=mt["u"], a=mt["a"], am=[mt["am0"], mt["am1"]], t=mt["t"], z=mt["z"], tt=mt["tt"])
            i, p = l.i, l.r % 2
            return Work(u=lane_u[i], a=lane_a[i], am=lane_am[i], t=lane_t[i], z=lane_z[i], tt=lane_tt[i][p],
                                   qk=lane_qk[i][p], qd=lane_qd[i][p], x=lane_x[i], z2=lane_z2[i])

        def heads_of(f, l):
            return f.bank[0:l.n, 0:len(l.hs) * l.n].rearrange("p (h c) -> p h c", h=len(l.hs))

        LE, GE = 0, 1
        amask = lambda m: tri[:, m * P:(m + 1) * P]
        omask = lambda m: tri[:, (2 + m) * P:(3 + m) * P]
        upto = lambda l: LE if l.d == "f" else GE

        top[0] = layer_base
        m_T = place(KD * SEQ).rearrange("p (k t) -> p k t", k=KD)
        m_tok = place(TT * D).rearrange("p (t c) -> p t c", t=TT)
        w_router = place(KD * 72).rearrange("p (k c) -> p k c", k=KD)
        rms4 = place(SEQ)
        router = place(TT * 72).rearrange("p (t c) -> p t c", t=TT)
        r_eq = place(64)
        r_cum = place(64)
        r_ones = place(64)
        pick = [place(64) for _ in range(2)]
        chosen = place(TT * 64).rearrange("p (t e) -> p t e", t=TT)
        weight = place(TT * 64).rearrange("p (t e) -> p t e", t=TT)
        code = place(TT * 64).rearrange("p (t e) -> p t e", t=TT)
        slot_of = place(PER * CAP)
        passes_f = place(16)
        pick_m = place(TT * P).rearrange("p (t s) -> p t s", t=TT)
        pick_w = place(TT * P).rearrange("p (t s) -> p t s", t=TT)
        pick_T = place(SEQ)
        act_g = place(FE)
        hid = place(FE)
        hid_T = place(2 * P).rearrange("p (f s) -> p f s", f=2)
        passes_i = place(1)[0:1, :].bitcast(mybir.dt.int32)
        xg = m_T.rearrange("p k t -> p (k t)")[:, 0:D].rearrange("p (k s) -> p k s", k=KD)
        yb = m_T.rearrange("p k t -> p (k t)")[:, D:2 * D]
        assert top[0] <= ARENA - 6 * BLOCK and zone <= ARENA - 3 * BLOCK, (top[0], zone)
        top[0] = ARENA - 6 * BLOCK
        odd = [place(BLOCK) for _ in range(3)]
        down = [place(BLOCK) for _ in range(2)]
        odd.append(place(BLOCK))
        gate_up = [[ring[(N_BLOCKS + j) % SLOTS] for j in range(PER)], odd]
        N_GROUPS = EXPERTS // PER
        gate_up_in = [16 * ((N_BLOCKS + j) // SLOTS + 1) for j in range(PER)]
        o_sq5 = down[0][:, 0:KD * SEQ].rearrange("p (k t) -> p k t", k=KD)
        out_T = m_T
        r_exp = pick_m.rearrange("p t s -> p (t s)")[:, 0:TT * 72].rearrange("p (t c) -> p t c", t=TT)
        r_nmax, r_sum, r_top, r_second, r_oh = stat(4), stat(4), stat(8), stat(2), stat(8)
        cap_steps = stat(MOST)
        slot_i = pick_T[:, 0:PER * CAP].bitcast(mybir.dt.int32)
        steps_i = pick_T[:, P:P + MOST].bitcast(mybir.dt.int32)

        def read_passes(engine, e):
            e.wait_ge(sem("passes"), 1)
            return engine.value_load(passes_i, min_val=1, max_val=MOST)

        def link2(ins, e, name, value):
            ins.then_inc(sem(name), 1)
            e.wait_ge(sem(name), value)

        block = ctx.enter_context(nc.Block())
        FRONT = A["front"]

        def two(bank):
            return bank[:, :].rearrange("p (j t) -> p j t", j=2)

        @block.tensor
        def _(pe):
            def begin(name, pool=WK, block=None):
                fill(name, pool, block)
                f = fills[name]
                if f.n > 0:
                    pe.wait_ge(free[f.b], f.n)
                return f

            def end(f, last):
                last.then_inc(full[f.b], 1)

            def loaded(b):
                pe.wait_ge(sem(f"slot{b % SLOTS}_in"), 16 * (b // SLOTS + 1))
                return ring[b % SLOTS]

            def project_T(names, b, rhs, n, first=0, stride=W1, kk=KD, per=2, pool=PJ):
                w = loaded(b)
                for i, name in enumerate(names):
                    f = begin(name, pool, b)
                    for j in range(per):
                        for k in range(kk):
                            c = k * stride + first + (i * per + j) * P
                            last = nc.tensor.matmul(f.bank[:, j * n:(j + 1) * n], w[:, c:c + P], rhs[:, k, :],
                                                    start=k == 0, stop=k == kk - 1)
                    end(f, last)

            def project_tok(names, b):
                w = loaded(b)
                for t, name in enumerate(names):
                    f = begin(name, PJ, b)
                    for k in range(KD):
                        last = nc.tensor.matmul(f.bank[:, :], h1[:, k, t * P:(t + 1) * P],
                                                w[:, k * W1:(k + 1) * W1], start=k == 0, stop=k == KD - 1)
                    end(f, last)

            def column_sums(name, src, n):
                f = begin(name)
                for k in range(KD):
                    last = nc.tensor.matmul(f.bank[:, 0:n], ones, src[:, k, :], start=k == 0, stop=k == KD - 1)
                end(f, last)

            sq = tmp.rearrange("p (k t) -> p k t", k=KD)
            pe.wait_ge(sem("consts_in"), 16)
            pe.wait_ge(sem("squares"), 1)
            column_sums("ssq1", sq, SEQ)

            w = loaded(blk(IDXB))
            pe.wait_ge(sem("normed"), KD)
            f = begin("c", WK, blk(IDXB))
            for t in range(TT):
                for k in range(KD):
                    last = nc.tensor.matmul(f.bank[:, t * SEQ:t * SEQ + P + 4], h1[:, k, t * P:(t + 1) * P],
                                            w[:, k * W1:k * W1 + P + 4], start=k == 0, stop=k == KD - 1)
            end(f, last)
            f = begin("f", WK, blk(IDXB))
            for k in range(KD):
                last = nc.tensor.matmul(f.bank[0:NH, 0:SEQ], w[:, k * W1 + 132:k * W1 + 136], h1[:, k, :],
                                        start=k == 0, stop=k == KD - 1)
            end(f, last)
            f = begin("qi", PJ, blk(IDXB))
            for j in range(2):
                for k in range(KD):
                    c = k * W1 + 136 + j * P
                    last = nc.tensor.matmul(f.bank[:, j * SEQ:(j + 1) * SEQ], w[:, c:c + P], h1[:, k, :],
                                            start=k == 0, stop=k == KD - 1)
            end(f, last)
            f = begin("ki", PJ, blk(IDXB))
            for k in range(KD):
                c = k * W1 + 392
                for half in range(2):
                    last = nc.tensor.matmul(f.bank[IDX * half:IDX * (half + 1), 0:SEQ], w[:, c:c + IDX], h1[:, k, :],
                                            start=k == 0, stop=k == KD - 1)
            end(f, last)
            project_T(("bq0", "bq1"), blk(BQ), h1, SEQ)
            pe.wait_ge(sem("cn"), TT)
            f = begin("cT")
            for t in range(TT):
                last = nc.tensor.transpose(f.bank[:, t * P:(t + 1) * P], cn[:, t, :], ident)
            end(f, last)
            project_T(("dq0", "dq1"), blk(DQ), h1, SEQ)
            pe.wait_ge(sem("qiki"), 2)
            for n, (t, odd) in enumerate(((0, 0), (0, 1), (1, 0), (1, 1))):
                f = begin(f"dots{n}")
                for i, h in enumerate((odd, odd + 2)):
                    a = IDX * (h % 2)
                    m = P * (t + 1)
                    last = nc.tensor.matmul(f.bank[:, i * m:(i + 1) * m], qi[a:a + IDX, h // 2, t * P:(t + 1) * P],
                                            ki[a:a + IDX, 0:m], start=True, stop=True)
                end(f, last)
            project_T(("dk0", "dk1"), blk(DK), h1, SEQ)
            pe.wait_ge(sem("small_in"), 16 * 6)
            pe.wait_ge(sem("bq"), 2)
            for i in range(2):
                f = begin(f"qlat{i}", PJ)
                for j in range(2):
                    last = nc.tensor.matmul(f.bank[:, j * SEQ:(j + 1) * SEQ], wuk[:, 2 * i + j, :], bq[:, 2 * i + j, :],
                                            start=True, stop=True)
                end(f, last)
            project_tok(("dv0", "dv1"), blk(DV))

            def logits(a, q, kT):
                for n, (t, hs) in enumerate(((0, range(4)), (1, (0, 1)), (1, (2, 3)))):
                    f = begin(f"{a}l{n}")
                    m = P * (t + 1)
                    for i, h in enumerate(hs):
                        o = f.bank[:, i * m:(i + 1) * m]
                        keys = kT(h)
                        last = nc.tensor.matmul(o, q[:, h, t * P:(t + 1) * P], keys[:, 0:m], start=True, stop=a == "b")
                        if a == "f":
                            nc.tensor.matmul(o, ff[0:NH, 3, t * P:(t + 1) * P], sel[0:NH, h, 0:m], start=False, stop=False)
                            last = nc.tensor.matmul(o, sel[0:NH, h, 0:P], ff[0:NH, 4, 0:m], start=False, stop=True)
                    end(f, last)

            def transpose_p(a):
                for n, (t, kt) in enumerate(((0, 0), (1, 0), (1, 1))):
                    pe.wait_ge(sem("soft_p"), t + 1 + (TT if a == "b" else 0))
                    f = begin(f"{a}pT{n}")
                    for h in range(NH):
                        last = nc.tensor.transpose(f.bank[:, h * P:(h + 1) * P], lg[a][t][:, h, kt * P:(kt + 1) * P], ident)
                    end(f, last)

            pe.wait_ge(sem("dq"), 2)
            pe.wait_ge(sem("dk"), 2)
            pe.wait_ge(sem("forget"), 2)
            logits("f", dq, lambda h: dk[:, h, :])
            project_tok(("av0", "av1"), blk(AV))
            project_T(("au0", "au1"), blk(AU), h1, SEQ)
            transpose_p("f")
            project_T(("az0", "az1"), blk(AZ), h1, SEQ)
            pe.wait_ge(sem("soft_pT"), 3)
            pe.wait_ge(sem("dv"), 2)
            for i in range(2):
                f = begin(f"fo{i}")
                for j in range(2):
                    h = 2 * i + j
                    o = f.bank[:, j * SEQ:(j + 1) * SEQ]
                    v = lambda t: dv[:, t, h * P:(h + 1) * P]
                    nc.tensor.matmul(o[:, 0:P], v(0), pT[:, 0, h, :], start=True, stop=True)
                    nc.tensor.matmul(o[:, P:SEQ], v(0), pT[:, 1, h, :], start=True, stop=False)
                    last = nc.tensor.matmul(o[:, P:SEQ], v(1), pT[:, 2, h, :], start=False, stop=True)
                end(f, last)
            pe.wait_ge(sem("av"), TT)
            pe.wait_ge(sem("ws_masked"), 1)
            for i in range(2):
                f = begin(f"mx{i}")
                for j in range(2):
                    gr = 2 * i + j
                    for t in range(TT):
                        o = f.bank[:, j * SEQ + t * P:j * SEQ + (t + 1) * P]
                        nc.tensor.matmul(o, av[:, t, gr * P:(gr + 1) * P], wsT[:, gr, :], start=True, stop=False)
                        last = nc.tensor.matmul(o, ones[0:1, :], bs[0:1, gr * P:(gr + 1) * P], start=False, stop=True)
                end(f, last)
            project_T(("dz0", "dz1"), blk(DZ), h1, SEQ)
            pe.wait_ge(sem("cT"), 1)
            pe.wait_ge(sem("qlat"), 2)
            logits("b", qlat, lambda h: cT)
            project_T(("bz0", "bz1"), blk(BZ), h1, SEQ)
            project_T(("cb0", "cb1"), blk(CB), h1, SEQ)
            project_T(("cc0", "cc1"), blk(CC), h1, SEQ)
            transpose_p("b")
            project_T(("cx0", "cx1"), blk(CX), h1, SEQ)
            pe.wait_ge(sem("soft_pT"), 6)
            flat = lambda j: pT[:, j, :, :].rearrange("p h q -> p (h q)")
            f = begin("ol0")
            end(f, nc.tensor.matmul(f.bank[:, :], cn[:, 0, :], flat(0), start=True, stop=True))
            f = begin("ol1")
            nc.tensor.matmul(f.bank[:, :], cn[:, 0, :], flat(1), start=True, stop=False)
            end(f, nc.tensor.matmul(f.bank[:, :], cn[:, 1, :], flat(2), start=False, stop=True))
            project_T(("cz0", "cz1"), blk(CZ), h1, SEQ)
            pe.wait_ge(sem("olat"), 2)
            for i in range(2):
                f = begin(f"bo{i}")
                for j in range(2):
                    last = nc.tensor.matmul(f.bank[:, j * SEQ:(j + 1) * SEQ], wuv[:, 2 * i + j, :], olat[:, 2 * i + j, :],
                                            start=True, stop=True)
                end(f, last)
            for n in ORDER:
                for half in range(2):
                    project_T([f"g{n}{2 * half + j}" for j in range(2)], blk(GATE[n] + half), h1, SEQ)
                pe.wait_ge(sem(f"y{n}"), 2)
                project_T([f"br{n}{j}" for j in range(4)], blk(WB[n]), y[n], SEQ, stride=D, kk=CW)
            pe.wait_ge(sem("merged"), 4 * 4)
            for half in range(2):
                project_T([f"wo{2 * half + j}" for j in range(2)], blk(WO + half), merged, SEQ)
            pe.wait_ge(sem("squares"), 5)
            column_sums("ssq2", sq, SEQ)

            pe.wait_ge(sem("squares"), 6)
            f = begin("ssq3")
            for k in range(KD):
                last = nc.tensor.matmul(f.bank[:, 0:LEN], ones, sq_all[:, k, :], start=k == 0, stop=k == KD - 1)
            end(f, last)
            pe.wait_ge(sem("normed"), 2 * KD)
            project_T([f"fin{g}" for g in range(4)], FIN, hn, LEN, per=1)
            pe.wait_ge(sem("second_in"), 16 * 5)
            f = begin("ab")
            for t, (a, n) in enumerate(((0, META), (META, P), (META + P, P))):
                for k in range(KD):
                    last = nc.tensor.matmul(f.bank[0:n, t * 32:(t + 1) * 32], hn[:, k, a:a + n], w_ab[:, k, :],
                                            start=k == 0, stop=k == KD - 1)
            end(f, last)
            for g in range(4):
                pe.wait_ge(sem("f_T"), g + 1)
                f = begin(f"fa{g}")
                for t in range(TT):
                    a = META + t * P
                    last = nc.tensor.matmul(f.bank[:, t * 2 * P:(t + 1) * 2 * P], f_T[:, g, a:a + P], dft_d, start=True, stop=True)
                end(f, last)
            for i in range(2):
                f = begin(f"fm{i}")
                for j in range(2):
                    last = nc.tensor.matmul(f.bank[0:META, j * 2 * P:(j + 1) * 2 * P], f_T[:, 2 * i + j, 0:META], dft_d,
                                            start=True, stop=True)
                end(f, last)
            project_T([f"k{h}" for h in range(4)], K0, hn, LEN, per=1)
            pe.wait_ge(sem("fa"), 6)
            for i in range(2):
                f = begin(f"yf{i}")
                for j in range(2):
                    g = 2 * i + j
                    o = f.bank[:, j * SEQ:(j + 1) * SEQ]
                    for part in range(2):
                        c = part * SEQ
                        d = slice(part * P, (part + 1) * P)
                        nc.tensor.matmul(o, fa0[0:META, g, d], dft_l[0:META, 0, c:c + SEQ], start=part == 0, stop=False)
                        for t in range(TT):
                            last = nc.tensor.matmul(o, fa[:, t, g, d], dft_l[:, 1 + t, c:c + SEQ], start=False,
                                                    stop=part == 1 and t == TT - 1)
                end(f, last)
            pe.wait_ge(sem("gl"), 2)
            f = begin("gsum")
            for t in range(3):
                n = META if t == 0 else P
                for d, m in ((0, LE), (1, GE)):
                    last = nc.tensor.matmul(f.bank[0:n, t * 32 + 8 * d:t * 32 + 8 * d + 8], omask(m)[0:n, 0:n],
                                            gl[0:n, t, 8 * d:8 * d + 8], start=True, stop=True)
                last = nc.tensor.matmul(f.bank[0:n, t * 32 + 16:t * 32 + 32], ones[0:n, 0:n], gl[0:n, t, :], start=True, stop=True)
            end(f, last)
            project_T([f"v{h}" for h in range(4)], V0, hn, LEN, per=1)
            pe.wait_ge(sem("yf_T"), 2)
            project_T([f"wf{j}" for j in range(4)], WF, yf_T, SEQ, stride=D, kk=4, pool=WK)

            def norms(kind, half, src_sem, n):
                pe.wait_ge(sem("sqn"), src_sem)
                for h in range(4):
                    f = begin(f"n{kind}{half}{h}")
                    last = nc.tensor.matmul(f.bank[:, 0:n], ones, sq2[:, h, 0:n], start=True, stop=True)
                    end(f, last)

            def to_tokens(kind, half, src, ready):
                pe.wait_ge(sem(f"{kind}_done"), ready)
                for t in (1, 2, 0):
                    n, a = (META, 0) if t == 0 else (P, META + (t - 1) * P)
                    f = begin(f"{kind}tr{half}{t}")
                    for h in range(4):
                        last = nc.tensor.transpose(f.bank[0:n, h * P:(h + 1) * P], src(h)[:, a:a + n], ident)
                    end(f, last)

            for j in range(2):
                project_T([f"gf{2 * j}", f"gf{2 * j + 1}"], GF + j, hn[:, :, META:], SEQ)
            norms("k", 0, 1, LEN)
            project_T([f"q{h}" for h in range(4)], Q0, hn, LEN, per=1)
            to_tokens("k", 0, lambda h: kT[:, h, :], 1)
            to_tokens("v", 0, lambda h: v_T[0][:, h, :], 1)
            project_T([f"k{h + 4}" for h in range(4)], K1, hn, LEN, per=1)
            norms("q", 0, 2, SEQ)
            project_T([f"v{h + 4}" for h in range(4)], V1, hn, LEN, per=1)
            norms("k", 1, 3, LEN)
            project_T([f"q{h + 4}" for h in range(4)], Q1, hn, LEN, per=1)
            to_tokens("k", 1, lambda h: kT[:, h + 4, :], 2)
            to_tokens("v", 1, lambda h: v_T[1][:, h, :], 2)
            norms("q", 1, 4, SEQ)

            def prepare(l):
                n, w = l.n, work(l)
                g = omask(upto(l))
                f = begin(f"row{l.key}")
                for i, h in enumerate(l.hs):
                    j = l.j + h
                    last = nc.tensor.matmul(f.bank[:, i * n:(i + 1) * n], gl[0:n, l.tile, j:j + 1].to_broadcast([n, P]),
                                            g[0:n, 0:n], start=True, stop=True)
                end(f, last)
                f = begin(f"kk{l.key}")
                for i, h in enumerate(l.hs):
                    k = kT[:, h, l.at:l.at + n]
                    last = nc.tensor.matmul(f.bank[0:n, i * n:(i + 1) * n], k, k, start=True, stop=True)
                end(f, last)
                if l.tile:
                    f = begin(f"kq{l.key}")
                    for i, h in enumerate(l.hs):
                        last = nc.tensor.matmul(f.bank[:, i * n:(i + 1) * n], kT[:, h, l.at:l.at + n],
                                                qT[:, h, l.at - META:l.at - META + n], start=True, stop=True)
                    end(f, last)

            def level(l, v):
                n, w = l.n, work(l)
                am = w.am[v % 2]
                pe.wait_ge(sem(f"am{l.i}"), am_count[l.i] + v + 1)
                if v:
                    pe.wait_ge(sem(f"tt{l.i}"), am_count[l.i] + v)
                f = begin(f"z{l.key}{v}")
                for i in range(len(l.hs)):
                    last = nc.tensor.matmul(f.bank[0:n, i * n:(i + 1) * n], am[0:n, i, 0:n],
                                            ident[0:n, 0:n] if v == 0 else w.tt[0:n, i, 0:n], start=True, stop=True)
                end(f, last)

            def level_end(l, v):
                n, w = l.n, work(l)
                pe.wait_ge(sem(f"z{l.i}"), z_count[l.i] + v)
                pe.wait_ge(sem(f"t{l.i}"), z_count[l.i] + v)
                f = begin(f"yt{l.key}{v}")
                for i in range(len(l.hs)):
                    last = nc.tensor.matmul(f.bank[0:n, i * n:(i + 1) * n], w.t[0:n, i, 0:n], w.z[0:n, i, 0:n], start=True, stop=True)
                end(f, last)
                if v < l.levels - 1:
                    f = begin(f"y{l.key}{v}")
                    for i in range(len(l.hs)):
                        last = nc.tensor.matmul(f.bank[0:n, i * n:(i + 1) * n], w.z[0:n, i, 0:n], w.t[0:n, i, 0:n], start=True, stop=True)
                    end(f, last)

            def step_keys(l):
                pe.wait_ge(sem(f"s_{l.d}"), l.s_before)
                f = begin(f"r{l.key}", PJ)
                for i, h in enumerate(l.hs):
                    last = nc.tensor.matmul(f.bank[:, i * P:(i + 1) * P], kT[:, h, l.at:l.at + P], state[l.d][:, h * P:(h + 1) * P],
                                            start=True, stop=True)
                end(f, last)

            def step_values(l):
                n, w = l.n, work(l)
                x = (lambda i: v_meta[0:n, i * P:(i + 1) * P]) if l.tile == 0 else (lambda i: w.x[:, i, :])
                pe.wait_ge(sem(f"tt{l.i}"), tt_end[l.key])
                if l.tile:
                    pe.wait_ge(sem(f"xk{l.i}"), l.r + 1)
                for part in range(len(l.hs) // 4):
                    f = begin(f"vn{l.key}{part}", PJ)
                    for i in range(4):
                        c = 4 * part + i
                        last = nc.tensor.matmul(f.bank[0:n, i * P:(i + 1) * P], w.tt[0:n, c, 0:n], x(c), start=True, stop=True)
                    end(f, last)

            def step_state(l):
                n, w = l.n, work(l)
                k = k_meta if l.tile == 0 else k_tok[:, l.tile - 1, :]
                for part in range(len(l.hs) // 4):
                    pe.wait_ge(sem(f"vd{l.i}"), l.r + 1 + part)
                    f = begin(f"ds{l.key}{part}", PJ)
                    for i in range(4):
                        h = l.hs[4 * part + i]
                        v = x_meta[0:n, h * P:(h + 1) * P] if l.tile == 0 else w.z2[:, i, :]
                        last = nc.tensor.matmul(f.bank[:, i * P:(i + 1) * P], k[0:n, h * P:(h + 1) * P], v, start=True, stop=True)
                    end(f, last)

            def step_out(l):
                w = work(l)
                pe.wait_ge(sem(f"vn{l.i}"), l.r + 1)
                pe.wait_ge(sem(f"q{l.i}"), 2 * l.r + 2)
                f = begin(f"o{l.key}", PJ)
                for i, h in enumerate(l.hs):
                    o = f.bank[:, i * P:(i + 1) * P]
                    nc.tensor.matmul(o, state[l.d][:, h * P:(h + 1) * P], w.qd[:, i, :], start=True, stop=False)
                    last = nc.tensor.matmul(o, w.x[:, i, :], w.qk[:, i, :], start=False, stop=True)
                end(f, last)

            am_count, z_count = [0, 0, 0], [0, 0, 0]
            pe.wait_ge(sem("k_done"), 2)
            pe.wait_ge(sem("q_done"), 2)
            pe.wait_ge(sem("to_tok"), 12)
            for r, lanes in enumerate(ROUNDS):
                now = ([meta] if r == 0 else []) + lanes
                before = ROUNDS[r - 1] if r else []
                for l in now:
                    prepare(l)
                for v in range(7):
                    for l in now:
                        if v < l.levels:
                            level(l, v)
                    if v == 1:
                        for l in before: step_keys(l)
                    if v == 2:
                        for l in before: step_values(l)
                    if v == 4:
                        for l in before: step_out(l)
                    if v == 5 and r < 3:
                        for l in before: step_state(l)
                    if v:
                        for l in now:
                            if v < l.levels:
                                level_end(l, v)
                    if r == 0 and v == 5:
                        step_values(meta)
                    if r == 0 and v == 6:
                        step_state(meta)
                for l in now:
                    am_count[l.i] += l.levels
                    z_count[l.i] += l.levels - 1
            for step in (step_keys, step_values, step_out):
                for l in ROUNDS[-1]:
                    step(l)
            pe.wait_ge(sem("o_sq"), 4)
            for i in range(4):
                f = begin(f"no{i}")
                for j in range(2):
                    last = nc.tensor.matmul(f.bank[:, j * SEQ:(j + 1) * SEQ], ones, o_sq[:, 2 * i + j, :], start=True, stop=True)
                end(f, last)
            for j in range(2):
                project_T([f"zz{2 * j}", f"zz{2 * j + 1}"], ZB + j, hn[:, :, META:], SEQ)
            for j in range(2):
                project_T([f"gd{2 * j}", f"gd{2 * j + 1}"], GD + 2 * j, hn[:, :, META:], SEQ)
                pe.wait_ge(sem("y_delta"), 4)
                project_T([f"wd{2 * j}", f"wd{2 * j + 1}"], WD + 2 * j, o_T, SEQ, pool=WK)
            pe.wait_ge(sem("merged2"), 4)
            for j in range(2):
                project_T([f"wp{2 * j}", f"wp{2 * j + 1}"], WO2 + j, y_four, SEQ)

            pe.wait_ge(sem("squares"), 10)
            column_sums("ssq4", o_sq, SEQ)
            pe.wait_ge(sem("normed"), 3 * KD)
            pe.wait_ge(sem("router_in"), 16)
            f = begin("router")
            for t in range(TT):
                for k in range(KD):
                    last = nc.tensor.matmul(f.bank[:, t * 72:(t + 1) * 72], m_T[:, k, t * P:(t + 1) * P], w_router[:, k, :],
                                            start=k == 0, stop=k == KD - 1)
            end(f, last)
            for t in range(TT):
                for i in range(2):
                    f = begin(f"m{t}{i}", PJ)
                    for j in range(4):
                        last = nc.tensor.transpose(f.bank[:, j * P:(j + 1) * P], m_T[:, 4 * i + j, t * P:(t + 1) * P], ident)
                    end(f, last)
            pe.wait_ge(sem("chosen"), TT)
            f = begin("ranks")
            nc.tensor.matmul(f.bank[:, 0:64], omask(LE), chosen[:, 0, :], start=True, stop=True)
            nc.tensor.matmul(f.bank[:, 64:128], omask(LE), chosen[:, 1, :], start=True, stop=False)
            nc.tensor.matmul(f.bank[:, 64:128], ones, chosen[:, 0, :], start=False, stop=True)
            nc.tensor.matmul(f.bank[:, 128:192], ones, chosen[:, 0, :], start=True, stop=False)
            end(f, nc.tensor.matmul(f.bank[:, 128:192], ones, chosen[:, 1, :], start=False, stop=True))

            for b in range(8):
                if uses[b]:
                    pe.wait_ge(free[b], uses[b])
            pe.wait_ge(sem("m_tok"), 4)
            pe.sem_inc(sem("down"), 2)
            n_passes = read_passes(nc.tensor, pe)
            with pe.Fori(0, n_passes) as p:
                with pe.Fori(0, N_GROUPS // 2) as pair:
                  for u in range(2):
                    q = 2 * pair + u
                    it = p * N_GROUPS + q
                    pe.wait_ge(sem("picks"), it + 1)
                    pe.wait_ge(sem("added"), it * 4 + 4)
                    for k in range(KD):
                        o = banks[k // 4][:, (k % 4) * P:(k % 4 + 1) * P]
                        for t in range(TT):
                            last = nc.tensor.matmul(o, m_tok[:, t, k * P:(k + 1) * P], pick_m[:, t, :], start=t == 0, stop=t == TT - 1)
                        if k % 4 == 3:
                            last.then_inc(sem("gathered"), 1)
                    for t in range(TT):
                        last = nc.tensor.transpose(banks[2][:, t * P:(t + 1) * P], pick_w[:, t, :], ident)
                    last.then_inc(sem("gathered"), 1)
                    pe.wait_ge(sem("xg"), 2 * it + 2)
                    for j in range(PER):
                        if u == 0:
                            pe.wait_ge(sem(f"slot{(N_BLOCKS + j) % SLOTS}_in"), gate_up_in[j] + 8 * it)
                    if u == 1:
                        pe.wait_ge(sem("odd_in"), 64 * (p * (N_GROUPS // 2) + pair) + 64)
                    for k in range(KD):
                        for j in range(PER):
                            last = nc.tensor.matmul(banks[3][j * CAP:(j + 1) * CAP, :], xg[:, k, j * CAP:(j + 1) * CAP],
                                                    gate_up[u][j][:, k * 2 * FE:(k + 1) * 2 * FE], start=k == 0, stop=k == KD - 1)
                    last.then_inc(sem("gate_up"), 1)
                    pe.wait_ge(sem("hid"), it + 2)
                    for i in range(2):
                        last = nc.tensor.transpose(banks[4][:, i * P:(i + 1) * P], hid[:, i * P:(i + 1) * P], ident)
                    last.then_inc(sem("hid_turned"), 1)
                    pe.wait_ge(sem("hid_T"), it + 1)
                    pe.wait_ge(sem("down_in"), 32 * it + 32)
                    for half in range(2):
                        for i in range(2):
                            for j in range(PER):
                                c = (j % 2) * (BLOCK // 2) + i * D + half * 512
                                last = nc.tensor.matmul(banks[5 + half][j * CAP:(j + 1) * CAP, :], hid_T[:, i, j * CAP:(j + 1) * CAP],
                                                        down[j // 2][:, c:c + 512], start=i == 0, stop=i == 1)
                        last.then_inc(sem("down"), 1)
                    pe.wait_ge(sem("yb"), 2 * it + 2)
                    pe.wait_ge(sem("pick_T"), it + 2)
                    for i, b in enumerate((0, 1, 2, 7)):
                        for j in range(2):
                            c = (2 * i + j) * P
                            last = nc.tensor.matmul(banks[b][:, j * SEQ:(j + 1) * SEQ], yb[:, c:c + P], pick_T, start=True, stop=True)
                        last.then_inc(sem("scattered"), 1)
            pe.wait_ge(sem("squares"), 14)
            for k in range(KD):
                last = nc.tensor.matmul(banks[3][:, 0:SEQ], ones, o_sq5[:, k, :], start=k == 0, stop=k == KD - 1)
            last.then_inc(sem("ssq5"), 1)

        @block.scalar
        def _(act):
            def got(name):
                f = fills[name]
                act.wait_ge(full[f.b], f.n + 1)
                return f

            chain = [0]

            def link(ins):
                chain[0] += 1
                ins.then_inc(sem("act_chain"), 1)
                act.wait_ge(sem("act_chain"), chain[0])

            def evacuate(name, out, done, func=ACT.Copy, scale=1.0):
                f = got(name)
                link(nc.scalar.activation(out, two(f.bank), func, scale=scale))
                act.sem_inc(free[f.b], 1)
                act.sem_inc(sem(done), 1)

            act.wait_ge(sem("res_in"), 16)
            sq = tmp.rearrange("p (k t) -> p k t", k=KD)
            nc.scalar.activation(sq, res[:, :, META:], ACT.Square).then_inc(sem("squares"), 1)
            act.wait_ge(sem("variance"), 1)
            nc.scalar.activation(rms, rms, ACT.Sqrt).then_inc(sem("deviation"), 1)
            f = got("c")
            for t in range(TT):
                last = nc.scalar.activation(tmp[:, t * P:(t + 1) * P], f.bank[:, t * SEQ:t * SEQ + P], ACT.Square,
                                            accum_out=css[:, t:t + 1])
            last.then_inc(sem("css"), 1)
            f = got("f")
            act.wait_ge(sem("cols_in"), 16)
            link(nc.scalar.activation(ff[0:NH, 0, :], f.bank[0:NH, 0:SEQ], ACT.Identity, bias=col("b_f")[0:NH]))
            act.sem_inc(free[f.b], 1)
            act.wait_ge(sem("variance"), 2)
            nc.scalar.activation(css, css, ACT.Sqrt).then_inc(sem("deviation"), 1)
            evacuate("qi", qi, "qiki")
            link(nc.scalar.activation(ff[0:NH, 1, :], ff[0:NH, 0, :], ACT.Abs))
            link(nc.scalar.activation(ff[0:NH, 1, :], ff[0:NH, 1, :], ACT.Exp, scale=-1.0))
            nc.scalar.activation(ff[0:NH, 1, :], ff[0:NH, 1, :], ACT.Ln, bias=1.0).then_inc(sem("ln_f"), 1)
            evacuate("dq0", dq[:, 0:2, :], "dq", scale=P ** -0.5)
            evacuate("dq1", dq[:, 2:4, :], "dq", scale=P ** -0.5)
            for n, (t, odd) in enumerate(((0, 0), (0, 1), (1, 0), (1, 1))):
                f = got(f"dots{n}")
                dst = (relu0, relu1)[t][:, odd::2, :]
                m = P * (t + 1)
                link(nc.scalar.activation(dst, f.bank[:, 0:2 * m].rearrange("p (h k) -> p h k", h=2), ACT.Relu))
                act.sem_inc(free[f.b], 1)
                act.sem_inc(sem("relu"), 1)
            evacuate("dk0", dk[:, 0:2, :], "dk")
            evacuate("dk1", dk[:, 2:4, :], "dk")
            evacuate("qlat0", qlat[:, 0:2, :], "qlat", scale=P ** -0.5)
            evacuate("qlat1", qlat[:, 2:4, :], "qlat", scale=P ** -0.5)
            for t in range(TT):
                f = got(f"dv{t}")
                link(nc.scalar.activation(dv[:, t, :], f.bank[:, :], ACT.Copy))
                act.sem_inc(free[f.b], 1)
                act.sem_inc(sem("dv"), 1)

            def exps(a):
                for t in range(TT):
                    act.wait_ge(sem("soft_max"), t + 1 + (TT if a == "b" else 0))
                    for h in range(NH):
                        last = nc.scalar.activation(lg[a][t][:, h, :], lg[a][t][:, h, :], ACT.Exp,
                                                    bias=nmax[a][:, t * NH + h:t * NH + h + 1],
                                                    accum_out=psum[a][:, t * NH + h:t * NH + h + 1])
                    last.then_inc(sem("soft_exp"), 1)

            exps("f")
            act.wait_ge(sem("variance"), 3)
            nc.scalar.activation(lnsd, lnsd, ACT.Sqrt).then_inc(sem("deviation"), 1)
            evacuate("az0", y[0][:, 0:2, :], "az", func=ACT.Silu)
            evacuate("az1", y[0][:, 2:4, :], "az", func=ACT.Silu)
            evacuate("dz0", y[3][:, 0:2, :], "dz", func=ACT.Silu)
            evacuate("dz1", y[3][:, 2:4, :], "dz", func=ACT.Silu)
            exps("b")
            evacuate("bz0", y[1][:, 0:2, :], "bz", func=ACT.Silu)
            evacuate("bz1", y[1][:, 2:4, :], "bz", func=ACT.Silu)
            act.wait_ge(sem("cc"), 1)
            evacuate("cb0", cc[:, 0:2, :], "cb")
            evacuate("cb1", cc[:, 2:4, :], "cb")
            evacuate("cz0", y[2][:, 0:2, :], "cz", func=ACT.Silu)
            evacuate("cz1", y[2][:, 2:4, :], "cz", func=ACT.Silu)
            gates = tmp.rearrange("p (k t) -> p k t", k=KD)
            for i, n in enumerate(ORDER):
                for j in range(4):
                    if i > 0:
                        act.wait_ge(sem("merged"), 4 * (i - 1) + j + 1)
                    evacuate(f"g{n}{j}", gates[:, 2 * j:2 * j + 2, :], "gate", func=ACT.Sigmoid)
            for j in range(4):
                act.wait_ge(sem("x1"), j + 1)
                nc.scalar.activation(sq[:, 2 * j:2 * j + 2, :], res[:, 2 * j:2 * j + 2, META:], ACT.Square).then_inc(sem("squares"), 1)
            act.wait_ge(sem("variance"), 4)
            nc.scalar.activation(rms, rms, ACT.Sqrt).then_inc(sem("deviation"), 1)

            act.wait_ge(sem("final"), KD)
            nc.scalar.activation(sq_all, res, ACT.Square).then_inc(sem("squares"), 1)
            act.wait_ge(sem("variance"), 5)
            nc.scalar.activation(rms2, rms2, ACT.Sqrt).then_inc(sem("deviation"), 1)
            for g in range(4):
                f = got(f"fin{g}")
                link(nc.scalar.activation(f_T[:, g, :], f.bank[:, 0:LEN], ACT.Copy))
                act.sem_inc(free[f.b], 1)
                act.sem_inc(sem("f_T"), 1)
            regions = ((slice(0, META), slice(0, 1)), (slice(0, P), slice(1, 3)))
            act.wait_ge(sem("ab"), 1)
            for p, t in regions:
                link(nc.scalar.activation(gx[p, t], gl[p, t], ACT.Abs))
                link(nc.scalar.activation(gx[p, t], gx[p, t], ACT.Exp, scale=-1.0))
                link(nc.scalar.activation(gx[p, t], gx[p, t], ACT.Ln, bias=1.0))
            link(nc.scalar.activation(nea, rows[:, ROWS["a_log"][0]:ROWS["a_log"][1]], ACT.Exp))
            act.sem_inc(sem("soft"), 1)
            for g in range(4):
                f = got(f"fa{g}")
                link(nc.scalar.activation(fa[:, :, g, :], two(f.bank), ACT.Copy))
                act.sem_inc(free[f.b], 1)
                act.sem_inc(sem("fa"), 1)
            for i in range(2):
                f = got(f"fm{i}")
                link(nc.scalar.activation(fa0[0:META, 2 * i:2 * i + 2, :], two(f.bank)[0:META], ACT.Copy))
                act.sem_inc(free[f.b], 1)
                act.sem_inc(sem("fa"), 1)
            for p, t in regions:
                nc.scalar.activation(beta[p, t], beta[p, t], ACT.Sigmoid)

            def silu_sq(kind, half, dst, n, squares=True):
                for h in range(4):
                    act.wait_ge(sem(f"conv_{kind}"), 4 * half + h + 1)
                    link(nc.scalar.activation(dst[:, h, 0:n], dst[:, h, 0:n], ACT.Silu))
                if squares:
                    link(nc.scalar.activation(sq2[:, :, 0:n], dst[:, :, 0:n], ACT.Square))
                    act.sem_inc(sem("sqn"), 1)

            def norm_sqrt(n):
                norm_sqrt.count += 1
                act.wait_ge(sem("ssn"), norm_sqrt.count)
                link(nc.scalar.activation(rn2[:, :, 0:n], rn2[:, :, 0:n], ACT.Sqrt))
                act.sem_inc(sem("sdn"), 1)
            norm_sqrt.count = 0

            def tokens(kind, half):
                dst, small = (k_tok, k_meta) if kind == "k" else (v_tok, v_meta)
                for t in (1, 2, 0):
                    f = got(f"{kind}tr{half}{t}")
                    o = small[0:META, half * 512:half * 512 + 512] if t == 0 else dst[:, t - 1, half * 512:half * 512 + 512]
                    link(nc.scalar.activation(o, f.bank[0:META if t == 0 else P, :], ACT.Copy))
                    act.sem_inc(free[f.b], 1)
                    act.sem_inc(sem("to_tok"), 1)

            for i in range(2):
                f = got(f"yf{i}")
                link(nc.scalar.activation(yf_T[:, 2 * i:2 * i + 2, :], two(f.bank), ACT.Copy))
                act.sem_inc(free[f.b], 1)
                act.sem_inc(sem("yf_T"), 1)
            act.wait_ge(sem("gsum"), 1)
            for p, t in regions:
                link(nc.scalar.activation(edec[p, t], gsum[p, t, 0:16], ACT.Exp))
                link(nc.scalar.activation(krem[p, t], krem[p, t], ACT.Exp))
                link(nc.scalar.activation(eall[p, t], gsum[p, t, 16:32], ACT.Exp))
            act.sem_inc(sem("edec"), 1)
            for j in range(4):
                f = got(f"gf{j}")
                if j >= 2:
                    act.wait_ge(sem("y_four"), j - 1)
                link(nc.scalar.activation(gate2[:, j % 2], two(f.bank), ACT.Sigmoid))
                act.sem_inc(free[f.b], 1)
                act.sem_inc(sem("gate_f"), 1)
            act.wait_ge(sem("y_four"), 4)
            silu_sq("k", 0, kT[:, 0:4], LEN)
            norm_sqrt(LEN)
            silu_sq("v", 0, v_T[0], LEN, squares=False)
            act.sem_inc(sem("v_done"), 1)
            silu_sq("q", 0, qT[:, 0:4], SEQ)
            tokens("k", 0)
            tokens("v", 0)
            norm_sqrt(SEQ)
            silu_sq("k", 1, kT[:, 4:8], LEN)
            norm_sqrt(LEN)
            silu_sq("v", 1, v_T[1], LEN, squares=False)
            act.sem_inc(sem("v_done"), 1)
            silu_sq("q", 1, qT[:, 4:8], SEQ)
            tokens("k", 1)
            tokens("v", 1)
            norm_sqrt(SEQ)

            def lane_exps(l):
                n, w = l.n, work(l)
                if l.tile:
                    f = got(f"row{l.key}")
                    act.wait_ge(sem(f"u{l.i}"), l.r + 1)
                    link(nc.scalar.activation(w.qd, heads_of(f, l), ACT.Exp))
                    act.sem_inc(free[f.b], 1)
                    act.sem_inc(sem(f"eg{l.i}"), 1)
                    link(nc.scalar.activation(w.qk, w.qk, ACT.Exp))
                else:
                    act.wait_ge(sem(f"u{l.i}"), l.r + 1)
                link(nc.scalar.activation(w.u[0:n, :, 0:n], w.u[0:n, :, 0:n], ACT.Exp, scale=-1.0))
                act.sem_inc(sem(f"d{l.i}"), 1)

            def copy_z(l, v):
                n, w = l.n, work(l)
                f = got(f"z{l.key}{v}")
                link(nc.scalar.activation(w.z[0:n, :, 0:n], heads_of(f, l), ACT.Copy))
                act.sem_inc(free[f.b], 1)
                act.sem_inc(sem(f"z{l.i}"), 1)

            def new_values(l):
                w = work(l)
                f = got(f"vn{l.key}0")
                link(nc.scalar.activation(w.x, heads_of(f, l), ACT.Copy))
                act.sem_inc(sem(f"vn{l.i}"), 1)

            for r, lanes in enumerate(ROUNDS):
                now = ([meta] if r == 0 else []) + lanes
                before = ROUNDS[r - 1] if r else []
                for l in now:
                    lane_exps(l)
                for v in range(7):
                    if v == 3:
                        for l in before: new_values(l)
                    if v:
                        for l in now:
                            if v < l.levels:
                                copy_z(l, v)
            for l in ROUNDS[-1]:
                new_values(l)
            for i in range(4):
                act.wait_ge(sem("o_b"), 2 if i < 2 else 4)
                link(nc.scalar.activation(o_sq[:, 2 * i:2 * i + 2, :], o_T[:, 2 * i:2 * i + 2, :], ACT.Square))
                act.sem_inc(sem("o_sq"), 1)
            for i in range(2):
                act.wait_ge(sem("ss_o"), 2 * i + 2)
                link(nc.scalar.activation(o_rn[:, 4 * i:4 * i + 4, :], o_rn[:, 4 * i:4 * i + 4, :], ACT.Sqrt))
                act.sem_inc(sem("sd_o"), 1)
            for j in range(4):
                f = got(f"zz{j}")
                link(nc.scalar.activation(z_g[:, j], two(f.bank), ACT.Silu))
                act.sem_inc(free[f.b], 1)
                act.sem_inc(sem("z_g"), 1)
            for j in range(4):
                f = got(f"gd{j}")
                act.wait_ge(sem("y_delta"), 4)
                link(nc.scalar.activation(z_g[:, j], two(f.bank), ACT.Sigmoid))
                act.sem_inc(free[f.b], 1)
                act.sem_inc(sem("z_g"), 1)

            for j in range(4):
                act.wait_ge(sem("h2"), j + 1)
                nc.scalar.activation(o_sq[:, 2 * j:2 * j + 2, :], res[:, 2 * j:2 * j + 2, META:], ACT.Square).then_inc(sem("squares"), 1)
            act.wait_ge(sem("variance"), 6)
            nc.scalar.activation(rms4, rms4, ACT.Sqrt).then_inc(sem("deviation"), 1)
            for t in range(TT):
                for i in range(2):
                    f = got(f"m{t}{i}")
                    link(nc.scalar.activation(m_tok[:, t, i * 512:(i + 1) * 512], f.bank[:, :], ACT.Copy))
                    act.sem_inc(free[f.b], 1)
                    act.sem_inc(sem("m_tok"), 1)
            for t in range(TT):
                act.wait_ge(sem("r_max"), t + 1)
                link(nc.scalar.activation(r_exp[:, t, 0:8], router[:, t, 0:8], ACT.Exp, bias=r_nmax[:, 2 * t:2 * t + 1],
                                          accum_out=r_sum[:, 2 * t:2 * t + 1]))
                nc.scalar.activation(r_exp[:, t, 8:72], router[:, t, 8:72], ACT.Exp, bias=r_nmax[:, 2 * t + 1:2 * t + 2],
                                     accum_out=r_sum[:, 2 * t + 1:2 * t + 2])
                link(nc.scalar.activation(r_second[:, t:t + 1], r_second[:, t:t + 1], ACT.Exp, bias=r_nmax[:, 2 * t + 1:2 * t + 2]))
                act.sem_inc(sem("r_exp"), 1)

            n_passes = read_passes(nc.scalar, act)
            with act.Fori(0, n_passes) as p:
                with act.Fori(0, N_GROUPS // 2) as pair:
                  for u in range(2):
                    q = 2 * pair + u
                    it = p * N_GROUPS + q
                    act.wait_ge(sem("gathered"), 3 * it + 1)
                    nc.scalar.activation(xg[:, 0:4, :].rearrange("p k s -> p (k s)"), banks[0][:, :], ACT.Copy).then_inc(sem("xg"), 1)
                    act.wait_ge(sem("gate_up"), it + 1)
                    act.wait_ge(sem("hid"), it + 1)
                    nc.scalar.activation(act_g, banks[3][:, 0:FE], ACT.Silu).then_inc(sem("silu"), 1)
                    act.wait_ge(sem("hid_turned"), it + 1)
                    nc.scalar.activation(hid_T.rearrange("p f s -> p (f s)"), banks[4][:, 0:2 * P], ACT.Copy).then_inc(sem("hid_T"), 1)
                    act.wait_ge(sem("down"), 2 * it + 3)
                    nc.scalar.activation(yb[:, 0:512], banks[5][:, :], ACT.Copy).then_inc(sem("yb"), 1)
            for j in range(4):
                act.wait_ge(sem("moe_done"), 1)
                nc.scalar.activation(o_sq5[:, 2 * j:2 * j + 2, :], res[:, 2 * j:2 * j + 2, META:], ACT.Square).then_inc(sem("squares"), 1)
            act.wait_ge(sem("variance"), 7)
            nc.scalar.activation(rms4, rms4, ACT.Sqrt).then_inc(sem("deviation"), 1)

        @block.vector
        def _(dve):
            def got(name):
                f = fills[name]
                dve.wait_ge(full[f.b], f.n + 1)
                return f

            chain = [0]

            def link(ins):
                chain[0] += 1
                ins.then_inc(sem("dve_chain"), 1)
                dve.wait_ge(sem("dve_chain"), chain[0])

            def evacuate(name, out, done=None):
                f = got(name)
                link(nc.vector.tensor_copy(out, two(f.bank)))
                dve.sem_inc(free[f.b], 1)
                if done:
                    dve.sem_inc(sem(done), 1)

            def rms_rows(name, i, n):
                f = got(name)
                nc.vector.tensor_scalar(rms[:, 0:n], f.bank[:, 0:n], 1.0 / D, EPS, ALU.mult, ALU.add).then_inc(sem("variance"), 1)
                dve.wait_ge(sem("deviation"), i)
                link(nc.vector.reciprocal(rms[:, 0:n], rms[:, 0:n]))
                dve.sem_inc(free[f.b], 1)

            dve.wait_ge(sem("cols_in"), 16)
            rms_rows("ssq1", 1, SEQ)
            dve.wait_ge(sem("res_in"), 16)
            for k in range(KD):
                nc.vector.scalar_tensor_tensor(h1[:, k, :], res[:, k, META:], col("norm_g", k), rms, ALU.mult,
                                               ALU.mult).then_inc(sem("normed"), 1)
            f = got("c")
            dve.wait_ge(sem("css"), 1)
            link(nc.vector.tensor_scalar(css, css, 1.0 / P, EPS, ALU.mult, ALU.add))
            dve.sem_inc(sem("variance"), 1)
            for t in range(TT):
                nc.vector.tensor_scalar(wi[:, t * NH:(t + 1) * NH], f.bank[:, t * SEQ + P:t * SEQ + P + NH],
                                        NH ** -0.5 * IDX ** -0.5, None, ALU.mult)
            dve.wait_ge(sem("deviation"), 2)
            link(nc.vector.reciprocal(css, css))
            for t in range(TT):
                link(nc.vector.tensor_scalar(cn[:, t, :], f.bank[:, t * SEQ:t * SEQ + P], css[:, t:t + 1], None, ALU.mult))
                dve.sem_inc(sem("cn"), 1)
            dve.sem_inc(free[f.b], 1)
            f = got("ki")
            link(nc.vector.tensor_copy(ki, f.bank[:, 0:SEQ]))
            dve.sem_inc(free[f.b], 1)
            dve.sem_inc(sem("qiki"), 1)
            evacuate("bq0", bq[:, 0:2, :], "bq")
            evacuate("bq1", bq[:, 2:4, :], "bq")
            dve.wait_ge(sem("ln_f"), 1)
            link(nc.vector.scalar_tensor_tensor(ff[0:NH, 2, :], ff[0:NH, 0, :], 0.0, ff[0:NH, 1, :], ALU.min, ALU.subtract))
            link(nc.vector.memset(ff[0:NH, 1, :], 1.0))
            nc.vector.tensor_tensor_scan(ff[0:NH, 3, :], ff[0:NH, 1, :], ff[0:NH, 2, :], 0.0, ALU.mult, ALU.add).then_inc(sem("forget"), 1)
            dve.wait_ge(sem("forget"), 1)
            nc.vector.tensor_scalar(ff[0:NH, 4, :], ff[0:NH, 3, :], -1.0, None, ALU.mult).then_inc(sem("forget"), 1)
            f = got("cT")
            link(nc.vector.tensor_scalar(cT, f.bank[:, 0:SEQ], col("kv_g"), None, ALU.mult))
            dve.sem_inc(free[f.b], 1)
            dve.sem_inc(sem("cT"), 1)
            dve.wait_ge(sem("consts_in"), 16)

            def top_scores(t):
                m = P * (t + 1)
                s, r = score[t], (relu0, relu1)[t]
                causal = mask[:, SEQ - m:SEQ]
                dve.wait_ge(sem("relu"), 2 + 2 * t)
                for h in range(NH):
                    link(nc.vector.scalar_tensor_tensor(s, r[:, h, :], wi[:, t * NH + h:t * NH + h + 1],
                                                        causal if h == 0 else s, ALU.mult, ALU.add))
                for _ in range(TOPK // 8):
                    link(nc.vector.max(best, s))
                    link(nc.vector.match_replace(s, best, s, -3.4e38))
                link(nc.vector.tensor_scalar(s, s, -3.2e38, -1e30, ALU.is_gt, ALU.mult))
                link(nc.vector.tensor_tensor(s, s, causal, ALU.add))

            def softmax_in(a, add):
                for t in range(TT):
                    m = P * (t + 1)
                    for n, hs in ((0, (0, 4)),) if t == 0 else ((1, (0, 2)), (2, (2, 4))):
                        f = got(f"{a}l{n}")
                        k = hs[1] - hs[0]
                        link(nc.vector.tensor_tensor(lg[a][t][:, hs[0]:hs[1], :], f.bank[:, :].rearrange("p (h k) -> p h k", h=k),
                                                     add(t).unsqueeze(1).to_broadcast([P, k, m]), ALU.add))
                        dve.sem_inc(free[f.b], 1)
                    nc.vector.tensor_reduce(nmax[a][:, t * NH:(t + 1) * NH], lg[a][t], AX.X, ALU.max,
                                            negate=True).then_inc(sem("soft_max"), 1)

            def softmax_out(a):
                for t in range(TT):
                    m = P * (t + 1)
                    dve.wait_ge(sem("soft_exp"), t + 1 + (TT if a == "b" else 0))
                    ps = psum[a][:, t * NH:(t + 1) * NH]
                    link(nc.vector.reciprocal(ps, ps))
                    nc.vector.tensor_tensor(lg[a][t], lg[a][t], ps.unsqueeze(2).to_broadcast([P, NH, m]),
                                            ALU.mult).then_inc(sem("soft_p"), 1)

            def weights_T(a):
                for n in range(3):
                    f = got(f"{a}pT{n}")
                    link(nc.vector.tensor_copy(pT[:, n, :, :].rearrange("p h q -> p (h q)"), f.bank[:, :]))
                    dve.sem_inc(free[f.b], 1)
                    dve.sem_inc(sem("soft_pT"), 1)

            top_scores(0)
            softmax_in("f", lambda t: mask[:, SEQ - P * (t + 1):SEQ])
            dve.wait_ge(sem("small_in"), 16 * 6)
            for t in range(TT):
                f = got(f"av{t}")
                link(nc.vector.bn_stats(bns, f.bank[:, :]))
                link(nc.vector.bn_aggr(mv[:, 2 * t:2 * t + 2], bns))
                link(nc.vector.tensor_scalar(av[:, t, :], f.bank[:, :], mv[:, 2 * t:2 * t + 1], None, ALU.subtract))
                dve.sem_inc(free[f.b], 1)
                link(nc.vector.tensor_scalar(lnsd[:, t:t + 1], mv[:, 2 * t + 1:2 * t + 2], EPS, None, ALU.add))
            softmax_out("f")
            dve.sem_inc(sem("variance"), 1)
            dve.wait_ge(sem("deviation"), 3)
            link(nc.vector.reciprocal(lnsd, lnsd))
            for t in range(TT):
                link(nc.vector.scalar_tensor_tensor(av[:, t, :], av[:, t, :], lnsd[:, t:t + 1], ln_rows[:, 0:W1], ALU.mult, ALU.mult))
                nc.vector.tensor_tensor(av[:, t, :], av[:, t, :], ln_rows[:, W1:], ALU.add).then_inc(sem("av"), 1)
            evacuate("au0", cpad[:, 0:2, 0:SEQ])
            evacuate("au1", cpad[:, 2:4, 0:SEQ])
            weights_T("f")

            def times(name, i, into, silu, done, other=None):
                f = got(name)
                dve.wait_ge(sem(silu), i + 1)
                if other is not None:
                    link(nc.vector.tensor_tensor(into, into, other, ALU.mult))
                link(nc.vector.tensor_tensor(into, into, two(f.bank), ALU.mult))
                dve.sem_inc(free[f.b], 1)
                dve.sem_inc(sem(done), 1)

            top_scores(1)
            softmax_fo = [(f"fo{i}", i) for i in range(2)]
            for i in range(2):
                times(f"mx{i}", i, y[0][:, 2 * i:2 * i + 2, :], "az", "y0", cpad[:, 2 * i:2 * i + 2, 0:SEQ])
            for name, i in softmax_fo:
                times(name, i, y[3][:, 2 * i:2 * i + 2, :], "dz", "y3")
            softmax_in("b", lambda t: score[t])
            softmax_out("b")
            link(nc.vector.memset(cpad[:, :, 0:2], 0.0))
            dve.sem_inc(sem("cc"), 1)
            evacuate("cc0", cv[:, 0:2, :])
            evacuate("cc1", cv[:, 2:4, :])
            weights_T("b")
            for i in range(2):
                f = got(f"cx{i}")
                link(nc.vector.tensor_tensor(cpad[:, 2 * i:2 * i + 2, 2:], two(f.bank), cv[:, 2 * i:2 * i + 2, :], ALU.mult))
                dve.sem_inc(free[f.b], 1)
            for j in range(CW):
                link(nc.vector.tensor_scalar(cv[:, j, :], cpad[:, j, 0:SEQ], col("conv_w", j), None, ALU.mult))
            for tap in (1, 2):
                for j in range(CW):
                    last = nc.vector.scalar_tensor_tensor(cv[:, j, :], cpad[:, j, tap:tap + SEQ], col("conv_w", tap * CW + j),
                                                          cv[:, j, :], ALU.mult, ALU.add)
                link(last)
            for t in range(TT):
                f = got(f"ol{t}")
                link(nc.vector.tensor_scalar(olat[:, :, t * P:(t + 1) * P], f.bank[:, :].rearrange("p (h q) -> p h q", h=NH),
                                             col("kv_g"), None, ALU.mult))
                dve.sem_inc(free[f.b], 1)
                dve.sem_inc(sem("olat"), 1)
            dve.wait_ge(sem("cb"), 2)
            link(nc.vector.tensor_tensor(cv, cv, cc, ALU.mult))
            dve.wait_ge(sem("cz"), 2)
            link(nc.vector.tensor_tensor(y[2], y[2], cv, ALU.mult))
            dve.sem_inc(sem("y2"), 2)
            for i in range(2):
                times(f"bo{i}", i, y[1][:, 2 * i:2 * i + 2, :], "bz", "y1")
            gates = tmp.rearrange("p (k t) -> p k t", k=KD)
            for i, n in enumerate(ORDER):
                for j in range(4):
                    f = got(f"br{n}{j}")
                    dve.wait_ge(sem("gate"), 4 * i + j + 1)
                    m = merged[:, 2 * j:2 * j + 2, :]
                    g = gates[:, 2 * j:2 * j + 2, :]
                    if i == 0:
                        link(nc.vector.tensor_tensor(m, two(f.bank), g, ALU.mult))
                    else:
                        link(nc.vector.tensor_tensor(g, two(f.bank), g, ALU.mult))
                        link(nc.vector.tensor_tensor(m, m, g, ALU.add))
                    dve.sem_inc(free[f.b], 1)
                    dve.sem_inc(sem("merged"), 1)
            for j in range(4):
                f = got(f"wo{j}")
                r = res[:, 2 * j:2 * j + 2, META:]
                link(nc.vector.tensor_tensor(r, r, two(f.bank), ALU.add))
                dve.sem_inc(free[f.b], 1)
                dve.sem_inc(sem("x1"), 1)
            rms_rows("ssq2", 4, SEQ)
            for k in range(KD):
                nc.vector.scalar_tensor_tensor(res[:, k, META:], res[:, k, META:], col("final_g", k), rms, ALU.mult,
                                               ALU.mult).then_inc(sem("final"), 1)

            f = got("ssq3")
            nc.vector.tensor_scalar(rms2, f.bank[:, 0:LEN], 1.0 / D, EPS, ALU.mult, ALU.add).then_inc(sem("variance"), 1)
            dve.wait_ge(sem("deviation"), 5)
            link(nc.vector.reciprocal(rms2, rms2))
            dve.sem_inc(free[f.b], 1)
            for k in range(KD):
                nc.vector.scalar_tensor_tensor(hn[:, k, :], res[:, k, :], col("norm1_g", k), rms2, ALU.mult,
                                               ALU.mult).then_inc(sem("normed"), 1)
            regions = ((slice(0, META), slice(0, 1)), (slice(0, P), slice(1, 3)))
            f = got("ab")
            ab = f.bank[:, 0:96].rearrange("p (t j) -> p t j", t=3)
            row = lambda n: rows[:, ROWS[n][0]:ROWS[n][1]]
            for p, t in regions:
                shape = [p.stop, t.stop - t.start, 16]
                nc.vector.tensor_tensor(gl[p, t], ab[p, t, 0:16], row("dt")[p].unsqueeze(1).to_broadcast(shape), ALU.add)
                last = nc.vector.tensor_copy(beta[p, t], ab[p, t, 16:32])
            link(last)
            dve.sem_inc(free[f.b], 1)
            dve.sem_inc(sem("ab"), 1)
            dve.wait_ge(sem("soft"), 1)
            link(nc.vector.tensor_scalar(nea, nea, -1.0, None, ALU.mult))
            for p, t in regions:
                shape = [p.stop, t.stop - t.start, 16]
                link(nc.vector.scalar_tensor_tensor(gl[p, t], gl[p, t], 0.0, gx[p, t], ALU.max, ALU.add))
                nc.vector.tensor_tensor(gl[p, t], gl[p, t], nea[p].unsqueeze(1).to_broadcast(shape), ALU.mult).then_inc(sem("gl"), 1)

            def conv(name, dst, kind, chunk, first):
                f = got(name)
                x = f.bank[:, 0:LEN]
                n = LEN - first
                tap = lambda j: col("conv5", j * 24 + chunk)
                link(nc.vector.tensor_scalar(dst, x[:, first:LEN], tap(2), None, ALU.mult))
                for j in (0, 1, 3, 4):
                    s = j - 2
                    lo, hi = max(0, -s - first), n - max(0, s)
                    link(nc.vector.scalar_tensor_tensor(dst[:, lo:hi], x[:, first + lo + s:first + hi + s], tap(j), dst[:, lo:hi],
                                                        ALU.mult, ALU.add))
                dve.sem_inc(free[f.b], 1)
                dve.sem_inc(sem(f"conv_{kind}"), 1)

            def normalize(kind, half, dst, n, scale):
                for h in range(4):
                    f = got(f"n{kind}{half}{h}")
                    link(nc.vector.tensor_scalar(rn2[:, h, 0:n], f.bank[:, 0:n], EPS, None, ALU.add))
                    dve.sem_inc(free[f.b], 1)
                dve.sem_inc(sem("ssn"), 1)
                normalize.count += 1
                dve.wait_ge(sem("sdn"), normalize.count)
                link(nc.vector.reciprocal(rn2[:, :, 0:n], rn2[:, :, 0:n]))
                link(nc.vector.scalar_tensor_tensor(dst[:, :, 0:n], dst[:, :, 0:n], scale, rn2[:, :, 0:n], ALU.mult, ALU.mult))
                dve.sem_inc(sem(f"{kind}_done"), 1)
            normalize.count = 0

            for h in range(4):
                conv(f"k{h}", kT[:, h, :], "k", 8 + h, 0)
            f = got("gsum")
            for p, t in regions:
                link(nc.vector.tensor_copy(gsum[p, t], f.bank[p, 0:96].rearrange("p (t j) -> p t j", t=3)[:, t]))
                link(nc.vector.tensor_tensor(krem[p, t], gsum[p, t, 16:32], gsum[p, t, 0:16], ALU.subtract))
            dve.sem_inc(free[f.b], 1)
            dve.sem_inc(sem("gsum"), 1)
            dve.wait_ge(sem("edec"), 1)
            for p, t in regions:
                link(nc.vector.tensor_scalar(edec[p, t], edec[p, t], -1.0, None, ALU.mult))
            for h in range(4):
                conv(f"v{h}", v_T[0][:, h, :], "v", 16 + h, 0)
            for j in range(4):
                f = got(f"wf{j}")
                link(nc.vector.tensor_copy(y_four[:, 2 * j:2 * j + 2, :], two(f.bank)))
                dve.sem_inc(free[f.b], 1)
            for j in range(4):
                dve.wait_ge(sem("gate_f"), j + 1)
                y4 = y_four[:, 2 * j:2 * j + 2, :]
                link(nc.vector.tensor_tensor(y4, y4, gate2[:, j % 2], ALU.mult))
                dve.sem_inc(sem("y_four"), 1)
            normalize("k", 0, kT[:, 0:4], LEN, 1.0)
            for h in range(4):
                conv(f"q{h}", qT[:, h, :], "q", h, META)
            for h in range(4):
                conv(f"k{h + 4}", kT[:, h + 4, :], "k", 12 + h, 0)
            normalize("q", 0, qT[:, 0:4], SEQ, P ** -0.5)
            for h in range(4):
                conv(f"v{h + 4}", v_T[1][:, h, :], "v", 20 + h, 0)
            normalize("k", 1, kT[:, 4:8], LEN, 1.0)
            for h in range(4):
                conv(f"q{h + 4}", qT[:, h + 4, :], "q", 4 + h, META)
            normalize("q", 1, qT[:, 4:8], SEQ, P ** -0.5)
            dve.wait_ge(sem("to_tok"), 12)
            link(nc.vector.memset(state["b"], 0.0))
            dve.sem_inc(sem("s_b"), 2)

            def over_heads(x, l, n=None):
                n = n or l.n
                return x[0:l.n, l.tile, l.j + l.hs[0]:l.j + l.hs[0] + len(l.hs)].unsqueeze(2).to_broadcast([l.n, len(l.hs), n])

            def mask_heads(m, l):
                return m[0:l.n, 0:l.n].unsqueeze(1).to_broadcast([l.n, len(l.hs), l.n])

            def lane_matrices(l):
                n, w = l.n, work(l)
                u = w.u[0:n, :, 0:n]
                a = w.a[0:n, :, 0:n]
                f = got(f"row{l.key}")
                link(nc.vector.tensor_tensor(u, heads_of(f, l), over_heads(gsum, l), ALU.subtract))
                if l.tile:
                    link(nc.vector.tensor_tensor(w.qk, u, mask_heads(amask(upto(l)), l), ALU.add))
                link(nc.vector.tensor_tensor(u, u, mask_heads(amask(1 - upto(l)), l), ALU.subtract))
                if l.tile == 0:
                    dve.sem_inc(free[f.b], 1)
                dve.sem_inc(sem(f"u{l.i}"), 1)
                if l.tile:
                    dve.wait_ge(sem(f"eg{l.i}"), l.r + 1)
                    q = qT[:, l.hs[0]:l.hs[0] + 4, l.at - META:l.at - META + n]
                    link(nc.vector.tensor_tensor(w.qd, w.qd, q, ALU.mult))
                    dve.sem_inc(sem(f"q{l.i}"), 1)
                dve.wait_ge(sem(f"d{l.i}"), l.r + 1)
                f = got(f"kk{l.key}")
                link(nc.vector.tensor_tensor(a, heads_of(f, l), u, ALU.mult))
                dve.sem_inc(free[f.b], 1)
                link(nc.vector.tensor_tensor(a, a, over_heads(beta, l), ALU.mult))
                dve.sem_inc(sem(f"a{l.i}"), 1)
                if l.tile:
                    f = got(f"kq{l.key}")
                    link(nc.vector.tensor_tensor(w.qk, w.qk, heads_of(f, l), ALU.mult))
                    dve.sem_inc(free[f.b], 1)
                    dve.sem_inc(sem(f"q{l.i}"), 1)

            def t_level(l, v):
                n, w = l.n, work(l)
                t, tt = w.t[0:n, :, 0:n], w.tt[0:n, :, 0:n]
                done = am_count[l.i] + v + 1
                if v == 0:
                    eye = mask_heads(ident, l)
                    dve.wait_ge(sem(f"am{l.i}"), done)
                    link(nc.vector.tensor_tensor(t, eye, w.am[0][0:n, :, 0:n], ALU.subtract))
                    f = got(f"z{l.key}0")
                    link(nc.vector.tensor_tensor(tt, eye, heads_of(f, l), ALU.subtract))
                    dve.sem_inc(free[f.b], 1)
                    dve.sem_inc(sem(f"tt{l.i}"), 1)
                    dve.sem_inc(sem(f"t{l.i}"), 1)
                    return
                f = got(f"yt{l.key}{v}")
                link(nc.vector.tensor_tensor(tt, tt, heads_of(f, l), ALU.subtract))
                dve.sem_inc(free[f.b], 1)
                if v == l.levels - 1:
                    link(nc.vector.tensor_tensor(tt, tt, over_heads(beta, l), ALU.mult))
                    dve.sem_inc(sem(f"tt{l.i}"), 1)
                    return
                dve.sem_inc(sem(f"tt{l.i}"), 1)
                f = got(f"y{l.key}{v}")
                link(nc.vector.tensor_tensor(t, t, heads_of(f, l), ALU.subtract))
                dve.sem_inc(free[f.b], 1)
                dve.sem_inc(sem(f"t{l.i}"), 1)

            def head_cols(x, l, t=None):
                return x[:, l.hs[0] * P:(l.hs[0] + 4) * P].rearrange("p (h c) -> p h c", h=4)

            def take_keys(l):
                w = work(l)
                f = got(f"r{l.key}")
                link(nc.vector.tensor_tensor(w.x, heads_of(f, l), over_heads(edec, l), ALU.mult))
                dve.sem_inc(free[f.b], 1)
                link(nc.vector.tensor_tensor(w.x, w.x, head_cols(v_tok[:, l.tile - 1, :], l), ALU.add))
                dve.sem_inc(sem(f"xk{l.i}"), 1)

            def take_values(l):
                w = work(l)
                f = got(f"vn{l.key}0")
                dve.wait_ge(sem(f"vn{l.i}"), l.r + 1)
                if l.r >= 2:
                    dve.sem_inc(free[f.b], 1)
                    return
                link(nc.vector.tensor_tensor(w.z2, heads_of(f, l), over_heads(krem, l), ALU.mult))
                dve.sem_inc(free[f.b], 1)
                dve.sem_inc(sem(f"vd{l.i}"), 1)

            def take_out(l):
                f = got(f"o{l.key}")
                o = o_T[:, l.hs[0]:l.hs[0] + 4, l.at - META:l.at - META + P]
                if l.first_out:
                    link(nc.vector.tensor_copy(o, heads_of(f, l)))
                else:
                    link(nc.vector.tensor_tensor(o, o, heads_of(f, l), ALU.add))
                dve.sem_inc(free[f.b], 1)
                if not l.first_out:
                    dve.sem_inc(sem("o_b"), 1)

            def take_state(l):
                s = head_cols(state[l.d], l)
                w = work(l)
                f = got(f"ds{l.key}0")
                link(nc.vector.tensor_tensor(s, s, over_heads(eall, l, P), ALU.mult))
                link(nc.vector.tensor_tensor(s, s, heads_of(f, l), ALU.add))
                dve.sem_inc(free[f.b], 1)
                dve.sem_inc(sem(f"s_{l.d}"), 1)

            am_count = [0, 0, 0]
            for r, lanes in enumerate(ROUNDS):
                now = ([meta] if r == 0 else []) + lanes
                before = ROUNDS[r - 1] if r else []
                for l in now:
                    lane_matrices(l)
                for v in range(7):
                    for l in now:
                        if v == 0:
                            t_level(l, v)
                    if v == 1:
                        for l in before: take_keys(l)
                    if v == 3:
                        for l in before: take_values(l)
                    if v == 5:
                        for l in before: take_out(l)
                    if v == 6 and r < 3:
                        for l in before: take_state(l)
                    if v:
                        for l in now:
                            if v < l.levels:
                                t_level(l, v)
                    if r == 0 and v == 5:
                        for part in range(2):
                            f = got(f"vn{meta.key}{part}")
                            k = krem[0:META, 0, 4 * part:4 * part + 4].unsqueeze(2).to_broadcast([META, 4, P])
                            link(nc.vector.tensor_tensor(x_meta[0:META, part * 512:(part + 1) * 512].rearrange("p (h c) -> p h c", h=4),
                                                         f.bank[0:META, :].rearrange("p (h c) -> p h c", h=4), k, ALU.mult))
                            dve.sem_inc(free[f.b], 1)
                            dve.sem_inc(sem("vd2"), 1)
                    if r == 0 and v == 6:
                        for part in range(2):
                            f = got(f"ds{meta.key}{part}")
                            link(nc.vector.tensor_copy(state["f"][:, part * 512:(part + 1) * 512], f.bank[:, :]))
                            dve.sem_inc(free[f.b], 1)
                            dve.sem_inc(sem("s_f"), 1)
                for l in now:
                    am_count[l.i] += l.levels
            for l in ROUNDS[-1]: take_keys(l)
            for l in ROUNDS[-1]: take_values(l)
            for l in ROUNDS[-1]: take_out(l)
            for i in range(4):
                f = got(f"no{i}")
                link(nc.vector.tensor_scalar(o_rn[:, 2 * i:2 * i + 2, :], two(f.bank), 1.0 / P, EPS, ALU.mult, ALU.add))
                dve.sem_inc(free[f.b], 1)
                dve.sem_inc(sem("ss_o"), 1)
            for i in range(2):
                dve.wait_ge(sem("sd_o"), i + 1)
                rn = o_rn[:, 4 * i:4 * i + 4, :]
                o = o_T[:, 4 * i:4 * i + 4, :]
                link(nc.vector.reciprocal(rn, rn))
                link(nc.vector.scalar_tensor_tensor(o, o, col("out_g"), rn, ALU.mult, ALU.mult))
            for j in range(4):
                dve.wait_ge(sem("z_g"), j + 1)
                o = o_T[:, 2 * j:2 * j + 2, :]
                link(nc.vector.tensor_tensor(o, o, z_g[:, j], ALU.mult))
                dve.sem_inc(sem("y_delta"), 1)
            for j in range(4):
                f = got(f"wd{j}")
                dve.wait_ge(sem("z_g"), 4 + j + 1)
                y4 = y_four[:, 2 * j:2 * j + 2, :]
                link(nc.vector.tensor_tensor(z_g[:, j], two(f.bank), z_g[:, j], ALU.mult))
                link(nc.vector.tensor_tensor(y4, y4, z_g[:, j], ALU.add))
                dve.sem_inc(free[f.b], 1)
                dve.sem_inc(sem("merged2"), 1)
            for j in range(4):
                f = got(f"wp{j}")
                r = res[:, 2 * j:2 * j + 2, META:]
                link(nc.vector.tensor_tensor(r, r, two(f.bank), ALU.add))
                dve.sem_inc(free[f.b], 1)
                dve.sem_inc(sem("h2"), 1)

            f = got("ssq4")
            nc.vector.tensor_scalar(rms4, f.bank[:, 0:SEQ], 1.0 / D, EPS, ALU.mult, ALU.add).then_inc(sem("variance"), 1)
            dve.wait_ge(sem("deviation"), 6)
            link(nc.vector.reciprocal(rms4, rms4))
            dve.sem_inc(free[f.b], 1)
            for k in range(KD):
                nc.vector.scalar_tensor_tensor(m_T[:, k, :], res[:, k, META:], col("norm2_g", k), rms4, ALU.mult,
                                               ALU.mult).then_inc(sem("normed"), 1)
            link(nc.vector.memset(r_ones, 1.0))
            f = got("router")
            for t in range(TT):
                link(nc.vector.tensor_tensor(router[:, t, :], f.bank[:, t * 72:(t + 1) * 72], row("b_router"), ALU.add))
            dve.sem_inc(free[f.b], 1)

            def first_of(out, x, value, n):
                link(nc.vector.tensor_scalar(r_eq[:, 0:n], x, value, None, ALU.is_equal))
                link(nc.vector.tensor_tensor_scan(r_cum[:, 0:n], r_ones[:, 0:n], r_eq[:, 0:n], 0.0, ALU.mult, ALU.add))
                link(nc.vector.scalar_tensor_tensor(out, r_cum[:, 0:n], 1.0, r_eq[:, 0:n], ALU.is_equal, ALU.mult))

            def top(out, x):
                link(nc.vector.tensor_reduce(out, x, AX.X, ALU.max))

            for t in range(TT):
                groups = router[:, t, 0:GROUPS]
                experts = router[:, t, GROUPS:]
                by_group = experts.rearrange("p (g e) -> p g e", g=GROUPS)
                top(r_top[:, 0:1], groups)
                first_of(r_oh, groups, r_top[:, 0:1], GROUPS)
                link(nc.vector.tensor_scalar(r_oh, r_oh, 1.0, BIG, ALU.subtract, ALU.mult))
                link(nc.vector.tensor_tensor(by_group, by_group, r_oh.unsqueeze(2).to_broadcast([P, GROUPS, GROUPS]), ALU.add))
                top(r_top[:, 1:2], experts)
                first_of(pick[0], experts, r_top[:, 1:2], EXPERTS)
                link(nc.vector.scalar_tensor_tensor(pick[1], pick[0], -BIG, experts, ALU.mult, ALU.add))
                top(r_second[:, t:t + 1], pick[1])
                link(nc.vector.tensor_scalar(r_nmax[:, 2 * t:2 * t + 2], r_top[:, 0:2], -1.0, None, ALU.mult))
                link(nc.vector.tensor_copy(code[:, t, :], pick[1]))
                first_of(pick[1], code[:, t, :], r_second[:, t:t + 1], EXPERTS)
                nc.vector.tensor_tensor(chosen[:, t, :], pick[0], pick[1], ALU.add).then_inc(sem("chosen"), 1)
                dve.wait_ge(sem("chosen"), t + 1)
                dve.sem_inc(sem("r_max"), 1)
                dve.wait_ge(sem("r_exp"), t + 1)
                rs = r_sum[:, 2 * t:2 * t + 2]
                sec = r_second[:, t:t + 1]
                link(nc.vector.reciprocal(rs, rs))
                link(nc.vector.tensor_tensor(sec, sec, rs[:, 1:2], ALU.mult))
                link(nc.vector.tensor_tensor(r_top[:, 2:3], rs[:, 1:2], sec, ALU.add))
                link(nc.vector.reciprocal(r_top[:, 2:3], r_top[:, 2:3]))
                link(nc.vector.tensor_tensor(r_top[:, 2:3], r_top[:, 2:3], rs[:, 0:1], ALU.mult))
                link(nc.vector.tensor_tensor(r_top[:, 3:4], r_top[:, 2:3], rs[:, 1:2], ALU.mult))
                link(nc.vector.tensor_tensor(r_top[:, 4:5], r_top[:, 2:3], sec, ALU.mult))
                link(nc.vector.tensor_scalar(weight[:, t, :], pick[0], r_top[:, 3:4], None, ALU.mult))
                link(nc.vector.scalar_tensor_tensor(weight[:, t, :], pick[1], r_top[:, 4:5], weight[:, t, :], ALU.mult, ALU.add))
            f = got("ranks")
            FAR = 1e6
            for t in range(TT):
                link(nc.vector.scalar_tensor_tensor(code[:, t, :], f.bank[:, 64 * t:64 * (t + 1)], FAR, chosen[:, t, :], ALU.add, ALU.mult))
                link(nc.vector.tensor_scalar(code[:, t, :], code[:, t, :], -(FAR + 1.0), None, ALU.add))
            link(nc.vector.tensor_reduce(r_top[:, 0:1], f.bank[:, 128:192], AX.X, ALU.max))
            dve.sem_inc(free[f.b], 1)
            dve.wait_ge(sem("slots"), 1)
            link(nc.vector.tensor_scalar(passes_f[:, 0:MOST], cap_steps, r_top[:, 0:1], None, ALU.is_lt))
            link(nc.vector.tensor_reduce(r_top[:, 1:2], passes_f[:, 0:MOST], AX.X, ALU.add))
            link(nc.vector.tensor_copy(passes_i, r_top[0:1, 1:2]))
            dve.sem_inc(sem("passes"), 1)

            n_passes = read_passes(nc.vector, dve)
            slots4 = slot_of.rearrange("p (j s) -> p j s", j=PER)
            dve.sem_inc(sem("pick_T"), 1)
            dve.sem_inc(sem("hid"), 1)
            dve.sem_inc(sem("added"), 4)
            with dve.Fori(0, n_passes) as p:
                with dve.Fori(0, N_GROUPS // 2) as pair:
                  for u in range(2):
                    q = 2 * pair + u
                    it = p * N_GROUPS + q
                    dve.wait_ge(sem("pick_T"), it + 1)
                    for t in range(TT):
                        link2(nc.vector.tensor_tensor(pick_m[:, t, :].rearrange("p (j s) -> p j s", j=PER), slots4,
                                                      code[:, t, bass.ds(q * PER, PER)].unsqueeze(2).to_broadcast([P, PER, CAP]),
                                                      ALU.is_equal), dve, "picks_m", it * 2 + t + 1)
                    for t in range(TT):
                        last = nc.vector.tensor_tensor(pick_w[:, t, :].rearrange("p (j s) -> p j s", j=PER),
                                                       pick_m[:, t, :].rearrange("p (j s) -> p j s", j=PER),
                                                       weight[:, t, bass.ds(q * PER, PER)].unsqueeze(2).to_broadcast([P, PER, CAP]),
                                                       ALU.mult)
                    last.then_inc(sem("picks"), 1)
                    dve.wait_ge(sem("gathered"), 3 * it + 2)
                    nc.vector.tensor_copy(xg[:, 4:8, :].rearrange("p k s -> p (k s)"), banks[1][:, :]).then_inc(sem("xg"), 1)
                    dve.wait_ge(sem("gathered"), 3 * it + 3)
                    nc.vector.tensor_copy(pick_T, banks[2][:, 0:SEQ]).then_inc(sem("pick_T"), 1)
                    dve.wait_ge(sem("silu"), it + 1)
                    nc.vector.tensor_tensor(hid, act_g, banks[3][:, FE:2 * FE], ALU.mult).then_inc(sem("hid"), 1)
                    dve.wait_ge(sem("down"), 2 * it + 4)
                    nc.vector.tensor_copy(yb[:, 512:D], banks[6][:, :]).then_inc(sem("yb"), 1)
                    for i, b in enumerate((0, 1, 2, 7)):
                        dve.wait_ge(sem("scattered"), 4 * it + i + 1)
                        x = res[:, 2 * i:2 * i + 2, META:]
                        nc.vector.tensor_tensor(x, x, two(banks[b]), ALU.add).then_inc(sem("added"), 1)
                nc.vector.tensor_scalar(code, code, -float(CAP), None, ALU.add).then_inc(sem("code"), 1)
                dve.wait_ge(sem("code"), p + 1)
            dve.sem_inc(sem("moe_done"), 1)
            dve.wait_ge(sem("ssq5"), 1)
            nc.vector.tensor_scalar(rms4, banks[3][:, 0:SEQ], 1.0 / D, EPS, ALU.mult, ALU.add).then_inc(sem("variance"), 1)
            dve.wait_ge(sem("deviation"), 7)
            link(nc.vector.reciprocal(rms4, rms4))
            for k in range(KD):
                nc.vector.scalar_tensor_tensor(out_T[:, k, :], res[:, k, META:], col("last_g", k), rms4, ALU.mult,
                                               ALU.mult).then_inc(sem("final"), 1)

        @block.gpsimd
        def _(pool):
            pool.wait_ge(sem("ws_in"), 16)
            nc.gpsimd.affine_select(out=wsT, in_=wsT, compare_op=ALU.is_ge, fill=0.0, base=0,
                                    pattern=[[0, NH], [1, P]], channel_multiplier=-1).then_inc(sem("ws_masked"), 1)

            t_count = [0, 0, 0]
            for r, lanes in enumerate(ROUNDS):
                now = ([meta] if r == 0 else []) + lanes
                for v in range(7):
                    for l in now:
                        if v >= l.levels:
                            continue
                        n, w = l.n, work(l)
                        if v == 0:
                            pool.wait_ge(sem(f"a{l.i}"), l.r + 1)
                            if r == 0:
                                pool.wait_ge(sem("second_in"), 16 * 5)
                        if v >= 2:
                            f = fills[f"z{l.key}{v - 2}"]
                            pool.wait_ge(full[f.b], f.n + 1)
                        if v == 2:
                            pool.wait_ge(sem(f"t{l.i}"), t_count[l.i] + 1)
                        m = level_mask[:, (v + (0 if l.d == "f" else 7)) * P:][:, 0:P]
                        nc.gpsimd.tensor_tensor(w.am[v % 2][0:n, :, 0:n], w.a[0:n, :, 0:n],
                                                m[0:n, 0:n].unsqueeze(1).to_broadcast([n, len(l.hs), n]),
                                                ALU.mult).then_inc(sem(f"am{l.i}"), 1)
                for l in now:
                    t_count[l.i] += l.levels - 1

            pool.wait_ge(sem("normed"), 2 * KD + 1)
            nc.gpsimd.iota(slot_i, pattern=[[0, PER], [1, CAP]], base=0, channel_multiplier=0).then_inc(sem("pool_chain"), 1)
            nc.gpsimd.iota(steps_i, pattern=[[CAP, MOST]], base=0, channel_multiplier=0).then_inc(sem("pool_chain"), 1)
            pool.wait_ge(sem("pool_chain"), 2)
            nc.gpsimd.tensor_copy(slot_of, slot_i).then_inc(sem("pool_chain"), 1)
            nc.gpsimd.tensor_copy(cap_steps, steps_i).then_inc(sem("pool_chain"), 1)
            pool.wait_ge(sem("pool_chain"), 4)
            pool.sem_inc(sem("slots"), 1)

        @block.sync
        def _(sp):
            sp.dma_start(res[:, :, :], A["hcatT"]).then_inc(sem("res_in"), 16)
            sp.dma_start(cols, A["cols"]).then_inc(sem("cols_in"), 16)
            sp.dma_start(arena[:, consts_at:consts_at + 4 * P], A["consts"]).then_inc(sem("consts_in"), 16)
            for b in range(N_BLOCKS):
                if b >= SLOTS:
                    last = readers[b - SLOTS]
                    sp.wait_ge(full[last.b], last.n + 1)
                sp.dma_start(ring[b % SLOTS], FRONT[b]).then_inc(sem(f"slot{b % SLOTS}_in"), 16)
                if b == FIN + 2:
                    sp.wait_ge(sem("final"), KD)
                    sp.dma_start(dft_d, A["dft_d"]).then_inc(sem("second_in"), 16)
                    sp.dma_start(dft_l, A["dft_l"]).then_inc(sem("second_in"), 16)
                    sp.dma_start(w_ab, A["w_ab"]).then_inc(sem("second_in"), 16)
                    sp.dma_start(tri[:, 0:4 * P], A["tri"]).then_inc(sem("second_in"), 16)
                    sp.dma_start(level_mask, A["level"]).then_inc(sem("second_in"), 16)
                if b == 3:
                    sp.dma_start(sel[0:NH], A["sel"]).then_inc(sem("small_in"), 16)
                    sp.dma_start(rows, A["rows"]).then_inc(sem("small_in"), 16)
                    sp.dma_start(ln_rows, A["ln_rows"]).then_inc(sem("small_in"), 16)
                    sp.dma_start(wuk, A["wuk"]).then_inc(sem("small_in"), 16)
                    sp.dma_start(wuv, A["wuv"]).then_inc(sem("small_in"), 16)
                    sp.dma_start(wsT, A["wsT"]).then_inc(sem("ws_in"), 16)
                    sp.dma_start(bs[0:1, :], A["bs"]).then_inc(sem("small_in"), 16)
            def load_gate_up(q, u, js=range(PER)):
                for j in js:
                    name = "odd_in" if u else f"slot{(N_BLOCKS + j) % SLOTS}_in"
                    src = A["gate_up"][q, j] if isinstance(q, int) else A["gate_up"][bass.ds(q, 1), j].rearrange("o p c -> (o p) c")
                    sp.dma_start(gate_up[u][j], src).then_inc(sem(name), 16)

            def load_down(q):
                for j in range(2):
                    src = A["down"][q, j] if isinstance(q, int) else A["down"][bass.ds(q, 1), j].rearrange("o p c -> (o p) c")
                    sp.dma_start(down[j], src).then_inc(sem("down_in"), 16)

            sp.wait_ge(sem("o_b"), 4)
            load_down(0)
            load_gate_up(1, 1, [3])
            sp.wait_ge(sem("merged2"), 4)
            sp.dma_start(w_router, A["w_router"]).then_inc(sem("router_in"), 16)
            for j in range(PER):
                last = readers[N_BLOCKS + j - SLOTS]
                sp.wait_ge(full[last.b], last.n + 1)
                load_gate_up(0, 0, [j])
            sp.wait_ge(sem("normed"), 2 * KD + 1)
            load_gate_up(1, 1, range(3))
            n_passes = read_passes(nc.sync, sp)
            with sp.Fori(0, n_passes * (N_GROUPS // 2) - 1) as pair:
                for u in range(2):
                    g = 2 * pair + u + 1
                    sp.wait_ge(sem("down"), 2 * g + 2)
                    load_down(g % N_GROUPS)
                    sp.wait_ge(sem("gate_up"), g)
                    load_gate_up((g + 1) % N_GROUPS, u)
            sp.wait_ge(sem("down"), n_passes * (2 * N_GROUPS))
            load_down(N_GROUPS - 1)
            for i in range(4):
                sp.wait_ge(sem("final"), KD + 2 * i + 2)
                sp.dma_start(A["o"][:, 2 * i:2 * i + 2, :], out_T[:, 2 * i:2 * i + 2, :]).then_inc(sem("out"), 16)
            sp.wait_ge(sem("out"), 64)


def constants():
    f32 = np.float32
    p, c = np.arange(P)[:, None], np.arange(P)[None]
    le, ge = p <= c, p >= c
    angle = 2 * np.pi * np.outer(np.arange(P), np.arange(P)) / P
    out = {
        "consts": np.concatenate([np.eye(P), np.ones((P, P)), np.zeros((P, P)), np.where(ge, 0, -BIG)], 1),
        "sel": np.repeat(np.eye(NH)[:, :, None], SEQ, 2),
        "tri": np.concatenate([np.where(le, 0, -1e30), np.where(ge, 0, -1e30), le, ge], 1),
        "dft_d": np.concatenate([np.cos(angle), -np.sin(angle)], 1),
    }
    angle = 2 * np.pi * (np.outer(np.arange(LEN), np.arange(META, LEN)) % LEN) / LEN
    both = np.concatenate([np.cos(angle), np.sin(angle)], 1) / np.sqrt(LEN * P)
    out["dft_l"] = np.zeros((P, 3, 2 * SEQ))
    out["dft_l"][:META, 0] = both[:META]
    out["dft_l"][:, 1:] = both[META:].reshape(TT, P, 2 * SEQ).transpose(1, 0, 2)
    lower = [((p >> (v + 1)) == (c >> (v + 1))) & ((p >> v) % 2 == 1) & ((c >> v) % 2 == 0) for v in range(7)]
    out["level"] = np.concatenate(lower + [m.T for m in lower], 1)
    return {name: np.ascontiguousarray(a, dtype=f32) for name, a in out.items()}


def by_rows(m, width=W1):
    if m.shape[1] < width:
        m = np.concatenate([m, np.zeros((m.shape[0], width - m.shape[1]), m.dtype)], 1)
    return m.reshape(-1, P, width).transpose(1, 0, 2).reshape(P, BLOCK)


def cut(w, names, sizes):
    ends = np.cumsum([0] + sizes)
    return {n: w[:, ends[i]:ends[i + 1]] for i, n in enumerate(names)}


def lay_out(I):
    halves = lambda m: [by_rows(m[:, :W1]), by_rows(m[:, W1:])]
    w = cut(I["w_in"][0], "au av az bq bc qi ki wi bz cb cc cx cz dq dk dv df dz gates".split(),
            [W1, W1, W1, W1, P, NH * IDX, IDX, NH, W1, W1, W1, W1, W1, W1, W1, W1, NH, W1, 4 * D])
    front = [by_rows(np.concatenate([w[n] for n in ("bc", "wi", "df", "qi", "ki")], 1))]
    front += [by_rows(w[n]) for n in "bq dq dk dv av au az dz bz cb cc cx cz".split()]
    for n in (0, 3, 2, 1):
        front += halves(w["gates"][:, n * D:(n + 1) * D]) + [by_rows(I["w_branch"][0, n], D)]
    front += halves(I["w_out"][0])
    w = cut(I["w_in_2"][0], "four q k v z a_f b_f a_b b_b gate_f gate_d".split(), [W1, D, D, D, D, 8, 8, 8, 8, D, D])
    q, k, v, z, gate_d, w_delta = (halves(m) for m in (w["q"], w["k"], w["v"], w["z"], w["gate_d"], I["w_delta_2"][0]))
    front += [by_rows(w["four"]), k[0], v[0], by_rows(I["w_fourier_2"][0], D)] + halves(w["gate_f"]) + [q[0], k[1], v[1], q[1]]
    front += z + [gate_d[0], w_delta[0], gate_d[1], w_delta[1]] + halves(I["w_out_2"][0])

    chunks = lambda a: a.reshape(-1, P).T
    b_f = np.concatenate([I["fox_b_f"][0], np.zeros(P - NH, I["fox_b_f"].dtype)])[:, None]
    cols = [chunks(a) for a in (I["norm_g"], I["final_g"], I["conv_w"], I["dsa_kv_g"])] + [b_f]
    cols += [chunks(I[n + "_2"]) for n in ("norm1_g", "norm2_g", "final_norm_g", "conv_w", "out_norm_g")]
    row = np.concatenate([I[n + "_2"].ravel() for n in ("dt_bias_fwd", "dt_bias_bwd", "a_log_fwd", "a_log_bwd",
                                                        "b_router_group", "b_router_expert")])
    ln = np.concatenate([I["gm_ln_g"][0], I["gm_ln_b"][0]])
    on_all = lambda a: np.broadcast_to(a, (P, a.size))
    tokens = np.concatenate([I["meta_tokens_2"], I["x"][0]], 0)
    router = np.concatenate([I["w_router_group_2"][0], I["w_router_expert_2"][0]], 1)
    gate_up = np.concatenate([I["w_gate_e_2"][0], I["w_up_e_2"][0]], 2)
    n = EXPERTS // PER
    out = {
        "front": np.stack(front),
        "cols": np.concatenate(cols, 1), "rows": on_all(row), "ln_rows": on_all(ln),
        "hcatT": tokens.T.reshape(KD, P, LEN).transpose(1, 0, 2),
        "wuk": I["dsa_w_uk"][0].transpose(2, 0, 1), "wuv": I["dsa_w_uv"][0].transpose(1, 0, 2),
        "wsT": I["gm_w_s"][0].transpose(2, 0, 1), "bs": I["gm_b_s"][0].reshape(1, W1),
        "w_ab": np.concatenate([w[x] for x in ("a_f", "a_b", "b_f", "b_b")], 1).reshape(KD, P, 32).transpose(1, 0, 2),
        "w_router": router.reshape(KD, P, 72).transpose(1, 0, 2),
        "gate_up": gate_up.reshape(n, PER, KD, P, 2 * FE).transpose(0, 1, 3, 2, 4).reshape(n, PER, P, BLOCK),
        "down": I["w_down_e_2"][0].reshape(n, 2, 2, 2, P, D).transpose(0, 1, 4, 2, 3, 5).reshape(n, 2, P, BLOCK),
    }
    return {name: np.ascontiguousarray(a) for name, a in out.items()}


def kernel(**inputs):
    import concourse.bacc as bacc
    from concourse.bass_utils import run_bass_kernel_spmd

    arrays = {**lay_out({name: np.asarray(a) for name, a in inputs.items()}), **constants()}
    nc = bacc.Bacc("TRN2", target_bir_lowering=False, num_devices=1)
    tensors = {name: nc.dram_tensor(name, a.shape, mybir.dt.from_np(a.dtype), kind="ExternalInput").ap()
               for name, a in arrays.items()}
    tensors["o"] = nc.dram_tensor("o", (P, KD, SEQ), mybir.dt.float32, kind="ExternalOutput").ap()
    build(nc, tensors)
    result = run_bass_kernel_spmd(nc, [arrays], core_ids=[0])
    got = result.results[0]["o"]
    return np.ascontiguousarray(got.transpose(2, 1, 0).reshape(1, SEQ, D))
```

```python
from contextlib import ExitStack

import numpy as np

import concourse.bass as bass
from concourse import mybir

D = 1024
SEQ = 256
P = 128
KD = D // P
TT = SEQ // P
META = 16
LEN = SEQ + META
W1 = 512
CW = W1 // P
NH = 4
TOPK = SEQ // 4
IDX = 64
EPS = 1e-6
BIG = 3e38
HEADS = 8
EXPERTS, GROUPS, FE = 64, 8, 256
SLOTS = 4
BLOCK = 4096
PER, CAP = 4, 32
MOST = SEQ // CAP
HALF = BLOCK // 2
QUARTER = HALF // 2
RAW, SPLIT = 4, 3

COLS, _at = {}, 0
for _n, _w in (("norm_g", KD), ("final_g", KD), ("conv_w", 3 * CW), ("kv_g", 1), ("b_f", 1), ("norm1_g", KD),
               ("norm2_g", KD), ("last_g", KD), ("conv5", 5 * 24), ("out_g", 1)):
    COLS[_n] = (_at, _at + _w)
    _at += _w
N_COLS = _at
ROWS, _at = {}, 0
for _n, _w in (("dt", 16), ("a_log", 16), ("b_router", 72)):
    ROWS[_n] = (_at, _at + _w)
    _at += _w
N_ROWS = _at


class Fill:

    def __init__(self, b, n, bank, order):
        self.b, self.n, self.bank, self.order = b, n, bank, order


class Lane:

    def __init__(self, i, d, tile, half):
        self.i, self.d, self.tile, self.half, self.r = i, d, tile, half, 0
        self.hs = list(range(HEADS)) if tile == 0 else list(range(4 * half, 4 * half + 4))
        self.n = META if tile == 0 else P
        self.at = 0 if tile == 0 else META + (tile - 1) * P
        self.j = 0 if d == "f" else 8
        self.levels = 4 if tile == 0 else 7
        self.key = f"{d}{tile}{half}"
        self.s_before, self.first_out = 0, False


class Work:

    def __init__(self, u, a, am, t, z, tt, qk=None, qd=None, x=None, z2=None):
        self.u, self.a, self.am, self.t, self.z, self.tt = u, a, am, t, z, tt
        self.qk, self.qd, self.x, self.z2 = qk, qd, x, z2


def build(nc, A):
    f32, f32r = mybir.dt.float32, mybir.dt.float32r
    ALU, ACT, AX = mybir.AluOpType, mybir.ActivationFunctionType, mybir.AxisListType
    ctx = ExitStack()
    with ctx:
        sems = {}

        def sem(name):
            if name not in sems:
                sems[name] = ctx.enter_context(nc.semaphore(name))
            return sems[name]

        RING, ARENA = SLOTS * BLOCK, 36824
        with nc.sbuf_tensor("weights", [P, RING], f32) as weights, nc.sbuf_tensor("arena", [P, ARENA], f32) as arena:
            pass
        top = [0]

        def place(cols):
            at = top[0]
            top[0] += cols
            assert top[0] <= ARENA, top[0]
            return arena[:, at:at + cols]

        def rounded(at, cols):
            assert at % 8 == 0
            name = f"{at}_{cols}"
            with nc.sbuf_tensor(f"below_{name}", [P, at], f32), nc.sbuf_tensor(f"rounded_{name}", [P, cols], f32r) as x:
                pass
            return x[:, :]

        def both(cols):
            x = place(cols)
            return x, rounded(RING + top[0] - cols, cols)

        raw = [weights[:, i * QUARTER:(i + 1) * QUARTER] for i in range(RAW)]
        w_hi = [rounded(RAW * QUARTER + i * HALF, HALF) for i in range(SPLIT)]
        w_lo = [rounded(RAW * QUARTER + (SPLIT + i) * HALF, HALF) for i in range(SPLIT)]
        ring = [weights[:, i * BLOCK:(i + 1) * BLOCK] for i in range(SLOTS)]
        res = place(KD * LEN).rearrange("p (k t) -> p k t", k=KD)
        cols = place(N_COLS)
        consts_at = top[0]
        ident = place(P)
        ones = place(P)
        mask = place(2 * P)
        stats = place(256)
        rows = place(N_ROWS)
        tri = place(4 * P)
        top[0] = layer_base = -(-top[0] // 8) * 8

        def col(name, j=0):
            a = COLS[name][0]
            return cols[:, a + j:a + j + 1]

        stat_at = [0]

        def stat(n):
            a = stat_at[0]
            stat_at[0] += n
            assert stat_at[0] <= 256
            return stats[:, a:a + n]

        banks = [ctx.enter_context(nc.psum_tensor(f"bank{b}", [P, 512], f32)) for b in range(8)]
        full = [sem(f"bank{b}_full") for b in range(8)]
        free = [sem(f"bank{b}_free") for b in range(8)]
        fills, uses, turn, readers = {}, [0] * 8, {}, {}

        def fill(name, pool, block=None):
            b = pool[turn.get(pool, 0) % len(pool)]
            turn[pool] = turn.get(pool, 0) + 1
            fills[name] = Fill(b, uses[b], banks[b], len(fills))
            uses[b] += 1
            if block is not None:
                readers[block] = fills[name]

        def quarter(q):
            return slice(q % 2 * QUARTER, (q % 2 + 1) * QUARTER)

        def whole_in(i):
            return 16 * (2 * N_HALVES // RAW + i // SLOTS + 1)

        PJ, WK = (0, 1, 2), (3, 4, 5, 6, 7)
        INDEX, BQ, DQ, DK, DV, AV, AU, AZ, DZ, BZ, CB, CC, CX, CZ = range(14)
        ORDER = (0, 3, 2, 1)
        GATE = {n: 14 + 3 * i for i, n in enumerate(ORDER)}
        WB = {n: 16 + 3 * i for i, n in enumerate(ORDER)}
        WO = 26
        FIN, K0, V0, WF, GF, Q0, K1, V1, Q1, ZB, GD, WD, WO2 = 28, 29, 30, 31, 32, 34, 35, 36, 37, 38, 40, 41, 44
        N_BLOCKS = 46
        N_HALVES = 2 * ZB

        top[0] = layer_base
        g_ = lambda n: place(n)
        chunked = lambda pair, k: [x.rearrange("p (k t) -> p k t", k=k) for x in pair]
        h1_hi, h1_hi_r = chunked(both(KD * SEQ), KD)
        h1_lo, h1_lo_r = chunked(both(KD * SEQ), KD)
        h1 = h1_hi_r, h1_lo_r
        qi = g_(2 * SEQ).rearrange("p (k t) -> p k t", k=2)
        ki = g_(SEQ)
        cn = g_(TT * P).rearrange("p (k t) -> p k t", k=TT)
        wi = stat(TT * NH)
        cT = g_(SEQ)
        ff = g_(5 * SEQ).rearrange("p (k t) -> p k t", k=5)
        sel = g_(NH * SEQ).rearrange("p (h t) -> p h t", h=NH)
        bq, bq_r = chunked(both(CW * SEQ), CW)
        qlat = g_(CW * SEQ).rearrange("p (k t) -> p k t", k=CW)
        dq, dq_r = chunked(both(CW * SEQ), CW)
        dk, dk_r = chunked(both(CW * SEQ), CW)
        dv_f, dv_r = both(TT * W1)
        dv = dv_f.rearrange("p (k t) -> p k t", k=TT)
        av = g_(TT * W1).rearrange("p (k t) -> p k t", k=TT)
        ln_rows = g_(2 * W1)
        relu0 = g_(NH * P).rearrange("p (h k) -> p h k", h=NH)
        relu1 = g_(NH * SEQ).rearrange("p (h k) -> p h k", h=NH)
        score = [g_(P), g_(SEQ)]
        lg = {a: [g_(NH * P).rearrange("p (h k) -> p h k", h=NH), g_(NH * SEQ).rearrange("p (h k) -> p h k", h=NH)] for a in "fb"}
        gates_at = top[0]
        pT = g_(3 * NH * P).rearrange("p (j h q) -> p j h q", j=3, h=NH)
        olat = g_(NH * SEQ).rearrange("p (h t) -> p h t", h=NH)
        gates = arena[:, gates_at:gates_at + KD * SEQ].rearrange("p (k t) -> p k t", k=KD)
        assert gates_at + KD * SEQ <= top[0]
        wuk = g_(NH * P).rearrange("p (h l) -> p h l", h=NH)
        wuv = g_(NH * P).rearrange("p (h l) -> p h l", h=NH)
        wsT = g_(NH * P).rearrange("p (h l) -> p h l", h=NH)
        bs = g_(NH * P)
        y_both = [chunked(both(CW * SEQ), CW) for _ in range(4)]
        y = [x[0] for x in y_both]
        y_lo = [x[1] for x in y_both]
        y_hi = [bq_r, dv_r.rearrange("p (k t) -> p k t", k=CW), dk_r, dq_r]
        cpad = g_(CW * (SEQ + 2)).rearrange("p (k t) -> p k t", k=CW)
        cc = relu1
        cv = lg["f"][1]
        rms = g_(SEQ)
        css, lnsd, best, bns, mv = stat(TT), stat(TT), stat(8), stat(6), stat(4)
        nmax = {a: stat(TT * NH) for a in "fb"}
        psum = {a: stat(TT * NH) for a in "fb"}
        merged, merged_lo_r = chunked(both(KD * SEQ), KD)

        top[0] = layer_base
        hn, hn_hi_r = chunked(both(KD * LEN), KD)
        qT = place(HEADS * SEQ).rearrange("p (h t) -> p h t", h=HEADS)
        kT = place(HEADS * LEN).rearrange("p (h t) -> p h t", h=HEADS)
        k_tok = place(TT * D).rearrange("p (t c) -> p t c", t=TT)
        v_tok = place(TT * D).rearrange("p (t c) -> p t c", t=TT)
        y_four = place(KD * SEQ).rearrange("p (k t) -> p k t", k=KD)
        o_T = place(HEADS * SEQ).rearrange("p (h t) -> p h t", h=HEADS)
        hn_lo, hn_lo_r = chunked(both(KD * LEN), KD)
        state = {d: hn_lo.rearrange("p k t -> p (k t)")[:, i * D:(i + 1) * D] for i, d in enumerate("fb")}
        level_mask = place(14 * P)
        top[0] = -(-top[0] // 8) * 8
        beta = place(3 * 16).rearrange("p (t j) -> p t j", t=3)
        gl = place(3 * 16).rearrange("p (t j) -> p t j", t=3)
        gx = place(3 * 16).rearrange("p (t j) -> p t j", t=3)
        gsum = place(3 * 32).rearrange("p (t j) -> p t j", t=3)
        edec = place(3 * 16).rearrange("p (t j) -> p t j", t=3)
        krem = place(3 * 16).rearrange("p (t j) -> p t j", t=3)
        eall = place(3 * 16).rearrange("p (t j) -> p t j", t=3)
        nea = place(16)
        k_meta, v_meta = (o_T[:, 4 * i:4 * i + 4, :].rearrange("p h t -> p (h t)") for i in range(2))
        zone = top[0]
        rms2 = place(LEN)
        dft_d = place(2 * P)
        dft_l = place(3 * 2 * SEQ).rearrange("p (t c) -> p t c", t=3)
        w_ab, w_ab_lo_r = chunked(both(KD * 32), KD)
        f_T_f, f_T_r = both(4 * LEN)
        f_T = f_T_f.rearrange("p (g t) -> p g t", g=4)
        yf_hi, yf_hi_r = chunked((f_T_f[:, 0:4 * SEQ], f_T_r[:, 0:4 * SEQ]), 4)
        fa = place(2 * 4 * 2 * P).rearrange("p (t g c) -> p t g c", t=2, g=4)
        fa0 = place(4 * 2 * P).rearrange("p (g c) -> p g c", g=4)
        yf_T, yf_lo_r = chunked(both(4 * SEQ), 4)
        gate2 = place(2 * 512).rearrange("p (j k t) -> p j k t", j=2, k=2)
        sq2 = place(4 * LEN).rearrange("p (h t) -> p h t", h=4)
        rn2_f, rn2_r = both(4 * LEN)
        rn2 = rn2_f.rearrange("p (h t) -> p h t", h=4)
        w_ab_hi, w_ab_hi_r = chunked((rn2_f[:, 0:KD * 32], rn2_r[:, 0:KD * 32]), KD)
        v_T = [place(4 * LEN).rearrange("p (h t) -> p h t", h=4) for _ in range(2)]
        top[0] = zone
        four = lambda: place(512).rearrange("p (h c) -> p h c", h=4)
        lane_u = [four() for _ in range(2)]
        lane_z = lane_u
        lane_a = [four() for _ in range(2)]
        lane_am = [[four() for _ in range(2)] for _ in range(2)]
        lane_t = [four() for _ in range(2)]
        lane_tt = [[four() for _ in range(2)] for _ in range(2)]
        lane_qk = [[four() for _ in range(2)] for _ in range(2)]
        lane_qd = [[four() for _ in range(2)] for _ in range(2)]
        x_meta = arena[:, top[0]:top[0] + D]
        lane_x = [four() for _ in range(2)]
        mt_at = top[0]
        lane_z2 = [four() for _ in range(2)]
        lanes_end = top[0]
        top[0] = mt_at
        mt = {n: place(P).rearrange("p (h c) -> p h c", h=HEADS) for n in ("u", "a", "am0", "am1", "t", "z", "tt")}
        assert top[0] <= lanes_end
        o_sq = k_tok.rearrange("p t c -> p (t c)").rearrange("p (h t) -> p h t", h=HEADS)
        o_rn = v_tok.rearrange("p t c -> p (t c)").rearrange("p (h t) -> p h t", h=HEADS)
        z_g = kT.rearrange("p h t -> p (h t)")[:, 0:4 * 512].rearrange("p (j k t) -> p j k t", j=4, k=2)

        sq_all = arena[:, layer_base + 3 * KD * LEN:layer_base + 4 * KD * LEN].rearrange("p (k t) -> p k t", k=KD)

        meta = Lane(2, "f", 0, 0)
        ROUNDS = [[Lane(0, "f", 1, 0), Lane(1, "b", 2, 0)], [Lane(0, "f", 1, 1), Lane(1, "b", 2, 1)],
                  [Lane(0, "f", 2, 0), Lane(1, "b", 1, 0)], [Lane(0, "f", 2, 1), Lane(1, "b", 1, 1)]]
        for _r, _round in enumerate(ROUNDS):
            for _l in _round:
                _l.r = _r
        meta.r = 0
        for _l in (x for r in ROUNDS for x in r):
            _l.s_before = {"f": 2, "b": 2}[_l.d] + (0 if _l.r < 2 else (_l.r % 2) + 1)
            _l.first_out = _l.r < 2
        tt_end = {meta.key: 4} | {x.key: 7 * (x.r + 1) for r in ROUNDS for x in r}

        def work(l):
            if l.tile == 0:
                return Work(u=mt["u"], a=mt["a"], am=[mt["am0"], mt["am1"]], t=mt["t"], z=mt["z"], tt=mt["tt"])
            i, p = l.i, l.r % 2
            return Work(u=lane_u[i], a=lane_a[i], am=lane_am[i], t=lane_t[i], z=lane_z[i], tt=lane_tt[i][p],
                                   qk=lane_qk[i][p], qd=lane_qd[i][p], x=lane_x[i], z2=lane_z2[i])

        def heads_of(f, l):
            return f.bank[0:l.n, 0:len(l.hs) * l.n].rearrange("p (h c) -> p h c", h=len(l.hs))

        LE, GE = 0, 1
        amask = lambda m: tri[:, m * P:(m + 1) * P]
        omask = lambda m: tri[:, (2 + m) * P:(3 + m) * P]
        upto = lambda l: LE if l.d == "f" else GE

        top[0] = layer_base
        m_T = place(KD * SEQ).rearrange("p (k t) -> p k t", k=KD)
        m_tok = place(TT * D).rearrange("p (t c) -> p t c", t=TT)
        w_router = place(KD * 72).rearrange("p (k c) -> p k c", k=KD)
        rms4 = place(SEQ)
        router = place(TT * 72).rearrange("p (t c) -> p t c", t=TT)
        r_eq = place(64)
        r_cum = place(64)
        r_ones = place(64)
        pick = [place(64) for _ in range(2)]
        chosen = place(TT * 64).rearrange("p (t e) -> p t e", t=TT)
        weight = place(TT * 64).rearrange("p (t e) -> p t e", t=TT)
        code = place(TT * 64).rearrange("p (t e) -> p t e", t=TT)
        slot_of = place(PER * CAP)
        passes_f = place(16)
        pick_m = place(TT * P).rearrange("p (t s) -> p t s", t=TT)
        pick_w = place(TT * P).rearrange("p (t s) -> p t s", t=TT)
        pick_T = place(SEQ)
        act_g = place(FE)
        hid = place(FE)
        hid_T = place(2 * P).rearrange("p (f s) -> p f s", f=2)
        passes_i = place(1)[0:1, :].bitcast(mybir.dt.int32)
        xg = m_T.rearrange("p k t -> p (k t)")[:, 0:D].rearrange("p (k s) -> p k s", k=KD)
        yb = m_T.rearrange("p k t -> p (k t)")[:, D:2 * D]
        assert top[0] <= ARENA - 6 * BLOCK and zone <= ARENA - 3 * BLOCK, (top[0], zone)
        top[0] = ARENA - 6 * BLOCK
        odd = [place(BLOCK) for _ in range(3)]
        down = [place(BLOCK) for _ in range(2)]
        odd.append(place(BLOCK))
        gate_up = [[ring[(N_BLOCKS - ZB + j) % SLOTS] for j in range(PER)], odd]
        N_GROUPS = EXPERTS // PER
        gate_up_in = [whole_in(N_BLOCKS - ZB + j) for j in range(PER)]
        o_sq5 = down[0][:, 0:KD * SEQ].rearrange("p (k t) -> p k t", k=KD)
        out_T = m_T
        r_exp = pick_m.rearrange("p t s -> p (t s)")[:, 0:TT * 72].rearrange("p (t c) -> p t c", t=TT)
        r_nmax, r_sum, r_top, r_second, r_oh = stat(4), stat(4), stat(8), stat(2), stat(8)
        cap_steps = stat(MOST)
        slot_i = pick_T[:, 0:PER * CAP].bitcast(mybir.dt.int32)
        steps_i = pick_T[:, P:P + MOST].bitcast(mybir.dt.int32)

        def read_passes(engine, e):
            e.wait_ge(sem("passes"), 1)
            return engine.value_load(passes_i, min_val=1, max_val=MOST)

        def link2(ins, e, name, value):
            ins.then_inc(sem(name), 1)
            e.wait_ge(sem(name), value)

        block = ctx.enter_context(nc.Block())
        FRONT = A["front"]

        def two(bank):
            return bank[:, :].rearrange("p (j t) -> p j t", j=2)

        @block.tensor
        def _(pe):
            def begin(name, pool=WK, block=None):
                fill(name, pool, block)
                f = fills[name]
                if f.n > 0:
                    pe.wait_ge(free[f.b], f.n)
                return f

            def end(f, last):
                last.then_inc(full[f.b], 1)

            def halved(b, half):
                h = 2 * b + half
                pe.wait_ge(sem("w_lo"), 2 * h + 2)
                return w_hi[h % SPLIT], w_lo[h % SPLIT]

            def matmul3(out, a, b, start, stop):
                nc.tensor.matmul(out, a[0], b[1], start=start, stop=False)
                nc.tensor.matmul(out, a[0], b[0], start=False, stop=False)
                return nc.tensor.matmul(out, a[1], b[0], start=False, stop=stop)

            def project_T(names, b, x, n, stride=W1, kk=KD, per=2, pool=PJ, ready=0, column=0):
                cols, had = stride // 2, None
                for i, name in enumerate(names):
                    half, at = divmod(column + i * per * P, cols)
                    if half != had:
                        w, had = halved(b, half), half
                    f = begin(name, pool, 2 * b + half)
                    for j in range(per):
                        for k in range(kk):
                            if ready and i == j == 0:
                                pe.wait_ge(sem("normed"), ready + k + 1)
                            c = k * cols + at + j * P
                            last = matmul3(f.bank[:, j * n:(j + 1) * n], [m[:, c:c + P] for m in w],
                                           [m[:, k, :] for m in x], k == 0, k == kk - 1)
                    end(f, last)

            def project_tok(names, b):
                fs = [begin(name, PJ, 2 * b + i) for i, name in enumerate(names)]
                readers[2 * b] = fs[1]
                for half in range(2):
                    w = halved(b, half)
                    for t, f in enumerate(fs):
                        for k in range(KD):
                            last = matmul3(f.bank[:, half * SEQ:(half + 1) * SEQ], [m[:, k, t * P:(t + 1) * P] for m in h1],
                                           [m[:, k * SEQ:(k + 1) * SEQ] for m in w], k == 0, k == KD - 1)
                        if half == 1:
                            end(f, last)

            def column_sums(name, src, n):
                f = begin(name)
                for k in range(KD):
                    last = nc.tensor.matmul(f.bank[:, 0:n], ones, src[:, k, :], start=k == 0, stop=k == KD - 1)
                end(f, last)

            sq = h1_lo
            pe.wait_ge(sem("consts_in"), 16)
            pe.wait_ge(sem("squares"), 1)
            column_sums("ssq1", sq, SEQ)

            w = halved(INDEX, 0)
            part = lambda x, c, n: [m[:, c:c + n] for m in x]
            rows_of = lambda k, t=0, n=SEQ: [m[:, k, t * P:t * P + n] for m in h1]
            f = begin("c", WK, 0)
            for t in range(TT):
                for k in range(KD):
                    if t == 0:
                        pe.wait_ge(sem("normed"), k + 1)
                    last = matmul3(f.bank[:, t * SEQ:t * SEQ + P + 4], rows_of(k, t, P), part(w, k * SEQ, P + 4), k == 0, k == KD - 1)
            end(f, last)
            f = begin("f", WK, 0)
            for k in range(KD):
                last = matmul3(f.bank[0:NH, 0:SEQ], part(w, k * SEQ + 132, NH), rows_of(k), k == 0, k == KD - 1)
            end(f, last)
            f = begin("ki", PJ, 0)
            for k in range(KD):
                last = matmul3(f.bank[0:IDX, 0:SEQ], part(w, k * SEQ + 136, IDX), rows_of(k), k == 0, k == KD - 1)
            end(f, last)
            project_T(("qi",), INDEX, h1, SEQ, column=SEQ)
            project_T(("bq0", "bq1"), BQ, h1, SEQ)
            pe.wait_ge(sem("cn"), TT + 1)
            f = begin("ki2")
            end(f, nc.tensor.matmul(f.bank[IDX:, 0:SEQ], ident[0:IDX, 0:IDX], ki[0:IDX, :], start=True, stop=True))
            f = begin("cT")
            for t in range(TT):
                last = nc.tensor.transpose(f.bank[:, t * P:(t + 1) * P], cn[:, t, :], ident)
            end(f, last)
            project_T(("dq0", "dq1"), DQ, h1, SEQ)
            pe.wait_ge(sem("qiki"), 2)
            for n, (t, odd) in enumerate(((0, 0), (0, 1), (1, 0), (1, 1))):
                f = begin(f"dots{n}")
                for i, h in enumerate((odd, odd + 2)):
                    a = IDX * (h % 2)
                    m = P * (t + 1)
                    last = nc.tensor.matmul(f.bank[:, i * m:(i + 1) * m], qi[a:a + IDX, h // 2, t * P:(t + 1) * P],
                                            ki[a:a + IDX, 0:m], start=True, stop=True)
                end(f, last)
            project_T(("dk0", "dk1"), DK, h1, SEQ)
            pe.wait_ge(sem("small_in"), 16 * 6)
            pe.wait_ge(sem("bq"), 2)
            for i in range(2):
                f = begin(f"qlat{i}", PJ)
                for j in range(2):
                    last = nc.tensor.matmul(f.bank[:, j * SEQ:(j + 1) * SEQ], wuk[:, 2 * i + j, :], bq[:, 2 * i + j, :],
                                            start=True, stop=True)
                end(f, last)
            project_tok(("dv0", "dv1"), DV)

            def logits(a, q, kT):
                for n, (t, hs) in enumerate(((0, range(4)), (1, (0, 1)), (1, (2, 3)))):
                    f = begin(f"{a}l{n}")
                    m = P * (t + 1)
                    for i, h in enumerate(hs):
                        o = f.bank[:, i * m:(i + 1) * m]
                        keys = kT(h)
                        last = nc.tensor.matmul(o, q[:, h, t * P:(t + 1) * P], keys[:, 0:m], start=True, stop=a == "b")
                        if a == "f":
                            nc.tensor.matmul(o, ff[0:NH, 3, t * P:(t + 1) * P], sel[0:NH, h, 0:m], start=False, stop=False)
                            last = nc.tensor.matmul(o, sel[0:NH, h, 0:P], ff[0:NH, 4, 0:m], start=False, stop=True)
                    end(f, last)

            def transpose_p(a):
                for n, (t, kt) in enumerate(((0, 0), (1, 0), (1, 1))):
                    pe.wait_ge(sem("soft_p"), t + 1 + (TT if a == "b" else 0))
                    f = begin(f"{a}pT{n}")
                    for h in range(NH):
                        last = nc.tensor.transpose(f.bank[:, h * P:(h + 1) * P], lg[a][t][:, h, kt * P:(kt + 1) * P], ident)
                    end(f, last)

            pe.wait_ge(sem("dq"), 2)
            pe.wait_ge(sem("dk"), 2)
            pe.wait_ge(sem("forget"), 2)
            logits("f", dq, lambda h: dk[:, h, :])
            project_tok(("av0", "av1"), AV)
            project_T(("au0", "au1"), AU, h1, SEQ)
            transpose_p("f")
            project_T(("az0", "az1"), AZ, h1, SEQ)
            pe.wait_ge(sem("soft_pT"), 3)
            pe.wait_ge(sem("dv"), 2)
            for i in range(2):
                f = begin(f"fo{i}")
                for j in range(2):
                    h = 2 * i + j
                    o = f.bank[:, j * SEQ:(j + 1) * SEQ]
                    v = lambda t: dv[:, t, h * P:(h + 1) * P]
                    nc.tensor.matmul(o[:, 0:P], v(0), pT[:, 0, h, :], start=True, stop=True)
                    nc.tensor.matmul(o[:, P:SEQ], v(0), pT[:, 1, h, :], start=True, stop=False)
                    last = nc.tensor.matmul(o[:, P:SEQ], v(1), pT[:, 2, h, :], start=False, stop=True)
                end(f, last)
            pe.wait_ge(sem("av"), TT)
            pe.wait_ge(sem("ws_masked"), 1)
            for i in range(2):
                f = begin(f"mx{i}")
                for j in range(2):
                    gr = 2 * i + j
                    for t in range(TT):
                        o = f.bank[:, j * SEQ + t * P:j * SEQ + (t + 1) * P]
                        nc.tensor.matmul(o, av[:, t, gr * P:(gr + 1) * P], wsT[:, gr, :], start=True, stop=False)
                        last = nc.tensor.matmul(o, ones[0:1, :], bs[0:1, gr * P:(gr + 1) * P], start=False, stop=True)
                end(f, last)
            project_T(("dz0", "dz1"), DZ, h1, SEQ)
            pe.wait_ge(sem("cT"), 1)
            pe.wait_ge(sem("qlat"), 2)
            logits("b", qlat, lambda h: cT)
            project_T(("bz0", "bz1"), BZ, h1, SEQ)
            project_T(("cb0", "cb1"), CB, h1, SEQ)
            project_T(("cc0", "cc1"), CC, h1, SEQ)
            transpose_p("b")
            project_T(("cx0", "cx1"), CX, h1, SEQ)
            pe.wait_ge(sem("soft_pT"), 6)
            flat = lambda j: pT[:, j, :, :].rearrange("p h q -> p (h q)")
            f = begin("ol0")
            end(f, nc.tensor.matmul(f.bank[:, :], cn[:, 0, :], flat(0), start=True, stop=True))
            f = begin("ol1")
            nc.tensor.matmul(f.bank[:, :], cn[:, 0, :], flat(1), start=True, stop=False)
            end(f, nc.tensor.matmul(f.bank[:, :], cn[:, 1, :], flat(2), start=False, stop=True))
            project_T(("cz0", "cz1"), CZ, h1, SEQ)
            pe.wait_ge(sem("olat"), 2)
            for i in range(2):
                f = begin(f"bo{i}")
                for j in range(2):
                    last = nc.tensor.matmul(f.bank[:, j * SEQ:(j + 1) * SEQ], wuv[:, 2 * i + j, :], olat[:, 2 * i + j, :],
                                            start=True, stop=True)
                end(f, last)
            for n in ORDER:
                for half in range(2):
                    project_T([f"g{n}{2 * half + j}" for j in range(2)], GATE[n] + half, h1, SEQ)
                pe.wait_ge(sem(f"y{n}"), 2)
                project_T([f"br{n}{j}" for j in range(4)], WB[n], (y_hi[n], y_lo[n]), SEQ, stride=D, kk=CW)
            pe.wait_ge(sem("merged"), 4 * 4)
            for half in range(2):
                project_T([f"wo{2 * half + j}" for j in range(2)], WO + half, (h1_hi_r, merged_lo_r), SEQ)
            pe.wait_ge(sem("squares"), 5)
            column_sums("ssq2", sq, SEQ)

            pe.wait_ge(sem("squares"), 6)
            f = begin("ssq3")
            for k in range(KD):
                last = nc.tensor.matmul(f.bank[:, 0:LEN], ones, sq_all[:, k, :], start=k == 0, stop=k == KD - 1)
            end(f, last)
            hn_all = hn_hi_r, hn_lo_r
            hn_x = [m[:, :, META:] for m in hn_all]
            project_T([f"fin{g}" for g in range(4)], FIN, hn_all, LEN, per=1, ready=KD)
            pe.wait_ge(sem("second_in"), 16 * 5)
            pe.wait_ge(sem("normed"), 2 * KD + 1)
            f = begin("ab")
            for t, (a, n) in enumerate(((0, META), (META, P), (META + P, P))):
                for k in range(KD):
                    last = matmul3(f.bank[0:n, t * 32:(t + 1) * 32], [m[:, k, a:a + n] for m in hn_all],
                                   (w_ab_hi_r[:, k, :], w_ab_lo_r[:, k, :]), k == 0, k == KD - 1)
            end(f, last)
            for g in range(4):
                pe.wait_ge(sem("f_T"), g + 1)
                f = begin(f"fa{g}")
                for t in range(TT):
                    a = META + t * P
                    last = nc.tensor.matmul(f.bank[:, t * 2 * P:(t + 1) * 2 * P], f_T[:, g, a:a + P], dft_d, start=True, stop=True)
                end(f, last)
            for i in range(2):
                f = begin(f"fm{i}")
                for j in range(2):
                    last = nc.tensor.matmul(f.bank[0:META, j * 2 * P:(j + 1) * 2 * P], f_T[:, 2 * i + j, 0:META], dft_d,
                                            start=True, stop=True)
                end(f, last)
            project_T([f"k{h}" for h in range(4)], K0, hn_all, LEN, per=1)
            pe.wait_ge(sem("fa"), 6)
            for i in range(2):
                f = begin(f"yf{i}")
                for j in range(2):
                    g = 2 * i + j
                    o = f.bank[:, j * SEQ:(j + 1) * SEQ]
                    for part in range(2):
                        c = part * SEQ
                        d = slice(part * P, (part + 1) * P)
                        nc.tensor.matmul(o, fa0[0:META, g, d], dft_l[0:META, 0, c:c + SEQ], start=part == 0, stop=False)
                        for t in range(TT):
                            last = nc.tensor.matmul(o, fa[:, t, g, d], dft_l[:, 1 + t, c:c + SEQ], start=False,
                                                    stop=part == 1 and t == TT - 1)
                end(f, last)
            pe.wait_ge(sem("gl"), 2)
            f = begin("gsum")
            for t in range(3):
                n = META if t == 0 else P
                for d, m in ((0, LE), (1, GE)):
                    last = nc.tensor.matmul(f.bank[0:n, t * 32 + 8 * d:t * 32 + 8 * d + 8], omask(m)[0:n, 0:n],
                                            gl[0:n, t, 8 * d:8 * d + 8], start=True, stop=True)
                last = nc.tensor.matmul(f.bank[0:n, t * 32 + 16:t * 32 + 32], ones[0:n, 0:n], gl[0:n, t, :], start=True, stop=True)
            end(f, last)
            project_T([f"v{h}" for h in range(4)], V0, hn_all, LEN, per=1)
            pe.wait_ge(sem("normed"), 2 * KD + 2)
            project_T([f"wf{j}" for j in range(4)], WF, (yf_hi_r, yf_lo_r), SEQ, stride=D, kk=4, pool=WK)

            def norms(kind, half, src_sem, n):
                pe.wait_ge(sem("sqn"), src_sem)
                for h in range(4):
                    f = begin(f"n{kind}{half}{h}")
                    last = nc.tensor.matmul(f.bank[:, 0:n], ones, sq2[:, h, 0:n], start=True, stop=True)
                    end(f, last)

            def to_tokens(kind, half, src, ready):
                pe.wait_ge(sem(f"{kind}_done"), ready)
                for t in (1, 2, 0):
                    n, a = (META, 0) if t == 0 else (P, META + (t - 1) * P)
                    f = begin(f"{kind}tr{half}{t}")
                    for h in range(4):
                        last = nc.tensor.transpose(f.bank[0:n, h * P:(h + 1) * P], src(h)[:, a:a + n], ident)
                    end(f, last)

            for j in range(2):
                project_T([f"gf{2 * j}", f"gf{2 * j + 1}"], GF + j, hn_x, SEQ)
            norms("k", 0, 1, LEN)
            project_T([f"q{h}" for h in range(4)], Q0, hn_all, LEN, per=1)
            to_tokens("k", 0, lambda h: kT[:, h, :], 1)
            to_tokens("v", 0, lambda h: v_T[0][:, h, :], 1)
            project_T([f"k{h + 4}" for h in range(4)], K1, hn_all, LEN, per=1)
            norms("q", 0, 2, SEQ)
            project_T([f"v{h + 4}" for h in range(4)], V1, hn_all, LEN, per=1)
            norms("k", 1, 3, LEN)
            project_T([f"q{h + 4}" for h in range(4)], Q1, hn_all, LEN, per=1)
            to_tokens("k", 1, lambda h: kT[:, h + 4, :], 2)
            to_tokens("v", 1, lambda h: v_T[1][:, h, :], 2)
            norms("q", 1, 4, SEQ)

            def project_whole(names, b, x, n, pool=PJ):
                pe.wait_ge(sem(f"slot{(b - ZB) % SLOTS}_in"), whole_in(b - ZB))
                w = ring[(b - ZB) % SLOTS]
                for i, name in enumerate(names):
                    f = begin(name, pool, f"block{b}")
                    for j in range(2):
                        for k in range(KD):
                            c = k * W1 + (2 * i + j) * P
                            last = nc.tensor.matmul(f.bank[:, j * n:(j + 1) * n], w[:, c:c + P], x[:, k, :],
                                                    start=k == 0, stop=k == KD - 1)
                    end(f, last)

            def prepare(l):
                n, w = l.n, work(l)
                g = omask(upto(l))
                f = begin(f"row{l.key}")
                for i, h in enumerate(l.hs):
                    j = l.j + h
                    last = nc.tensor.matmul(f.bank[:, i * n:(i + 1) * n], gl[0:n, l.tile, j:j + 1].to_broadcast([n, P]),
                                            g[0:n, 0:n], start=True, stop=True)
                end(f, last)
                f = begin(f"kk{l.key}")
                for i, h in enumerate(l.hs):
                    k = kT[:, h, l.at:l.at + n]
                    last = nc.tensor.matmul(f.bank[0:n, i * n:(i + 1) * n], k, k, start=True, stop=True)
                end(f, last)
                if l.tile:
                    f = begin(f"kq{l.key}")
                    for i, h in enumerate(l.hs):
                        last = nc.tensor.matmul(f.bank[:, i * n:(i + 1) * n], kT[:, h, l.at:l.at + n],
                                                qT[:, h, l.at - META:l.at - META + n], start=True, stop=True)
                    end(f, last)

            def level(l, v):
                n, w = l.n, work(l)
                am = w.am[v % 2]
                pe.wait_ge(sem(f"am{l.i}"), am_count[l.i] + v + 1)
                if v:
                    pe.wait_ge(sem(f"tt{l.i}"), am_count[l.i] + v)
                f = begin(f"z{l.key}{v}")
                for i in range(len(l.hs)):
                    last = nc.tensor.matmul(f.bank[0:n, i * n:(i + 1) * n], am[0:n, i, 0:n],
                                            ident[0:n, 0:n] if v == 0 else w.tt[0:n, i, 0:n], start=True, stop=True)
                end(f, last)

            def level_end(l, v):
                n, w = l.n, work(l)
                pe.wait_ge(sem(f"z{l.i}"), z_count[l.i] + v)
                pe.wait_ge(sem(f"t{l.i}"), z_count[l.i] + v)
                f = begin(f"yt{l.key}{v}")
                for i in range(len(l.hs)):
                    last = nc.tensor.matmul(f.bank[0:n, i * n:(i + 1) * n], w.t[0:n, i, 0:n], w.z[0:n, i, 0:n], start=True, stop=True)
                end(f, last)
                if v < l.levels - 1:
                    f = begin(f"y{l.key}{v}")
                    for i in range(len(l.hs)):
                        last = nc.tensor.matmul(f.bank[0:n, i * n:(i + 1) * n], w.z[0:n, i, 0:n], w.t[0:n, i, 0:n], start=True, stop=True)
                    end(f, last)

            def step_keys(l):
                pe.wait_ge(sem(f"s_{l.d}"), l.s_before)
                f = begin(f"r{l.key}", PJ)
                for i, h in enumerate(l.hs):
                    last = nc.tensor.matmul(f.bank[:, i * P:(i + 1) * P], kT[:, h, l.at:l.at + P], state[l.d][:, h * P:(h + 1) * P],
                                            start=True, stop=True)
                end(f, last)

            def step_values(l):
                n, w = l.n, work(l)
                x = (lambda i: v_meta[0:n, i * P:(i + 1) * P]) if l.tile == 0 else (lambda i: w.x[:, i, :])
                pe.wait_ge(sem(f"tt{l.i}"), tt_end[l.key])
                if l.tile:
                    pe.wait_ge(sem(f"xk{l.i}"), l.r + 1)
                for part in range(len(l.hs) // 4):
                    f = begin(f"vn{l.key}{part}", PJ)
                    for i in range(4):
                        c = 4 * part + i
                        last = nc.tensor.matmul(f.bank[0:n, i * P:(i + 1) * P], w.tt[0:n, c, 0:n], x(c), start=True, stop=True)
                    end(f, last)

            def step_state(l):
                n, w = l.n, work(l)
                k = k_meta if l.tile == 0 else k_tok[:, l.tile - 1, :]
                for part in range(len(l.hs) // 4):
                    pe.wait_ge(sem(f"vd{l.i}"), l.r + 1 + part)
                    f = begin(f"ds{l.key}{part}", PJ)
                    for i in range(4):
                        h = l.hs[4 * part + i]
                        v = x_meta[0:n, h * P:(h + 1) * P] if l.tile == 0 else w.z2[:, i, :]
                        last = nc.tensor.matmul(f.bank[:, i * P:(i + 1) * P], k[0:n, h * P:(h + 1) * P], v, start=True, stop=True)
                    end(f, last)

            def step_out(l):
                w = work(l)
                pe.wait_ge(sem(f"vn{l.i}"), l.r + 1)
                pe.wait_ge(sem(f"q{l.i}"), 2 * l.r + 2)
                f = begin(f"o{l.key}", PJ)
                for i, h in enumerate(l.hs):
                    o = f.bank[:, i * P:(i + 1) * P]
                    nc.tensor.matmul(o, state[l.d][:, h * P:(h + 1) * P], w.qd[:, i, :], start=True, stop=False)
                    last = nc.tensor.matmul(o, w.x[:, i, :], w.qk[:, i, :], start=False, stop=True)
                end(f, last)

            am_count, z_count = [0, 0, 0], [0, 0, 0]
            pe.wait_ge(sem("k_done"), 2)
            pe.wait_ge(sem("q_done"), 2)
            pe.wait_ge(sem("to_tok"), 12)
            for r, lanes in enumerate(ROUNDS):
                now = ([meta] if r == 0 else []) + lanes
                before = ROUNDS[r - 1] if r else []
                for l in now:
                    prepare(l)
                for v in range(7):
                    for l in now:
                        if v < l.levels:
                            level(l, v)
                    if v == 1:
                        for l in before: step_keys(l)
                    if v == 2:
                        for l in before: step_values(l)
                    if v == 4:
                        for l in before: step_out(l)
                    if v == 5 and r < 3:
                        for l in before: step_state(l)
                    if v:
                        for l in now:
                            if v < l.levels:
                                level_end(l, v)
                    if r == 0 and v == 5:
                        step_values(meta)
                    if r == 0 and v == 6:
                        step_state(meta)
                for l in now:
                    am_count[l.i] += l.levels
                    z_count[l.i] += l.levels - 1
            for step in (step_keys, step_values, step_out):
                for l in ROUNDS[-1]:
                    step(l)
            pe.wait_ge(sem("o_sq"), 4)
            for i in range(4):
                f = begin(f"no{i}")
                for j in range(2):
                    last = nc.tensor.matmul(f.bank[:, j * SEQ:(j + 1) * SEQ], ones, o_sq[:, 2 * i + j, :], start=True, stop=True)
                end(f, last)
            for j in range(2):
                project_whole([f"zz{2 * j}", f"zz{2 * j + 1}"], ZB + j, hn[:, :, META:], SEQ)
            for j in range(2):
                project_whole([f"gd{2 * j}", f"gd{2 * j + 1}"], GD + 2 * j, hn[:, :, META:], SEQ)
                pe.wait_ge(sem("y_delta"), 4)
                project_whole([f"wd{2 * j}", f"wd{2 * j + 1}"], WD + 2 * j, o_T, SEQ, pool=WK)
            pe.wait_ge(sem("merged2"), 4)
            for j in range(2):
                project_whole([f"wp{2 * j}", f"wp{2 * j + 1}"], WO2 + j, y_four, SEQ)

            pe.wait_ge(sem("squares"), 10)
            column_sums("ssq4", o_sq, SEQ)
            pe.wait_ge(sem("normed"), 3 * KD + 2)
            pe.wait_ge(sem("router_in"), 16)
            f = begin("router")
            for t in range(TT):
                for k in range(KD):
                    last = nc.tensor.matmul(f.bank[:, t * 72:(t + 1) * 72], m_T[:, k, t * P:(t + 1) * P], w_router[:, k, :],
                                            start=k == 0, stop=k == KD - 1)
            end(f, last)
            for t in range(TT):
                for i in range(2):
                    f = begin(f"m{t}{i}", PJ)
                    for j in range(4):
                        last = nc.tensor.transpose(f.bank[:, j * P:(j + 1) * P], m_T[:, 4 * i + j, t * P:(t + 1) * P], ident)
                    end(f, last)
            pe.wait_ge(sem("chosen"), TT)
            f = begin("ranks")
            nc.tensor.matmul(f.bank[:, 0:64], omask(LE), chosen[:, 0, :], start=True, stop=True)
            nc.tensor.matmul(f.bank[:, 64:128], omask(LE), chosen[:, 1, :], start=True, stop=False)
            nc.tensor.matmul(f.bank[:, 64:128], ones, chosen[:, 0, :], start=False, stop=True)
            nc.tensor.matmul(f.bank[:, 128:192], ones, chosen[:, 0, :], start=True, stop=False)
            end(f, nc.tensor.matmul(f.bank[:, 128:192], ones, chosen[:, 1, :], start=False, stop=True))

            for b in range(8):
                if uses[b]:
                    pe.wait_ge(free[b], uses[b])
            pe.wait_ge(sem("m_tok"), 4)
            pe.sem_inc(sem("down"), 2)
            n_passes = read_passes(nc.tensor, pe)
            with pe.Fori(0, n_passes) as p:
                with pe.Fori(0, N_GROUPS // 2) as pair:
                  for u in range(2):
                    q = 2 * pair + u
                    it = p * N_GROUPS + q
                    pe.wait_ge(sem("picks"), it + 1)
                    pe.wait_ge(sem("added"), it * 4 + 4)
                    for k in range(KD):
                        o = banks[k // 4][:, (k % 4) * P:(k % 4 + 1) * P]
                        for t in range(TT):
                            last = nc.tensor.matmul(o, m_tok[:, t, k * P:(k + 1) * P], pick_m[:, t, :], start=t == 0, stop=t == TT - 1)
                        if k % 4 == 3:
                            last.then_inc(sem("gathered"), 1)
                    for t in range(TT):
                        last = nc.tensor.transpose(banks[2][:, t * P:(t + 1) * P], pick_w[:, t, :], ident)
                    last.then_inc(sem("gathered"), 1)
                    pe.wait_ge(sem("xg"), 2 * it + 2)
                    for j in range(PER):
                        if u == 0:
                            pe.wait_ge(sem(f"slot{(N_BLOCKS - ZB + j) % SLOTS}_in"), gate_up_in[j] + 8 * it)
                    if u == 1:
                        pe.wait_ge(sem("odd_in"), 64 * (p * (N_GROUPS // 2) + pair) + 64)
                    for k in range(KD):
                        for j in range(PER):
                            last = nc.tensor.matmul(banks[3][j * CAP:(j + 1) * CAP, :], xg[:, k, j * CAP:(j + 1) * CAP],
                                                    gate_up[u][j][:, k * 2 * FE:(k + 1) * 2 * FE], start=k == 0, stop=k == KD - 1)
                    last.then_inc(sem("gate_up"), 1)
                    pe.wait_ge(sem("hid"), it + 2)
                    for i in range(2):
                        last = nc.tensor.transpose(banks[4][:, i * P:(i + 1) * P], hid[:, i * P:(i + 1) * P], ident)
                    last.then_inc(sem("hid_turned"), 1)
                    pe.wait_ge(sem("hid_T"), it + 1)
                    pe.wait_ge(sem("down_in"), 32 * it + 32)
                    for half in range(2):
                        for i in range(2):
                            for j in range(PER):
                                c = (j % 2) * (BLOCK // 2) + i * D + half * 512
                                last = nc.tensor.matmul(banks[5 + half][j * CAP:(j + 1) * CAP, :], hid_T[:, i, j * CAP:(j + 1) * CAP],
                                                        down[j // 2][:, c:c + 512], start=i == 0, stop=i == 1)
                        last.then_inc(sem("down"), 1)
                    pe.wait_ge(sem("yb"), 2 * it + 2)
                    pe.wait_ge(sem("pick_T"), it + 2)
                    for i, b in enumerate((0, 1, 2, 7)):
                        for j in range(2):
                            c = (2 * i + j) * P
                            last = nc.tensor.matmul(banks[b][:, j * SEQ:(j + 1) * SEQ], yb[:, c:c + P], pick_T, start=True, stop=True)
                        last.then_inc(sem("scattered"), 1)
            pe.wait_ge(sem("squares"), 14)
            for k in range(KD):
                last = nc.tensor.matmul(banks[3][:, 0:SEQ], ones, o_sq5[:, k, :], start=k == 0, stop=k == KD - 1)
            last.then_inc(sem("ssq5"), 1)

        @block.scalar
        def _(act):
            halves = [0]

            def lead(n):
                for _ in range(n):
                    h = halves[0]
                    halves[0] += 1
                    if h >= SPLIT:
                        before = readers[h - SPLIT]
                        act.wait_ge(full[before.b], before.n + 1)
                    for q in (2 * h, 2 * h + 1):
                        act.wait_ge(sem(f"slot{q % RAW}_in"), 16 * (q // RAW + 1))
                        nc.scalar.activation(w_hi[h % SPLIT][:, quarter(q)], raw[q % RAW], ACT.Copy).then_inc(sem("w_hi"), 1)

            def lead_for(name):
                while halves[0] < N_HALVES and readers[halves[0] - SPLIT].order < fills[name].order:
                    lead(1)

            def got(name):
                f = fills[name]
                lead_for(name)
                act.wait_ge(full[f.b], f.n + 1)
                return f

            chain = [0]

            def link(ins):
                chain[0] += 1
                ins.then_inc(sem("act_chain"), 1)
                act.wait_ge(sem("act_chain"), chain[0])

            def evacuate(name, out, done, func=ACT.Copy, scale=1.0):
                f = got(name)
                link(nc.scalar.activation(out, two(f.bank), func, scale=scale))
                act.sem_inc(free[f.b], 1)
                act.sem_inc(sem(done), 1)

            act.wait_ge(sem("res_in"), 16)
            sq = h1_lo
            nc.scalar.activation(sq, res[:, :, META:], ACT.Square).then_inc(sem("squares"), 1)
            act.wait_ge(sem("variance"), 1)
            nc.scalar.activation(rms, rms, ACT.Sqrt).then_inc(sem("deviation"), 1)
            lead(SPLIT)
            f = got("c")
            for t in range(TT):
                last = nc.scalar.activation(gates[:, t, 0:P], f.bank[:, t * SEQ:t * SEQ + P], ACT.Square,
                                            accum_out=css[:, t:t + 1])
            last.then_inc(sem("css"), 1)
            f = got("f")
            act.wait_ge(sem("cols_in"), 16)
            link(nc.scalar.activation(ff[0:NH, 0, :], f.bank[0:NH, 0:SEQ], ACT.Identity, bias=col("b_f")[0:NH]))
            act.sem_inc(free[f.b], 1)
            act.wait_ge(sem("variance"), 2)
            nc.scalar.activation(css, css, ACT.Sqrt).then_inc(sem("deviation"), 1)
            evacuate("qi", qi, "qiki")
            link(nc.scalar.activation(ff[0:NH, 1, :], ff[0:NH, 0, :], ACT.Abs))
            link(nc.scalar.activation(ff[0:NH, 1, :], ff[0:NH, 1, :], ACT.Exp, scale=-1.0))
            nc.scalar.activation(ff[0:NH, 1, :], ff[0:NH, 1, :], ACT.Ln, bias=1.0).then_inc(sem("ln_f"), 1)
            evacuate("dq0", dq[:, 0:2, :], "dq", scale=P ** -0.5)
            evacuate("dq1", dq[:, 2:4, :], "dq", scale=P ** -0.5)
            for n, (t, odd) in enumerate(((0, 0), (0, 1), (1, 0), (1, 1))):
                f = got(f"dots{n}")
                dst = (relu0, relu1)[t][:, odd::2, :]
                m = P * (t + 1)
                link(nc.scalar.activation(dst, f.bank[:, 0:2 * m].rearrange("p (h k) -> p h k", h=2), ACT.Relu))
                act.sem_inc(free[f.b], 1)
                act.sem_inc(sem("relu"), 1)
            evacuate("dk0", dk[:, 0:2, :], "dk")
            evacuate("dk1", dk[:, 2:4, :], "dk")
            evacuate("qlat0", qlat[:, 0:2, :], "qlat", scale=P ** -0.5)
            evacuate("qlat1", qlat[:, 2:4, :], "qlat", scale=P ** -0.5)
            for t in range(TT):
                f = got(f"dv{t}")
                link(nc.scalar.activation(dv[:, t, :], f.bank[:, :], ACT.Copy))
                act.sem_inc(free[f.b], 1)
                act.sem_inc(sem("dv"), 1)

            def exps(a):
                for t in range(TT):
                    act.wait_ge(sem("soft_max"), t + 1 + (TT if a == "b" else 0))
                    for h in range(NH):
                        last = nc.scalar.activation(lg[a][t][:, h, :], lg[a][t][:, h, :], ACT.Exp,
                                                    bias=nmax[a][:, t * NH + h:t * NH + h + 1],
                                                    accum_out=psum[a][:, t * NH + h:t * NH + h + 1])
                    last.then_inc(sem("soft_exp"), 1)

            exps("f")
            lead_for("av1")
            act.wait_ge(sem("variance"), 3)
            nc.scalar.activation(lnsd, lnsd, ACT.Sqrt).then_inc(sem("deviation"), 1)
            evacuate("az0", y[0][:, 0:2, :], "az", func=ACT.Silu)
            evacuate("az1", y[0][:, 2:4, :], "az", func=ACT.Silu)
            evacuate("dz0", y[3][:, 0:2, :], "dz", func=ACT.Silu)
            evacuate("dz1", y[3][:, 2:4, :], "dz", func=ACT.Silu)
            exps("b")
            evacuate("bz0", y[1][:, 0:2, :], "bz", func=ACT.Silu)
            evacuate("bz1", y[1][:, 2:4, :], "bz", func=ACT.Silu)
            act.wait_ge(sem("cc"), 1)
            evacuate("cb0", cc[:, 0:2, :], "cb")
            evacuate("cb1", cc[:, 2:4, :], "cb")
            evacuate("cz0", y[2][:, 0:2, :], "cz", func=ACT.Silu)
            evacuate("cz1", y[2][:, 2:4, :], "cz", func=ACT.Silu)
            for i, n in enumerate(ORDER):
                for j in range(4):
                    if i > 0:
                        lead_for(f"br{ORDER[i - 1]}{j}")
                        act.wait_ge(sem("merged"), 4 * (i - 1) + j + 1)
                    evacuate(f"g{n}{j}", gates[:, 2 * j:2 * j + 2, :], "gate", func=ACT.Sigmoid)
            for j in range(4):
                lead_for(f"wo{j}")
                act.wait_ge(sem("x1"), j + 1)
                nc.scalar.activation(sq[:, 2 * j:2 * j + 2, :], res[:, 2 * j:2 * j + 2, META:], ACT.Square).then_inc(sem("squares"), 1)
            lead_for("ssq2")
            act.wait_ge(sem("variance"), 4)
            nc.scalar.activation(rms, rms, ACT.Sqrt).then_inc(sem("deviation"), 1)

            act.wait_ge(sem("final"), KD)
            nc.scalar.activation(sq_all, res, ACT.Square).then_inc(sem("squares"), 1)
            lead_for("ssq3")
            act.wait_ge(sem("variance"), 5)
            nc.scalar.activation(rms2, rms2, ACT.Sqrt).then_inc(sem("deviation"), 1)
            for g in range(4):
                f = got(f"fin{g}")
                link(nc.scalar.activation(f_T[:, g, :], f.bank[:, 0:LEN], ACT.Copy))
                act.sem_inc(free[f.b], 1)
                act.sem_inc(sem("f_T"), 1)
            regions = ((slice(0, META), slice(0, 1)), (slice(0, P), slice(1, 3)))
            lead_for("ab")
            act.wait_ge(sem("ab"), 1)
            for p, t in regions:
                link(nc.scalar.activation(gx[p, t], gl[p, t], ACT.Abs))
                link(nc.scalar.activation(gx[p, t], gx[p, t], ACT.Exp, scale=-1.0))
                link(nc.scalar.activation(gx[p, t], gx[p, t], ACT.Ln, bias=1.0))
            link(nc.scalar.activation(nea, rows[:, ROWS["a_log"][0]:ROWS["a_log"][1]], ACT.Exp))
            act.sem_inc(sem("soft"), 1)
            for g in range(4):
                f = got(f"fa{g}")
                link(nc.scalar.activation(fa[:, :, g, :], two(f.bank), ACT.Copy))
                act.sem_inc(free[f.b], 1)
                act.sem_inc(sem("fa"), 1)
            for i in range(2):
                f = got(f"fm{i}")
                link(nc.scalar.activation(fa0[0:META, 2 * i:2 * i + 2, :], two(f.bank)[0:META], ACT.Copy))
                act.sem_inc(free[f.b], 1)
                act.sem_inc(sem("fa"), 1)
            for p, t in regions:
                nc.scalar.activation(beta[p, t], beta[p, t], ACT.Sigmoid)

            def silu_sq(kind, half, dst, n, squares=True):
                for h in range(4):
                    lead_for(f"{kind}{4 * half + h}")
                    act.wait_ge(sem(f"conv_{kind}"), 4 * half + h + 1)
                    link(nc.scalar.activation(dst[:, h, 0:n], dst[:, h, 0:n], ACT.Silu))
                if squares:
                    link(nc.scalar.activation(sq2[:, :, 0:n], dst[:, :, 0:n], ACT.Square))
                    act.sem_inc(sem("sqn"), 1)

            def norm_sqrt(kind, half, n):
                lead_for(f"n{kind}{half}3")
                norm_sqrt.count += 1
                act.wait_ge(sem("ssn"), norm_sqrt.count)
                link(nc.scalar.activation(rn2[:, :, 0:n], rn2[:, :, 0:n], ACT.Sqrt))
                act.sem_inc(sem("sdn"), 1)
            norm_sqrt.count = 0

            def tokens(kind, half):
                dst, small = (k_tok, k_meta) if kind == "k" else (v_tok, v_meta)
                for t in (1, 2, 0):
                    f = got(f"{kind}tr{half}{t}")
                    o = small[0:META, half * 512:half * 512 + 512] if t == 0 else dst[:, t - 1, half * 512:half * 512 + 512]
                    link(nc.scalar.activation(o, f.bank[0:META if t == 0 else P, :], ACT.Copy))
                    act.sem_inc(free[f.b], 1)
                    act.sem_inc(sem("to_tok"), 1)

            for i in range(2):
                f = got(f"yf{i}")
                link(nc.scalar.activation(yf_T[:, 2 * i:2 * i + 2, :], two(f.bank), ACT.Copy))
                act.sem_inc(free[f.b], 1)
                act.sem_inc(sem("yf_T"), 1)
            lead_for("gsum")
            act.wait_ge(sem("gsum"), 1)
            for p, t in regions:
                link(nc.scalar.activation(edec[p, t], gsum[p, t, 0:16], ACT.Exp))
                link(nc.scalar.activation(krem[p, t], krem[p, t], ACT.Exp))
                link(nc.scalar.activation(eall[p, t], gsum[p, t, 16:32], ACT.Exp))
            act.sem_inc(sem("edec"), 1)
            for j in range(4):
                f = got(f"gf{j}")
                if j >= 2:
                    act.wait_ge(sem("y_four"), j - 1)
                link(nc.scalar.activation(gate2[:, j % 2], two(f.bank), ACT.Sigmoid))
                act.sem_inc(free[f.b], 1)
                act.sem_inc(sem("gate_f"), 1)
            lead_for("wf3")
            act.wait_ge(sem("y_four"), 4)
            silu_sq("k", 0, kT[:, 0:4], LEN)
            norm_sqrt("k", 0, LEN)
            silu_sq("v", 0, v_T[0], LEN, squares=False)
            act.sem_inc(sem("v_done"), 1)
            silu_sq("q", 0, qT[:, 0:4], SEQ)
            tokens("k", 0)
            tokens("v", 0)
            norm_sqrt("q", 0, SEQ)
            silu_sq("k", 1, kT[:, 4:8], LEN)
            norm_sqrt("k", 1, LEN)
            silu_sq("v", 1, v_T[1], LEN, squares=False)
            act.sem_inc(sem("v_done"), 1)
            silu_sq("q", 1, qT[:, 4:8], SEQ)
            tokens("k", 1)
            tokens("v", 1)
            norm_sqrt("q", 1, SEQ)

            def lane_exps(l):
                n, w = l.n, work(l)
                if l.tile:
                    f = got(f"row{l.key}")
                    act.wait_ge(sem(f"u{l.i}"), l.r + 1)
                    link(nc.scalar.activation(w.qd, heads_of(f, l), ACT.Exp))
                    act.sem_inc(free[f.b], 1)
                    act.sem_inc(sem(f"eg{l.i}"), 1)
                    link(nc.scalar.activation(w.qk, w.qk, ACT.Exp))
                else:
                    act.wait_ge(sem(f"u{l.i}"), l.r + 1)
                link(nc.scalar.activation(w.u[0:n, :, 0:n], w.u[0:n, :, 0:n], ACT.Exp, scale=-1.0))
                act.sem_inc(sem(f"d{l.i}"), 1)

            def copy_z(l, v):
                n, w = l.n, work(l)
                f = got(f"z{l.key}{v}")
                link(nc.scalar.activation(w.z[0:n, :, 0:n], heads_of(f, l), ACT.Copy))
                act.sem_inc(free[f.b], 1)
                act.sem_inc(sem(f"z{l.i}"), 1)

            def new_values(l):
                w = work(l)
                f = got(f"vn{l.key}0")
                link(nc.scalar.activation(w.x, heads_of(f, l), ACT.Copy))
                act.sem_inc(sem(f"vn{l.i}"), 1)

            for r, lanes in enumerate(ROUNDS):
                now = ([meta] if r == 0 else []) + lanes
                before = ROUNDS[r - 1] if r else []
                for l in now:
                    lane_exps(l)
                for v in range(7):
                    if v == 3:
                        for l in before: new_values(l)
                    if v:
                        for l in now:
                            if v < l.levels:
                                copy_z(l, v)
            for l in ROUNDS[-1]:
                new_values(l)
            for i in range(4):
                act.wait_ge(sem("o_b"), 2 if i < 2 else 4)
                link(nc.scalar.activation(o_sq[:, 2 * i:2 * i + 2, :], o_T[:, 2 * i:2 * i + 2, :], ACT.Square))
                act.sem_inc(sem("o_sq"), 1)
            for i in range(2):
                act.wait_ge(sem("ss_o"), 2 * i + 2)
                link(nc.scalar.activation(o_rn[:, 4 * i:4 * i + 4, :], o_rn[:, 4 * i:4 * i + 4, :], ACT.Sqrt))
                act.sem_inc(sem("sd_o"), 1)
            for j in range(4):
                f = got(f"zz{j}")
                link(nc.scalar.activation(z_g[:, j], two(f.bank), ACT.Silu))
                act.sem_inc(free[f.b], 1)
                act.sem_inc(sem("z_g"), 1)
            for j in range(4):
                f = got(f"gd{j}")
                act.wait_ge(sem("y_delta"), 4)
                link(nc.scalar.activation(z_g[:, j], two(f.bank), ACT.Sigmoid))
                act.sem_inc(free[f.b], 1)
                act.sem_inc(sem("z_g"), 1)

            for j in range(4):
                act.wait_ge(sem("h2"), j + 1)
                nc.scalar.activation(o_sq[:, 2 * j:2 * j + 2, :], res[:, 2 * j:2 * j + 2, META:], ACT.Square).then_inc(sem("squares"), 1)
            act.wait_ge(sem("variance"), 6)
            nc.scalar.activation(rms4, rms4, ACT.Sqrt).then_inc(sem("deviation"), 1)
            for t in range(TT):
                for i in range(2):
                    f = got(f"m{t}{i}")
                    link(nc.scalar.activation(m_tok[:, t, i * 512:(i + 1) * 512], f.bank[:, :], ACT.Copy))
                    act.sem_inc(free[f.b], 1)
                    act.sem_inc(sem("m_tok"), 1)
            for t in range(TT):
                act.wait_ge(sem("r_max"), t + 1)
                link(nc.scalar.activation(r_exp[:, t, 0:8], router[:, t, 0:8], ACT.Exp, bias=r_nmax[:, 2 * t:2 * t + 1],
                                          accum_out=r_sum[:, 2 * t:2 * t + 1]))
                nc.scalar.activation(r_exp[:, t, 8:72], router[:, t, 8:72], ACT.Exp, bias=r_nmax[:, 2 * t + 1:2 * t + 2],
                                     accum_out=r_sum[:, 2 * t + 1:2 * t + 2])
                link(nc.scalar.activation(r_second[:, t:t + 1], r_second[:, t:t + 1], ACT.Exp, bias=r_nmax[:, 2 * t + 1:2 * t + 2]))
                act.sem_inc(sem("r_exp"), 1)

            n_passes = read_passes(nc.scalar, act)
            with act.Fori(0, n_passes) as p:
                with act.Fori(0, N_GROUPS // 2) as pair:
                  for u in range(2):
                    q = 2 * pair + u
                    it = p * N_GROUPS + q
                    act.wait_ge(sem("gathered"), 3 * it + 1)
                    nc.scalar.activation(xg[:, 0:4, :].rearrange("p k s -> p (k s)"), banks[0][:, :], ACT.Copy).then_inc(sem("xg"), 1)
                    act.wait_ge(sem("gate_up"), it + 1)
                    act.wait_ge(sem("hid"), it + 1)
                    nc.scalar.activation(act_g, banks[3][:, 0:FE], ACT.Silu).then_inc(sem("silu"), 1)
                    act.wait_ge(sem("hid_turned"), it + 1)
                    nc.scalar.activation(hid_T.rearrange("p f s -> p (f s)"), banks[4][:, 0:2 * P], ACT.Copy).then_inc(sem("hid_T"), 1)
                    act.wait_ge(sem("down"), 2 * it + 3)
                    nc.scalar.activation(yb[:, 0:512], banks[5][:, :], ACT.Copy).then_inc(sem("yb"), 1)
            for j in range(4):
                act.wait_ge(sem("moe_done"), 1)
                nc.scalar.activation(o_sq5[:, 2 * j:2 * j + 2, :], res[:, 2 * j:2 * j + 2, META:], ACT.Square).then_inc(sem("squares"), 1)
            act.wait_ge(sem("variance"), 7)
            nc.scalar.activation(rms4, rms4, ACT.Sqrt).then_inc(sem("deviation"), 1)

        @block.vector
        def _(dve):
            def got(name):
                f = fills[name]
                dve.wait_ge(full[f.b], f.n + 1)
                return f

            chain = [0]

            def link(ins):
                chain[0] += 1
                ins.then_inc(sem("dve_chain"), 1)
                dve.wait_ge(sem("dve_chain"), chain[0])

            def evacuate(name, out, done=None):
                f = got(name)
                link(nc.vector.tensor_copy(out, two(f.bank)))
                dve.sem_inc(free[f.b], 1)
                if done:
                    dve.sem_inc(sem(done), 1)

            def rms_rows(name, i, n):
                f = got(name)
                nc.vector.tensor_scalar(rms[:, 0:n], f.bank[:, 0:n], 1.0 / D, EPS, ALU.mult, ALU.add).then_inc(sem("variance"), 1)
                dve.wait_ge(sem("deviation"), i)
                link(nc.vector.reciprocal(rms[:, 0:n], rms[:, 0:n]))
                dve.sem_inc(free[f.b], 1)

            def split(x, hi, lo):
                link(nc.vector.tensor_copy(hi, x))
                link(nc.vector.tensor_tensor(lo, x, hi.bitcast(f32), ALU.subtract))

            def split_y(n, i):
                js = slice(2 * i, 2 * i + 2)
                split(y[n][:, js], y_hi[n][:, js], y_lo[n][:, js])

            dve.wait_ge(sem("cols_in"), 16)
            rms_rows("ssq1", 1, SEQ)
            dve.wait_ge(sem("res_in"), 16)
            for k in range(KD):
                nc.vector.scalar_tensor_tensor(h1_hi_r[:, k, :], res[:, k, META:], col("norm_g", k), rms, ALU.mult, ALU.mult)
                link(nc.vector.scalar_tensor_tensor(h1_lo[:, k, :], res[:, k, META:], col("norm_g", k), rms, ALU.mult, ALU.mult))
                nc.vector.tensor_tensor(h1_lo_r[:, k, :], h1_lo[:, k, :], h1_hi_r[:, k, :].bitcast(f32), ALU.subtract).then_inc(sem("normed"), 1)
            f = got("c")
            dve.wait_ge(sem("css"), 1)
            link(nc.vector.tensor_scalar(css, css, 1.0 / P, EPS, ALU.mult, ALU.add))
            dve.sem_inc(sem("variance"), 1)
            for t in range(TT):
                nc.vector.tensor_scalar(wi[:, t * NH:(t + 1) * NH], f.bank[:, t * SEQ + P:t * SEQ + P + NH],
                                        NH ** -0.5 * IDX ** -0.5, None, ALU.mult)
            dve.wait_ge(sem("deviation"), 2)
            link(nc.vector.reciprocal(css, css))
            for t in range(TT):
                link(nc.vector.tensor_scalar(cn[:, t, :], f.bank[:, t * SEQ:t * SEQ + P], css[:, t:t + 1], None, ALU.mult))
                dve.sem_inc(sem("cn"), 1)
            dve.sem_inc(free[f.b], 1)
            f = got("ki")
            link(nc.vector.tensor_copy(ki[0:IDX], f.bank[0:IDX, 0:SEQ]))
            dve.sem_inc(free[f.b], 1)
            dve.sem_inc(sem("cn"), 1)
            evacuate("bq0", bq[:, 0:2, :], "bq")
            evacuate("bq1", bq[:, 2:4, :], "bq")
            f = got("ki2")
            link(nc.vector.tensor_copy(ki[IDX:], f.bank[IDX:, 0:SEQ]))
            dve.sem_inc(free[f.b], 1)
            dve.sem_inc(sem("qiki"), 1)
            dve.wait_ge(sem("ln_f"), 1)
            link(nc.vector.scalar_tensor_tensor(ff[0:NH, 2, :], ff[0:NH, 0, :], 0.0, ff[0:NH, 1, :], ALU.min, ALU.subtract))
            link(nc.vector.memset(ff[0:NH, 1, :], 1.0))
            nc.vector.tensor_tensor_scan(ff[0:NH, 3, :], ff[0:NH, 1, :], ff[0:NH, 2, :], 0.0, ALU.mult, ALU.add).then_inc(sem("forget"), 1)
            dve.wait_ge(sem("forget"), 1)
            nc.vector.tensor_scalar(ff[0:NH, 4, :], ff[0:NH, 3, :], -1.0, None, ALU.mult).then_inc(sem("forget"), 1)
            f = got("cT")
            link(nc.vector.tensor_scalar(cT, f.bank[:, 0:SEQ], col("kv_g"), None, ALU.mult))
            dve.sem_inc(free[f.b], 1)
            dve.sem_inc(sem("cT"), 1)
            dve.wait_ge(sem("consts_in"), 16)

            def top_scores(t):
                m = P * (t + 1)
                s, r = score[t], (relu0, relu1)[t]
                causal = mask[:, SEQ - m:SEQ]
                dve.wait_ge(sem("relu"), 2 + 2 * t)
                for h in range(NH):
                    link(nc.vector.scalar_tensor_tensor(s, r[:, h, :], wi[:, t * NH + h:t * NH + h + 1],
                                                        causal if h == 0 else s, ALU.mult, ALU.add))
                for _ in range(TOPK // 8):
                    link(nc.vector.max(best, s))
                    link(nc.vector.match_replace(s, best, s, -3.4e38))
                link(nc.vector.tensor_scalar(s, s, -3.2e38, -1e30, ALU.is_gt, ALU.mult))
                link(nc.vector.tensor_tensor(s, s, causal, ALU.add))

            def softmax_in(a, add):
                for t in range(TT):
                    m = P * (t + 1)
                    for n, hs in ((0, (0, 4)),) if t == 0 else ((1, (0, 2)), (2, (2, 4))):
                        f = got(f"{a}l{n}")
                        k = hs[1] - hs[0]
                        link(nc.vector.tensor_tensor(lg[a][t][:, hs[0]:hs[1], :], f.bank[:, :].rearrange("p (h k) -> p h k", h=k),
                                                     add(t).unsqueeze(1).to_broadcast([P, k, m]), ALU.add))
                        dve.sem_inc(free[f.b], 1)
                    nc.vector.tensor_reduce(nmax[a][:, t * NH:(t + 1) * NH], lg[a][t], AX.X, ALU.max,
                                            negate=True).then_inc(sem("soft_max"), 1)

            def softmax_out(a):
                for t in range(TT):
                    m = P * (t + 1)
                    dve.wait_ge(sem("soft_exp"), t + 1 + (TT if a == "b" else 0))
                    ps = psum[a][:, t * NH:(t + 1) * NH]
                    link(nc.vector.reciprocal(ps, ps))
                    nc.vector.tensor_tensor(lg[a][t], lg[a][t], ps.unsqueeze(2).to_broadcast([P, NH, m]),
                                            ALU.mult).then_inc(sem("soft_p"), 1)

            def weights_T(a):
                for n in range(3):
                    f = got(f"{a}pT{n}")
                    link(nc.vector.tensor_copy(pT[:, n, :, :].rearrange("p h q -> p (h q)"), f.bank[:, :]))
                    dve.sem_inc(free[f.b], 1)
                    dve.sem_inc(sem("soft_pT"), 1)

            top_scores(0)
            softmax_in("f", lambda t: mask[:, SEQ - P * (t + 1):SEQ])
            dve.wait_ge(sem("small_in"), 16 * 6)
            for t in range(TT):
                f = got(f"av{t}")
                link(nc.vector.bn_stats(bns, f.bank[:, :]))
                link(nc.vector.bn_aggr(mv[:, 2 * t:2 * t + 2], bns))
                link(nc.vector.tensor_scalar(av[:, t, :], f.bank[:, :], mv[:, 2 * t:2 * t + 1], None, ALU.subtract))
                dve.sem_inc(free[f.b], 1)
                link(nc.vector.tensor_scalar(lnsd[:, t:t + 1], mv[:, 2 * t + 1:2 * t + 2], EPS, None, ALU.add))
            softmax_out("f")
            dve.sem_inc(sem("variance"), 1)
            dve.wait_ge(sem("deviation"), 3)
            link(nc.vector.reciprocal(lnsd, lnsd))
            for t in range(TT):
                link(nc.vector.scalar_tensor_tensor(av[:, t, :], av[:, t, :], lnsd[:, t:t + 1], ln_rows[:, 0:W1], ALU.mult, ALU.mult))
                nc.vector.tensor_tensor(av[:, t, :], av[:, t, :], ln_rows[:, W1:], ALU.add).then_inc(sem("av"), 1)
            evacuate("au0", cpad[:, 0:2, 0:SEQ])
            evacuate("au1", cpad[:, 2:4, 0:SEQ])
            weights_T("f")

            def times(name, i, into, silu, done, other=None):
                f = got(name)
                dve.wait_ge(sem(silu), i + 1)
                if other is not None:
                    link(nc.vector.tensor_tensor(into, into, other, ALU.mult))
                link(nc.vector.tensor_tensor(into, into, two(f.bank), ALU.mult))
                dve.sem_inc(free[f.b], 1)
                split_y(int(done[1]), i)
                dve.sem_inc(sem(done), 1)

            top_scores(1)
            softmax_fo = [(f"fo{i}", i) for i in range(2)]
            for i in range(2):
                times(f"mx{i}", i, y[0][:, 2 * i:2 * i + 2, :], "az", "y0", cpad[:, 2 * i:2 * i + 2, 0:SEQ])
            for name, i in softmax_fo:
                times(name, i, y[3][:, 2 * i:2 * i + 2, :], "dz", "y3")
            softmax_in("b", lambda t: score[t])
            softmax_out("b")
            link(nc.vector.memset(cpad[:, :, 0:2], 0.0))
            dve.sem_inc(sem("cc"), 1)
            evacuate("cc0", cv[:, 0:2, :])
            evacuate("cc1", cv[:, 2:4, :])
            weights_T("b")
            for i in range(2):
                f = got(f"cx{i}")
                link(nc.vector.tensor_tensor(cpad[:, 2 * i:2 * i + 2, 2:], two(f.bank), cv[:, 2 * i:2 * i + 2, :], ALU.mult))
                dve.sem_inc(free[f.b], 1)
            for j in range(CW):
                link(nc.vector.tensor_scalar(cv[:, j, :], cpad[:, j, 0:SEQ], col("conv_w", j), None, ALU.mult))
            for tap in (1, 2):
                for j in range(CW):
                    last = nc.vector.scalar_tensor_tensor(cv[:, j, :], cpad[:, j, tap:tap + SEQ], col("conv_w", tap * CW + j),
                                                          cv[:, j, :], ALU.mult, ALU.add)
                link(last)
            for t in range(TT):
                f = got(f"ol{t}")
                link(nc.vector.tensor_scalar(olat[:, :, t * P:(t + 1) * P], f.bank[:, :].rearrange("p (h q) -> p h q", h=NH),
                                             col("kv_g"), None, ALU.mult))
                dve.sem_inc(free[f.b], 1)
                dve.sem_inc(sem("olat"), 1)
            dve.wait_ge(sem("cb"), 2)
            link(nc.vector.tensor_tensor(cv, cv, cc, ALU.mult))
            dve.wait_ge(sem("cz"), 2)
            link(nc.vector.tensor_tensor(y[2], y[2], cv, ALU.mult))
            for i in range(2):
                split_y(2, i)
            dve.sem_inc(sem("y2"), 2)
            for i in range(2):
                times(f"bo{i}", i, y[1][:, 2 * i:2 * i + 2, :], "bz", "y1")
            for i, n in enumerate(ORDER):
                for j in range(4):
                    f = got(f"br{n}{j}")
                    dve.wait_ge(sem("gate"), 4 * i + j + 1)
                    m = merged[:, 2 * j:2 * j + 2, :]
                    g = gates[:, 2 * j:2 * j + 2, :]
                    if i == 0:
                        link(nc.vector.tensor_tensor(m, two(f.bank), g, ALU.mult))
                    else:
                        link(nc.vector.tensor_tensor(g, two(f.bank), g, ALU.mult))
                        link(nc.vector.tensor_tensor(m, m, g, ALU.add))
                    dve.sem_inc(free[f.b], 1)
                    if i == 3:
                        js = slice(2 * j, 2 * j + 2)
                        split(merged[:, js], h1_hi_r[:, js], merged_lo_r[:, js])
                    dve.sem_inc(sem("merged"), 1)
            for j in range(4):
                f = got(f"wo{j}")
                r = res[:, 2 * j:2 * j + 2, META:]
                link(nc.vector.tensor_tensor(r, r, two(f.bank), ALU.add))
                dve.sem_inc(free[f.b], 1)
                dve.sem_inc(sem("x1"), 1)
            rms_rows("ssq2", 4, SEQ)
            for k in range(KD):
                nc.vector.scalar_tensor_tensor(res[:, k, META:], res[:, k, META:], col("final_g", k), rms, ALU.mult,
                                               ALU.mult).then_inc(sem("final"), 1)

            f = got("ssq3")
            nc.vector.tensor_scalar(rms2, f.bank[:, 0:LEN], 1.0 / D, EPS, ALU.mult, ALU.add).then_inc(sem("variance"), 1)
            dve.wait_ge(sem("deviation"), 5)
            link(nc.vector.reciprocal(rms2, rms2))
            dve.sem_inc(free[f.b], 1)
            for k in range(KD):
                nc.vector.scalar_tensor_tensor(hn_hi_r[:, k, :], res[:, k, :], col("norm1_g", k), rms2, ALU.mult, ALU.mult)
                link(nc.vector.scalar_tensor_tensor(hn_lo[:, k, :], res[:, k, :], col("norm1_g", k), rms2, ALU.mult, ALU.mult))
                nc.vector.tensor_tensor(hn_lo_r[:, k, :], hn_lo[:, k, :], hn_hi_r[:, k, :].bitcast(f32), ALU.subtract).then_inc(sem("normed"), 1)
            dve.wait_ge(sem("second_in"), 16 * 5)
            split(w_ab, w_ab_hi_r, w_ab_lo_r)
            dve.sem_inc(sem("normed"), 1)
            regions = ((slice(0, META), slice(0, 1)), (slice(0, P), slice(1, 3)))
            f = got("ab")
            ab = f.bank[:, 0:96].rearrange("p (t j) -> p t j", t=3)
            row = lambda n: rows[:, ROWS[n][0]:ROWS[n][1]]
            for p, t in regions:
                shape = [p.stop, t.stop - t.start, 16]
                nc.vector.tensor_tensor(gl[p, t], ab[p, t, 0:16], row("dt")[p].unsqueeze(1).to_broadcast(shape), ALU.add)
                last = nc.vector.tensor_copy(beta[p, t], ab[p, t, 16:32])
            link(last)
            dve.sem_inc(free[f.b], 1)
            dve.sem_inc(sem("ab"), 1)
            dve.wait_ge(sem("soft"), 1)
            link(nc.vector.tensor_scalar(nea, nea, -1.0, None, ALU.mult))
            for p, t in regions:
                shape = [p.stop, t.stop - t.start, 16]
                link(nc.vector.scalar_tensor_tensor(gl[p, t], gl[p, t], 0.0, gx[p, t], ALU.max, ALU.add))
                nc.vector.tensor_tensor(gl[p, t], gl[p, t], nea[p].unsqueeze(1).to_broadcast(shape), ALU.mult).then_inc(sem("gl"), 1)

            def conv(name, dst, kind, chunk, first):
                f = got(name)
                x = f.bank[:, 0:LEN]
                n = LEN - first
                tap = lambda j: col("conv5", j * 24 + chunk)
                link(nc.vector.tensor_scalar(dst, x[:, first:LEN], tap(2), None, ALU.mult))
                for j in (0, 1, 3, 4):
                    s = j - 2
                    lo, hi = max(0, -s - first), n - max(0, s)
                    link(nc.vector.scalar_tensor_tensor(dst[:, lo:hi], x[:, first + lo + s:first + hi + s], tap(j), dst[:, lo:hi],
                                                        ALU.mult, ALU.add))
                dve.sem_inc(free[f.b], 1)
                dve.sem_inc(sem(f"conv_{kind}"), 1)

            def normalize(kind, half, dst, n, scale):
                for h in range(4):
                    f = got(f"n{kind}{half}{h}")
                    link(nc.vector.tensor_scalar(rn2[:, h, 0:n], f.bank[:, 0:n], EPS, None, ALU.add))
                    dve.sem_inc(free[f.b], 1)
                dve.sem_inc(sem("ssn"), 1)
                normalize.count += 1
                dve.wait_ge(sem("sdn"), normalize.count)
                link(nc.vector.reciprocal(rn2[:, :, 0:n], rn2[:, :, 0:n]))
                link(nc.vector.scalar_tensor_tensor(dst[:, :, 0:n], dst[:, :, 0:n], scale, rn2[:, :, 0:n], ALU.mult, ALU.mult))
                dve.sem_inc(sem(f"{kind}_done"), 1)
            normalize.count = 0

            for h in range(4):
                conv(f"k{h}", kT[:, h, :], "k", 8 + h, 0)
            f = got("gsum")
            for p, t in regions:
                link(nc.vector.tensor_copy(gsum[p, t], f.bank[p, 0:96].rearrange("p (t j) -> p t j", t=3)[:, t]))
                link(nc.vector.tensor_tensor(krem[p, t], gsum[p, t, 16:32], gsum[p, t, 0:16], ALU.subtract))
            dve.sem_inc(free[f.b], 1)
            dve.sem_inc(sem("gsum"), 1)
            dve.wait_ge(sem("edec"), 1)
            for p, t in regions:
                link(nc.vector.tensor_scalar(edec[p, t], edec[p, t], -1.0, None, ALU.mult))
            dve.wait_ge(sem("yf_T"), 2)
            split(yf_T, yf_hi_r, yf_lo_r)
            dve.sem_inc(sem("normed"), 1)
            for h in range(4):
                conv(f"v{h}", v_T[0][:, h, :], "v", 16 + h, 0)
            for j in range(4):
                f = got(f"wf{j}")
                link(nc.vector.tensor_copy(y_four[:, 2 * j:2 * j + 2, :], two(f.bank)))
                dve.sem_inc(free[f.b], 1)
            for j in range(4):
                dve.wait_ge(sem("gate_f"), j + 1)
                y4 = y_four[:, 2 * j:2 * j + 2, :]
                link(nc.vector.tensor_tensor(y4, y4, gate2[:, j % 2], ALU.mult))
                dve.sem_inc(sem("y_four"), 1)
            normalize("k", 0, kT[:, 0:4], LEN, 1.0)
            for h in range(4):
                conv(f"q{h}", qT[:, h, :], "q", h, META)
            for h in range(4):
                conv(f"k{h + 4}", kT[:, h + 4, :], "k", 12 + h, 0)
            normalize("q", 0, qT[:, 0:4], SEQ, P ** -0.5)
            for h in range(4):
                conv(f"v{h + 4}", v_T[1][:, h, :], "v", 20 + h, 0)
            normalize("k", 1, kT[:, 4:8], LEN, 1.0)
            for h in range(4):
                conv(f"q{h + 4}", qT[:, h + 4, :], "q", 4 + h, META)
            normalize("q", 1, qT[:, 4:8], SEQ, P ** -0.5)
            dve.wait_ge(sem("to_tok"), 12)
            link(nc.vector.tensor_tensor(hn, hn_hi_r.bitcast(f32), hn_lo_r.bitcast(f32), ALU.add))
            link(nc.vector.memset(state["b"], 0.0))
            dve.sem_inc(sem("s_b"), 2)

            def over_heads(x, l, n=None):
                n = n or l.n
                return x[0:l.n, l.tile, l.j + l.hs[0]:l.j + l.hs[0] + len(l.hs)].unsqueeze(2).to_broadcast([l.n, len(l.hs), n])

            def mask_heads(m, l):
                return m[0:l.n, 0:l.n].unsqueeze(1).to_broadcast([l.n, len(l.hs), l.n])

            def lane_matrices(l):
                n, w = l.n, work(l)
                u = w.u[0:n, :, 0:n]
                a = w.a[0:n, :, 0:n]
                f = got(f"row{l.key}")
                link(nc.vector.tensor_tensor(u, heads_of(f, l), over_heads(gsum, l), ALU.subtract))
                if l.tile:
                    link(nc.vector.tensor_tensor(w.qk, u, mask_heads(amask(upto(l)), l), ALU.add))
                link(nc.vector.tensor_tensor(u, u, mask_heads(amask(1 - upto(l)), l), ALU.subtract))
                if l.tile == 0:
                    dve.sem_inc(free[f.b], 1)
                dve.sem_inc(sem(f"u{l.i}"), 1)
                if l.tile:
                    dve.wait_ge(sem(f"eg{l.i}"), l.r + 1)
                    q = qT[:, l.hs[0]:l.hs[0] + 4, l.at - META:l.at - META + n]
                    link(nc.vector.tensor_tensor(w.qd, w.qd, q, ALU.mult))
                    dve.sem_inc(sem(f"q{l.i}"), 1)
                dve.wait_ge(sem(f"d{l.i}"), l.r + 1)
                f = got(f"kk{l.key}")
                link(nc.vector.tensor_tensor(a, heads_of(f, l), u, ALU.mult))
                dve.sem_inc(free[f.b], 1)
                link(nc.vector.tensor_tensor(a, a, over_heads(beta, l), ALU.mult))
                dve.sem_inc(sem(f"a{l.i}"), 1)
                if l.tile:
                    f = got(f"kq{l.key}")
                    link(nc.vector.tensor_tensor(w.qk, w.qk, heads_of(f, l), ALU.mult))
                    dve.sem_inc(free[f.b], 1)
                    dve.sem_inc(sem(f"q{l.i}"), 1)

            def t_level(l, v):
                n, w = l.n, work(l)
                t, tt = w.t[0:n, :, 0:n], w.tt[0:n, :, 0:n]
                done = am_count[l.i] + v + 1
                if v == 0:
                    eye = mask_heads(ident, l)
                    dve.wait_ge(sem(f"am{l.i}"), done)
                    link(nc.vector.tensor_tensor(t, eye, w.am[0][0:n, :, 0:n], ALU.subtract))
                    f = got(f"z{l.key}0")
                    link(nc.vector.tensor_tensor(tt, eye, heads_of(f, l), ALU.subtract))
                    dve.sem_inc(free[f.b], 1)
                    dve.sem_inc(sem(f"tt{l.i}"), 1)
                    dve.sem_inc(sem(f"t{l.i}"), 1)
                    return
                f = got(f"yt{l.key}{v}")
                link(nc.vector.tensor_tensor(tt, tt, heads_of(f, l), ALU.subtract))
                dve.sem_inc(free[f.b], 1)
                if v == l.levels - 1:
                    link(nc.vector.tensor_tensor(tt, tt, over_heads(beta, l), ALU.mult))
                    dve.sem_inc(sem(f"tt{l.i}"), 1)
                    return
                dve.sem_inc(sem(f"tt{l.i}"), 1)
                f = got(f"y{l.key}{v}")
                link(nc.vector.tensor_tensor(t, t, heads_of(f, l), ALU.subtract))
                dve.sem_inc(free[f.b], 1)
                dve.sem_inc(sem(f"t{l.i}"), 1)

            def head_cols(x, l, t=None):
                return x[:, l.hs[0] * P:(l.hs[0] + 4) * P].rearrange("p (h c) -> p h c", h=4)

            def take_keys(l):
                w = work(l)
                f = got(f"r{l.key}")
                link(nc.vector.tensor_tensor(w.x, heads_of(f, l), over_heads(edec, l), ALU.mult))
                dve.sem_inc(free[f.b], 1)
                link(nc.vector.tensor_tensor(w.x, w.x, head_cols(v_tok[:, l.tile - 1, :], l), ALU.add))
                dve.sem_inc(sem(f"xk{l.i}"), 1)

            def take_values(l):
                w = work(l)
                f = got(f"vn{l.key}0")
                dve.wait_ge(sem(f"vn{l.i}"), l.r + 1)
                if l.r >= 2:
                    dve.sem_inc(free[f.b], 1)
                    return
                link(nc.vector.tensor_tensor(w.z2, heads_of(f, l), over_heads(krem, l), ALU.mult))
                dve.sem_inc(free[f.b], 1)
                dve.sem_inc(sem(f"vd{l.i}"), 1)

            def take_out(l):
                f = got(f"o{l.key}")
                o = o_T[:, l.hs[0]:l.hs[0] + 4, l.at - META:l.at - META + P]
                if l.first_out:
                    link(nc.vector.tensor_copy(o, heads_of(f, l)))
                else:
                    link(nc.vector.tensor_tensor(o, o, heads_of(f, l), ALU.add))
                dve.sem_inc(free[f.b], 1)
                if not l.first_out:
                    dve.sem_inc(sem("o_b"), 1)

            def take_state(l):
                s = head_cols(state[l.d], l)
                w = work(l)
                f = got(f"ds{l.key}0")
                link(nc.vector.tensor_tensor(s, s, over_heads(eall, l, P), ALU.mult))
                link(nc.vector.tensor_tensor(s, s, heads_of(f, l), ALU.add))
                dve.sem_inc(free[f.b], 1)
                dve.sem_inc(sem(f"s_{l.d}"), 1)

            am_count = [0, 0, 0]
            for r, lanes in enumerate(ROUNDS):
                now = ([meta] if r == 0 else []) + lanes
                before = ROUNDS[r - 1] if r else []
                for l in now:
                    lane_matrices(l)
                for v in range(7):
                    for l in now:
                        if v == 0:
                            t_level(l, v)
                    if v == 1:
                        for l in before: take_keys(l)
                    if v == 3:
                        for l in before: take_values(l)
                    if v == 5:
                        for l in before: take_out(l)
                    if v == 6 and r < 3:
                        for l in before: take_state(l)
                    if v:
                        for l in now:
                            if v < l.levels:
                                t_level(l, v)
                    if r == 0 and v == 5:
                        for part in range(2):
                            f = got(f"vn{meta.key}{part}")
                            k = krem[0:META, 0, 4 * part:4 * part + 4].unsqueeze(2).to_broadcast([META, 4, P])
                            link(nc.vector.tensor_tensor(x_meta[0:META, part * 512:(part + 1) * 512].rearrange("p (h c) -> p h c", h=4),
                                                         f.bank[0:META, :].rearrange("p (h c) -> p h c", h=4), k, ALU.mult))
                            dve.sem_inc(free[f.b], 1)
                            dve.sem_inc(sem("vd2"), 1)
                    if r == 0 and v == 6:
                        for part in range(2):
                            f = got(f"ds{meta.key}{part}")
                            link(nc.vector.tensor_copy(state["f"][:, part * 512:(part + 1) * 512], f.bank[:, :]))
                            dve.sem_inc(free[f.b], 1)
                            dve.sem_inc(sem("s_f"), 1)
                for l in now:
                    am_count[l.i] += l.levels
            for l in ROUNDS[-1]: take_keys(l)
            for l in ROUNDS[-1]: take_values(l)
            for l in ROUNDS[-1]: take_out(l)
            for i in range(4):
                f = got(f"no{i}")
                link(nc.vector.tensor_scalar(o_rn[:, 2 * i:2 * i + 2, :], two(f.bank), 1.0 / P, EPS, ALU.mult, ALU.add))
                dve.sem_inc(free[f.b], 1)
                dve.sem_inc(sem("ss_o"), 1)
            for i in range(2):
                dve.wait_ge(sem("sd_o"), i + 1)
                rn = o_rn[:, 4 * i:4 * i + 4, :]
                o = o_T[:, 4 * i:4 * i + 4, :]
                link(nc.vector.reciprocal(rn, rn))
                link(nc.vector.scalar_tensor_tensor(o, o, col("out_g"), rn, ALU.mult, ALU.mult))
            for j in range(4):
                dve.wait_ge(sem("z_g"), j + 1)
                o = o_T[:, 2 * j:2 * j + 2, :]
                link(nc.vector.tensor_tensor(o, o, z_g[:, j], ALU.mult))
                dve.sem_inc(sem("y_delta"), 1)
            for j in range(4):
                f = got(f"wd{j}")
                dve.wait_ge(sem("z_g"), 4 + j + 1)
                y4 = y_four[:, 2 * j:2 * j + 2, :]
                link(nc.vector.tensor_tensor(z_g[:, j], two(f.bank), z_g[:, j], ALU.mult))
                link(nc.vector.tensor_tensor(y4, y4, z_g[:, j], ALU.add))
                dve.sem_inc(free[f.b], 1)
                dve.sem_inc(sem("merged2"), 1)
            for j in range(4):
                f = got(f"wp{j}")
                r = res[:, 2 * j:2 * j + 2, META:]
                link(nc.vector.tensor_tensor(r, r, two(f.bank), ALU.add))
                dve.sem_inc(free[f.b], 1)
                dve.sem_inc(sem("h2"), 1)

            f = got("ssq4")
            nc.vector.tensor_scalar(rms4, f.bank[:, 0:SEQ], 1.0 / D, EPS, ALU.mult, ALU.add).then_inc(sem("variance"), 1)
            dve.wait_ge(sem("deviation"), 6)
            link(nc.vector.reciprocal(rms4, rms4))
            dve.sem_inc(free[f.b], 1)
            for k in range(KD):
                nc.vector.scalar_tensor_tensor(m_T[:, k, :], res[:, k, META:], col("norm2_g", k), rms4, ALU.mult,
                                               ALU.mult).then_inc(sem("normed"), 1)
            link(nc.vector.memset(r_ones, 1.0))
            f = got("router")
            for t in range(TT):
                link(nc.vector.tensor_tensor(router[:, t, :], f.bank[:, t * 72:(t + 1) * 72], row("b_router"), ALU.add))
            dve.sem_inc(free[f.b], 1)

            def first_of(out, x, value, n):
                link(nc.vector.tensor_scalar(r_eq[:, 0:n], x, value, None, ALU.is_equal))
                link(nc.vector.tensor_tensor_scan(r_cum[:, 0:n], r_ones[:, 0:n], r_eq[:, 0:n], 0.0, ALU.mult, ALU.add))
                link(nc.vector.scalar_tensor_tensor(out, r_cum[:, 0:n], 1.0, r_eq[:, 0:n], ALU.is_equal, ALU.mult))

            def top(out, x):
                link(nc.vector.tensor_reduce(out, x, AX.X, ALU.max))

            for t in range(TT):
                groups = router[:, t, 0:GROUPS]
                experts = router[:, t, GROUPS:]
                by_group = experts.rearrange("p (g e) -> p g e", g=GROUPS)
                top(r_top[:, 0:1], groups)
                first_of(r_oh, groups, r_top[:, 0:1], GROUPS)
                link(nc.vector.tensor_scalar(r_oh, r_oh, 1.0, BIG, ALU.subtract, ALU.mult))
                link(nc.vector.tensor_tensor(by_group, by_group, r_oh.unsqueeze(2).to_broadcast([P, GROUPS, GROUPS]), ALU.add))
                top(r_top[:, 1:2], experts)
                first_of(pick[0], experts, r_top[:, 1:2], EXPERTS)
                link(nc.vector.scalar_tensor_tensor(pick[1], pick[0], -BIG, experts, ALU.mult, ALU.add))
                top(r_second[:, t:t + 1], pick[1])
                link(nc.vector.tensor_scalar(r_nmax[:, 2 * t:2 * t + 2], r_top[:, 0:2], -1.0, None, ALU.mult))
                link(nc.vector.tensor_copy(code[:, t, :], pick[1]))
                first_of(pick[1], code[:, t, :], r_second[:, t:t + 1], EXPERTS)
                nc.vector.tensor_tensor(chosen[:, t, :], pick[0], pick[1], ALU.add).then_inc(sem("chosen"), 1)
                dve.wait_ge(sem("chosen"), t + 1)
                dve.sem_inc(sem("r_max"), 1)
                dve.wait_ge(sem("r_exp"), t + 1)
                rs = r_sum[:, 2 * t:2 * t + 2]
                sec = r_second[:, t:t + 1]
                link(nc.vector.reciprocal(rs, rs))
                link(nc.vector.tensor_tensor(sec, sec, rs[:, 1:2], ALU.mult))
                link(nc.vector.tensor_tensor(r_top[:, 2:3], rs[:, 1:2], sec, ALU.add))
                link(nc.vector.reciprocal(r_top[:, 2:3], r_top[:, 2:3]))
                link(nc.vector.tensor_tensor(r_top[:, 2:3], r_top[:, 2:3], rs[:, 0:1], ALU.mult))
                link(nc.vector.tensor_tensor(r_top[:, 3:4], r_top[:, 2:3], rs[:, 1:2], ALU.mult))
                link(nc.vector.tensor_tensor(r_top[:, 4:5], r_top[:, 2:3], sec, ALU.mult))
                link(nc.vector.tensor_scalar(weight[:, t, :], pick[0], r_top[:, 3:4], None, ALU.mult))
                link(nc.vector.scalar_tensor_tensor(weight[:, t, :], pick[1], r_top[:, 4:5], weight[:, t, :], ALU.mult, ALU.add))
            f = got("ranks")
            FAR = 1e6
            for t in range(TT):
                link(nc.vector.scalar_tensor_tensor(code[:, t, :], f.bank[:, 64 * t:64 * (t + 1)], FAR, chosen[:, t, :], ALU.add, ALU.mult))
                link(nc.vector.tensor_scalar(code[:, t, :], code[:, t, :], -(FAR + 1.0), None, ALU.add))
            link(nc.vector.tensor_reduce(r_top[:, 0:1], f.bank[:, 128:192], AX.X, ALU.max))
            dve.sem_inc(free[f.b], 1)
            dve.wait_ge(sem("slots"), 1)
            link(nc.vector.tensor_scalar(passes_f[:, 0:MOST], cap_steps, r_top[:, 0:1], None, ALU.is_lt))
            link(nc.vector.tensor_reduce(r_top[:, 1:2], passes_f[:, 0:MOST], AX.X, ALU.add))
            link(nc.vector.tensor_copy(passes_i, r_top[0:1, 1:2]))
            dve.sem_inc(sem("passes"), 1)

            n_passes = read_passes(nc.vector, dve)
            slots4 = slot_of.rearrange("p (j s) -> p j s", j=PER)
            dve.sem_inc(sem("pick_T"), 1)
            dve.sem_inc(sem("hid"), 1)
            dve.sem_inc(sem("added"), 4)
            with dve.Fori(0, n_passes) as p:
                with dve.Fori(0, N_GROUPS // 2) as pair:
                  for u in range(2):
                    q = 2 * pair + u
                    it = p * N_GROUPS + q
                    dve.wait_ge(sem("pick_T"), it + 1)
                    for t in range(TT):
                        link2(nc.vector.tensor_tensor(pick_m[:, t, :].rearrange("p (j s) -> p j s", j=PER), slots4,
                                                      code[:, t, bass.ds(q * PER, PER)].unsqueeze(2).to_broadcast([P, PER, CAP]),
                                                      ALU.is_equal), dve, "picks_m", it * 2 + t + 1)
                    for t in range(TT):
                        last = nc.vector.tensor_tensor(pick_w[:, t, :].rearrange("p (j s) -> p j s", j=PER),
                                                       pick_m[:, t, :].rearrange("p (j s) -> p j s", j=PER),
                                                       weight[:, t, bass.ds(q * PER, PER)].unsqueeze(2).to_broadcast([P, PER, CAP]),
                                                       ALU.mult)
                    last.then_inc(sem("picks"), 1)
                    dve.wait_ge(sem("gathered"), 3 * it + 2)
                    nc.vector.tensor_copy(xg[:, 4:8, :].rearrange("p k s -> p (k s)"), banks[1][:, :]).then_inc(sem("xg"), 1)
                    dve.wait_ge(sem("gathered"), 3 * it + 3)
                    nc.vector.tensor_copy(pick_T, banks[2][:, 0:SEQ]).then_inc(sem("pick_T"), 1)
                    dve.wait_ge(sem("silu"), it + 1)
                    nc.vector.tensor_tensor(hid, act_g, banks[3][:, FE:2 * FE], ALU.mult).then_inc(sem("hid"), 1)
                    dve.wait_ge(sem("down"), 2 * it + 4)
                    nc.vector.tensor_copy(yb[:, 512:D], banks[6][:, :]).then_inc(sem("yb"), 1)
                    for i, b in enumerate((0, 1, 2, 7)):
                        dve.wait_ge(sem("scattered"), 4 * it + i + 1)
                        x = res[:, 2 * i:2 * i + 2, META:]
                        nc.vector.tensor_tensor(x, x, two(banks[b]), ALU.add).then_inc(sem("added"), 1)
                nc.vector.tensor_scalar(code, code, -float(CAP), None, ALU.add).then_inc(sem("code"), 1)
                dve.wait_ge(sem("code"), p + 1)
            dve.sem_inc(sem("moe_done"), 1)
            dve.wait_ge(sem("ssq5"), 1)
            nc.vector.tensor_scalar(rms4, banks[3][:, 0:SEQ], 1.0 / D, EPS, ALU.mult, ALU.add).then_inc(sem("variance"), 1)
            dve.wait_ge(sem("deviation"), 7)
            link(nc.vector.reciprocal(rms4, rms4))
            for k in range(KD):
                nc.vector.scalar_tensor_tensor(out_T[:, k, :], res[:, k, META:], col("last_g", k), rms4, ALU.mult,
                                               ALU.mult).then_inc(sem("final"), 1)

        @block.gpsimd
        def _(pool):
            def trail(hs):
                for q in range(2 * hs.start, 2 * hs.stop):
                    pool.wait_ge(sem("w_hi"), q + 1)
                    hi, lo = w_hi[q // 2 % SPLIT][:, quarter(q)], w_lo[q // 2 % SPLIT][:, quarter(q)]
                    nc.gpsimd.tensor_tensor(lo, raw[q % RAW], hi.bitcast(f32), ALU.subtract).then_inc(sem("w_lo"), 1)

            WS_HALVES = 10
            trail(range(WS_HALVES))
            pool.wait_ge(sem("ws_in"), 16)
            nc.gpsimd.affine_select(out=wsT, in_=wsT, compare_op=ALU.is_ge, fill=0.0, base=0,
                                    pattern=[[0, NH], [1, P]], channel_multiplier=-1).then_inc(sem("ws_masked"), 1)
            trail(range(WS_HALVES, N_HALVES))

            t_count = [0, 0, 0]
            for r, lanes in enumerate(ROUNDS):
                now = ([meta] if r == 0 else []) + lanes
                for v in range(7):
                    for l in now:
                        if v >= l.levels:
                            continue
                        n, w = l.n, work(l)
                        if v == 0:
                            pool.wait_ge(sem(f"a{l.i}"), l.r + 1)
                            if r == 0:
                                pool.wait_ge(sem("second_in"), 16 * 5)
                        if v >= 2:
                            f = fills[f"z{l.key}{v - 2}"]
                            pool.wait_ge(full[f.b], f.n + 1)
                        if v == 2:
                            pool.wait_ge(sem(f"t{l.i}"), t_count[l.i] + 1)
                        m = level_mask[:, (v + (0 if l.d == "f" else 7)) * P:][:, 0:P]
                        nc.gpsimd.tensor_tensor(w.am[v % 2][0:n, :, 0:n], w.a[0:n, :, 0:n],
                                                m[0:n, 0:n].unsqueeze(1).to_broadcast([n, len(l.hs), n]),
                                                ALU.mult).then_inc(sem(f"am{l.i}"), 1)
                for l in now:
                    t_count[l.i] += l.levels - 1

            pool.wait_ge(sem("normed"), 2 * KD + 3)
            nc.gpsimd.iota(slot_i, pattern=[[0, PER], [1, CAP]], base=0, channel_multiplier=0).then_inc(sem("pool_chain"), 1)
            nc.gpsimd.iota(steps_i, pattern=[[CAP, MOST]], base=0, channel_multiplier=0).then_inc(sem("pool_chain"), 1)
            pool.wait_ge(sem("pool_chain"), 2)
            nc.gpsimd.tensor_copy(slot_of, slot_i).then_inc(sem("pool_chain"), 1)
            nc.gpsimd.tensor_copy(cap_steps, steps_i).then_inc(sem("pool_chain"), 1)
            pool.wait_ge(sem("pool_chain"), 4)
            pool.sem_inc(sem("slots"), 1)

        @block.sync
        def _(sp):
            sp.dma_start(res[:, :, :], A["hcatT"]).then_inc(sem("res_in"), 16)
            sp.dma_start(cols, A["cols"]).then_inc(sem("cols_in"), 16)
            sp.dma_start(arena[:, consts_at:consts_at + 4 * P], A["consts"]).then_inc(sem("consts_in"), 16)
            for h in range(N_HALVES):
                for q in (2 * h, 2 * h + 1):
                    if q >= RAW:
                        sp.wait_ge(sem("w_lo"), q - RAW + 1)
                    sp.dma_start(raw[q % RAW], FRONT[q // 4][:, q % 4 * QUARTER:(q % 4 + 1) * QUARTER]).then_inc(sem(f"slot{q % RAW}_in"), 16)
                if h == 4:
                    sp.dma_start(sel[0:NH], A["sel"]).then_inc(sem("small_in"), 16)
                    sp.dma_start(rows, A["rows"]).then_inc(sem("small_in"), 16)
                    sp.dma_start(ln_rows, A["ln_rows"]).then_inc(sem("small_in"), 16)
                    sp.dma_start(wuk, A["wuk"]).then_inc(sem("small_in"), 16)
                    sp.dma_start(wuv, A["wuv"]).then_inc(sem("small_in"), 16)
                    sp.dma_start(wsT, A["wsT"]).then_inc(sem("ws_in"), 16)
                    sp.dma_start(bs[0:1, :], A["bs"]).then_inc(sem("small_in"), 16)
                if h == 2 * FIN + 3:
                    sp.wait_ge(sem("final"), KD)
                    sp.dma_start(dft_d, A["dft_d"]).then_inc(sem("second_in"), 16)
                    sp.dma_start(dft_l, A["dft_l"]).then_inc(sem("second_in"), 16)
                    sp.dma_start(w_ab, A["w_ab"]).then_inc(sem("second_in"), 16)
                    sp.dma_start(tri[:, 0:4 * P], A["tri"]).then_inc(sem("second_in"), 16)
                    sp.dma_start(level_mask, A["level"]).then_inc(sem("second_in"), 16)
            last = readers[N_HALVES - 1]
            sp.wait_ge(full[last.b], last.n + 1)
            for b in range(ZB, N_BLOCKS):
                if b >= ZB + SLOTS:
                    last = readers[f"block{b - SLOTS}"]
                    sp.wait_ge(full[last.b], last.n + 1)
                sp.dma_start(ring[(b - ZB) % SLOTS], FRONT[b]).then_inc(sem(f"slot{(b - ZB) % SLOTS}_in"), 16)
            def load_gate_up(q, u, js=range(PER)):
                for j in js:
                    name = "odd_in" if u else f"slot{(N_BLOCKS - ZB + j) % SLOTS}_in"
                    src = A["gate_up"][q, j] if isinstance(q, int) else A["gate_up"][bass.ds(q, 1), j].rearrange("o p c -> (o p) c")
                    sp.dma_start(gate_up[u][j], src).then_inc(sem(name), 16)

            def load_down(q):
                for j in range(2):
                    src = A["down"][q, j] if isinstance(q, int) else A["down"][bass.ds(q, 1), j].rearrange("o p c -> (o p) c")
                    sp.dma_start(down[j], src).then_inc(sem("down_in"), 16)

            sp.wait_ge(sem("o_b"), 4)
            load_down(0)
            load_gate_up(1, 1, [3])
            sp.wait_ge(sem("merged2"), 4)
            sp.dma_start(w_router, A["w_router"]).then_inc(sem("router_in"), 16)
            for j in range(PER):
                last = readers[f"block{N_BLOCKS + j - SLOTS}"]
                sp.wait_ge(full[last.b], last.n + 1)
                load_gate_up(0, 0, [j])
            sp.wait_ge(sem("normed"), 2 * KD + 3)
            load_gate_up(1, 1, range(3))
            n_passes = read_passes(nc.sync, sp)
            with sp.Fori(0, n_passes * (N_GROUPS // 2) - 1) as pair:
                for u in range(2):
                    g = 2 * pair + u + 1
                    sp.wait_ge(sem("down"), 2 * g + 2)
                    load_down(g % N_GROUPS)
                    sp.wait_ge(sem("gate_up"), g)
                    load_gate_up((g + 1) % N_GROUPS, u)
            sp.wait_ge(sem("down"), n_passes * (2 * N_GROUPS))
            load_down(N_GROUPS - 1)
            for i in range(4):
                sp.wait_ge(sem("final"), KD + 2 * i + 2)
                sp.dma_start(A["o"][:, 2 * i:2 * i + 2, :], out_T[:, 2 * i:2 * i + 2, :]).then_inc(sem("out"), 16)
            sp.wait_ge(sem("out"), 64)


def constants():
    f32 = np.float32
    p, c = np.arange(P)[:, None], np.arange(P)[None]
    le, ge = p <= c, p >= c
    angle = 2 * np.pi * np.outer(np.arange(P), np.arange(P)) / P
    out = {
        "consts": np.concatenate([np.eye(P), np.ones((P, P)), np.zeros((P, P)), np.where(ge, 0, -BIG)], 1),
        "sel": np.repeat(np.eye(NH)[:, :, None], SEQ, 2),
        "tri": np.concatenate([np.where(le, 0, -1e30), np.where(ge, 0, -1e30), le, ge], 1),
        "dft_d": np.concatenate([np.cos(angle), -np.sin(angle)], 1),
    }
    angle = 2 * np.pi * (np.outer(np.arange(LEN), np.arange(META, LEN)) % LEN) / LEN
    both = np.concatenate([np.cos(angle), np.sin(angle)], 1) / np.sqrt(LEN * P)
    out["dft_l"] = np.zeros((P, 3, 2 * SEQ))
    out["dft_l"][:META, 0] = both[:META]
    out["dft_l"][:, 1:] = both[META:].reshape(TT, P, 2 * SEQ).transpose(1, 0, 2)
    lower = [((p >> (v + 1)) == (c >> (v + 1))) & ((p >> v) % 2 == 1) & ((c >> v) % 2 == 0) for v in range(7)]
    out["level"] = np.concatenate(lower + [m.T for m in lower], 1)
    return {name: np.ascontiguousarray(a, dtype=f32) for name, a in out.items()}


def by_rows(m):
    return m.reshape(-1, P, m.shape[1]).transpose(1, 0, 2).reshape(P, BLOCK)


def in_halves(m):
    return m.reshape(-1, P, 2, m.shape[1] // 2).transpose(1, 2, 0, 3).reshape(P, BLOCK)


def cut(w, names, sizes):
    ends = np.cumsum([0] + sizes)
    return {n: w[:, ends[i]:ends[i + 1]] for i, n in enumerate(names)}


def lay_out(I):
    parts = lambda m: [in_halves(m[:, :W1]), in_halves(m[:, W1:])]
    whole = lambda m: [by_rows(m[:, :W1]), by_rows(m[:, W1:])]
    w = cut(I["w_in"][0], "au av az bq bc qi ki wi bz cb cc cx cz dq dk dv df dz gates".split(),
            [W1, W1, W1, W1, P, NH * IDX, IDX, NH, W1, W1, W1, W1, W1, W1, W1, W1, NH, W1, 4 * D])
    pad = np.zeros((D, 2 * P - P - 2 * NH - IDX), w["bc"].dtype)
    front = [in_halves(np.concatenate([w["bc"], w["wi"], w["df"], w["ki"], pad, w["qi"]], 1))]
    front += [in_halves(w[n]) for n in "bq dq dk dv av au az dz bz cb cc cx cz".split()]
    for n in (0, 3, 2, 1):
        front += parts(w["gates"][:, n * D:(n + 1) * D]) + [in_halves(I["w_branch"][0, n])]
    front += parts(I["w_out"][0])
    w = cut(I["w_in_2"][0], "four q k v z a_f b_f a_b b_b gate_f gate_d".split(), [W1, D, D, D, D, 8, 8, 8, 8, D, D])
    q, k, v = (parts(w[n]) for n in "qkv")
    z, gate_d, w_delta = (whole(m) for m in (w["z"], w["gate_d"], I["w_delta_2"][0]))
    front += [in_halves(w["four"]), k[0], v[0], in_halves(I["w_fourier_2"][0])] + parts(w["gate_f"]) + [q[0], k[1], v[1], q[1]]
    front += z + [gate_d[0], w_delta[0], gate_d[1], w_delta[1]] + whole(I["w_out_2"][0])

    chunks = lambda a: a.reshape(-1, P).T
    b_f = np.concatenate([I["fox_b_f"][0], np.zeros(P - NH, I["fox_b_f"].dtype)])[:, None]
    cols = [chunks(a) for a in (I["norm_g"], I["final_g"], I["conv_w"], I["dsa_kv_g"])] + [b_f]
    cols += [chunks(I[n + "_2"]) for n in ("norm1_g", "norm2_g", "final_norm_g", "conv_w", "out_norm_g")]
    row = np.concatenate([I[n + "_2"].ravel() for n in ("dt_bias_fwd", "dt_bias_bwd", "a_log_fwd", "a_log_bwd",
                                                        "b_router_group", "b_router_expert")])
    ln = np.concatenate([I["gm_ln_g"][0], I["gm_ln_b"][0]])
    on_all = lambda a: np.broadcast_to(a, (P, a.size))
    tokens = np.concatenate([I["meta_tokens_2"], I["x"][0]], 0)
    router = np.concatenate([I["w_router_group_2"][0], I["w_router_expert_2"][0]], 1)
    gate_up = np.concatenate([I["w_gate_e_2"][0], I["w_up_e_2"][0]], 2)
    n = EXPERTS // PER
    out = {
        "front": np.stack(front),
        "cols": np.concatenate(cols, 1), "rows": on_all(row), "ln_rows": on_all(ln),
        "hcatT": tokens.T.reshape(KD, P, LEN).transpose(1, 0, 2),
        "wuk": I["dsa_w_uk"][0].transpose(2, 0, 1), "wuv": I["dsa_w_uv"][0].transpose(1, 0, 2),
        "wsT": I["gm_w_s"][0].transpose(2, 0, 1), "bs": I["gm_b_s"][0].reshape(1, W1),
        "w_ab": np.concatenate([w[x] for x in ("a_f", "a_b", "b_f", "b_b")], 1).reshape(KD, P, 32).transpose(1, 0, 2),
        "w_router": router.reshape(KD, P, 72).transpose(1, 0, 2),
        "gate_up": gate_up.reshape(n, PER, KD, P, 2 * FE).transpose(0, 1, 3, 2, 4).reshape(n, PER, P, BLOCK),
        "down": I["w_down_e_2"][0].reshape(n, 2, 2, 2, P, D).transpose(0, 1, 4, 2, 3, 5).reshape(n, 2, P, BLOCK),
    }
    return {name: np.ascontiguousarray(a) for name, a in out.items()}


def kernel(**inputs):
    import concourse.bacc as bacc
    from concourse.bass_utils import run_bass_kernel_spmd

    arrays = {**lay_out({name: np.asarray(a) for name, a in inputs.items()}), **constants()}
    nc = bacc.Bacc("TRN2", target_bir_lowering=False, num_devices=1)
    tensors = {name: nc.dram_tensor(name, a.shape, mybir.dt.from_np(a.dtype), kind="ExternalInput").ap()
               for name, a in arrays.items()}
    tensors["o"] = nc.dram_tensor("o", (P, KD, SEQ), mybir.dt.float32, kind="ExternalOutput").ap()
    build(nc, tensors)
    result = run_bass_kernel_spmd(nc, [arrays], core_ids=[0])
    got = result.results[0]["o"]
    return np.ascontiguousarray(got.transpose(2, 1, 0).reshape(1, SEQ, D))
```
